# Optimizing a Trainium2 kernel written in Bass

```python
import jax, jax.numpy as jnp
from jax import lax
import numpy as np

D_MODEL = 1024
BATCH = 1
SEQ = 512
DEPTH = 1

HEAD_DIM = 64
A_HEADS = 8
A_Q_RANK = 256
A_V_LATENT = 128
IDX_HEADS = 8
IDX_DIM = 64
B_HEADS = 8
D_FF = 2816
MAX_TOPK = 256
Q_BLOCK = 128
ROPE_THETA = 10000.0
EPS = 1e-6
A_WIDTH = A_HEADS * HEAD_DIM
B_WIDTH = B_HEADS * HEAD_DIM
IN_SPLITS = (A_Q_RANK, HEAD_DIM, A_V_LATENT, IDX_DIM, IDX_HEADS,
             B_WIDTH, B_WIDTH, B_WIDTH, D_MODEL, D_MODEL)
IN_COLS = sum(IN_SPLITS)


def rms_norm(x, g):
    xf = x.astype(jnp.float32)
    y = xf * lax.rsqrt(jnp.mean(xf * xf, axis=-1, keepdims=True) + EPS)
    return (y * g.astype(jnp.float32)).astype(x.dtype)

def swiglu(h, w_gate, w_up, w_down):
    return (jax.nn.silu(h @ w_gate) * (h @ w_up)) @ w_down

def rope_tables(positions, dim):
    inv_freq = ROPE_THETA ** (-jnp.arange(0, dim, 2, dtype=jnp.float32) / dim)
    ang = positions.astype(jnp.float32)[..., None] * inv_freq
    return jnp.cos(ang), jnp.sin(ang)

def apply_rope(x, cos, sin):
    xf = x.astype(jnp.float32)
    x1, x2 = jnp.split(xf, 2, axis=-1)
    return jnp.concatenate([x1 * cos - x2 * sin, x1 * sin + x2 * cos], axis=-1).astype(x.dtype)

def dsa_attention(q_a, k_a, v_a, q_idx, k_idx, w_idx, w_uv, top_k):
    bsz, seq = k_a.shape[0], k_a.shape[1]
    n_blocks = seq // Q_BLOCK
    key_pos = jnp.arange(seq)

    def block(i):
        q0 = i * Q_BLOCK
        qa = lax.dynamic_slice_in_dim(q_a, q0, Q_BLOCK, axis=1)
        qi = lax.dynamic_slice_in_dim(q_idx, q0, Q_BLOCK, axis=1)
        wi = lax.dynamic_slice_in_dim(w_idx, q0, Q_BLOCK, axis=1)
        t_pos = q0 + jnp.arange(Q_BLOCK)
        dots = jnp.einsum('bthd,bsd->bths', qi.astype(jnp.float32), k_idx.astype(jnp.float32))
        score = jnp.einsum('bths,bth->bts', jax.nn.relu(dots), wi.astype(jnp.float32))
        causal = key_pos[None, :] <= t_pos[:, None]
        score = jnp.where(causal[None], score, -jnp.inf)
        _, idx = lax.top_k(score, top_k)
        valid = idx <= t_pos[None, :, None]
        flat = idx.reshape(bsz, Q_BLOCK * top_k)[:, :, None]
        kg = jnp.take_along_axis(k_a, flat, axis=1).reshape(bsz, Q_BLOCK, top_k, HEAD_DIM)
        vg = jnp.take_along_axis(v_a, flat, axis=1).reshape(bsz, Q_BLOCK, top_k, A_V_LATENT)
        logits = jnp.einsum('bthd,btkd->bthk', qa.astype(jnp.float32), kg.astype(jnp.float32)) * (HEAD_DIM ** -0.5)
        logits = jnp.where(valid[:, :, None, :], logits, -jnp.inf)
        p = jax.nn.softmax(logits, axis=-1).astype(v_a.dtype)
        o_lat = jnp.einsum('bthk,btkc->bthc', p, vg)
        o = jnp.einsum('bthc,hcd->bthd', o_lat, w_uv)
        return o.reshape(bsz, Q_BLOCK, A_WIDTH)

    out = lax.map(block, jnp.arange(n_blocks))
    return out.transpose(1, 0, 2, 3).reshape(bsz, seq, A_WIDTH)

def stick_breaking_attention(q_b, k_b, v_b):
    bsz, seq = q_b.shape[0], q_b.shape[1]
    n_blocks = seq // Q_BLOCK
    key_pos = jnp.arange(seq)

    def block(i):
        q0 = i * Q_BLOCK
        qb = lax.dynamic_slice_in_dim(q_b, q0, Q_BLOCK, axis=1)
        t_pos = q0 + jnp.arange(Q_BLOCK)
        z = jnp.einsum('bthd,bshd->bhts', qb.astype(jnp.float32), k_b.astype(jnp.float32)) * (HEAD_DIM ** -0.5)
        strict = (key_pos[None, :] < t_pos[:, None])[None, None]
        log_not = jnp.where(strict, jax.nn.log_sigmoid(-z), 0.0)
        between = lax.cumsum(log_not, axis=3, reverse=True) - log_not
        log_a = jax.nn.log_sigmoid(z) + between
        a = jnp.where(strict, jnp.exp(log_a), 0.0).astype(v_b.dtype)
        o = jnp.einsum('bhts,bshd->bthd', a, v_b)
        return o.reshape(bsz, Q_BLOCK, B_WIDTH)

    out = lax.map(block, jnp.arange(n_blocks))
    return out.transpose(1, 0, 2, 3).reshape(bsz, seq, B_WIDTH)

def first_inputs(seed: int = 0) -> dict:
    key = jax.random.key(seed)
    ks = jax.random.split(key, 24)
    f32 = jnp.float32

    def w(k, shape, fan_in):
        return jax.random.normal(k, shape, f32) * (fan_in ** -0.5)

    def gain(k, shape):
        return 1.0 + 0.02 * jax.random.normal(k, shape, f32)

    L = DEPTH
    return {
        'x': jax.random.normal(ks[0], (BATCH, SEQ, D_MODEL), f32),
        'positions': jnp.broadcast_to(jnp.arange(SEQ, dtype=jnp.int32), (BATCH, SEQ)),
        'g_ffn1': gain(ks[1], (L, D_MODEL)),
        'w1_gate': w(ks[2], (L, D_MODEL, D_FF), D_MODEL),
        'w1_up': w(ks[3], (L, D_MODEL, D_FF), D_MODEL),
        'w1_down': w(ks[4], (L, D_FF, D_MODEL), D_FF),
        'g_mix': gain(ks[5], (L, D_MODEL)),
        'w_in': w(ks[6], (L, D_MODEL, IN_COLS), D_MODEL),
        'g_cq': gain(ks[7], (L, A_Q_RANK)),
        'w_uq_a': w(ks[8], (L, A_Q_RANK, A_WIDTH), A_Q_RANK),
        'w_q_idx': w(ks[9], (L, A_Q_RANK, IDX_HEADS * IDX_DIM), A_Q_RANK),
        'g_q_a': gain(ks[10], (L, HEAD_DIM)),
        'g_k_a': gain(ks[11], (L, HEAD_DIM)),
        'w_uv_a': w(ks[12], (L, A_HEADS, A_V_LATENT, HEAD_DIM), A_V_LATENT),
        'w_o_a': w(ks[13], (L, A_WIDTH, D_MODEL), A_WIDTH),
        'w_o_b': w(ks[14], (L, B_WIDTH, D_MODEL), B_WIDTH),
        'w_out': w(ks[15], (L, D_MODEL, D_MODEL), D_MODEL),
        'g_ffn2': gain(ks[16], (L, D_MODEL)),
        'w2_gate': w(ks[17], (L, D_MODEL, D_FF), D_MODEL),
        'w2_up': w(ks[18], (L, D_MODEL, D_FF), D_MODEL),
        'w2_down': w(ks[19], (L, D_FF, D_MODEL), D_FF),
    }

def first_block(x, positions, g_ffn1, w1_gate, w1_up, w1_down, g_mix, w_in, g_cq, w_uq_a, w_q_idx,
              g_q_a, g_k_a, w_uv_a, w_o_a, w_o_b, w_out, g_ffn2, w2_gate, w2_up, w2_down):
    bsz, seq, _ = x.shape
    top_k = min(MAX_TOPK, seq // 4)
    cos, sin = rope_tables(positions, HEAD_DIM)
    cos_h, sin_h = cos[:, :, None, :], sin[:, :, None, :]
    offsets = [int(o) for o in np.cumsum(IN_SPLITS)[:-1]]
    for l in range(DEPTH):
        x = x + 0.5 * swiglu(rms_norm(x, g_ffn1[l]), w1_gate[l], w1_up[l], w1_down[l])

        h = rms_norm(x, g_mix[l])
        proj = h @ w_in[l]
        (c_q, k_a, v_a, k_idx, w_idx, q_b, k_b, v_b, gate_a, gate_b) = jnp.split(proj, offsets, axis=-1)

        c_q = rms_norm(c_q, g_cq[l])
        q_a = (c_q @ w_uq_a[l]).reshape(bsz, seq, A_HEADS, HEAD_DIM)
        q_a = apply_rope(rms_norm(q_a, g_q_a[l]), cos_h, sin_h)
        k_a = apply_rope(rms_norm(k_a, g_k_a[l]), cos, sin)
        q_idx = apply_rope((c_q @ w_q_idx[l]).reshape(bsz, seq, IDX_HEADS, IDX_DIM), cos_h, sin_h)
        k_idx = apply_rope(k_idx, cos, sin)
        w_idx = w_idx * ((IDX_HEADS ** -0.5) * (IDX_DIM ** -0.5))
        y_a = dsa_attention(q_a, k_a, v_a, q_idx, k_idx, w_idx, w_uv_a[l], top_k)

        y_b = stick_breaking_attention(q_b.reshape(bsz, seq, B_HEADS, HEAD_DIM),
                                       k_b.reshape(bsz, seq, B_HEADS, HEAD_DIM),
                                       v_b.reshape(bsz, seq, B_HEADS, HEAD_DIM))

        merged = jax.nn.sigmoid(gate_a) * (y_a @ w_o_a[l]) + jax.nn.sigmoid(gate_b) * (y_b @ w_o_b[l])
        x = x + merged @ w_out[l]

        x = x + 0.5 * swiglu(rms_norm(x, g_ffn2[l]), w2_gate[l], w2_up[l], w2_down[l])
    return x


RET_HEADS = 8
RET_DK = 64
RET_DV = 128
DN_HEADS = 8
DN_DK = 128
DN_DV = 128
CHUNK = 128
SHORT_CONV = 4
FFN_CONV = 3
ROPE_BASE = 10000.0
GN_EPS = 1e-5

RET_QK = RET_HEADS * RET_DK
RET_V = RET_HEADS * RET_DV
DN_QK = DN_HEADS * DN_DK
DN_V = DN_HEADS * DN_DV
SPLITS = (RET_QK, RET_QK, RET_V, RET_V, DN_QK, DN_QK, DN_V, DN_V, DN_HEADS, DN_HEADS, D_MODEL, D_MODEL)
D_IN = sum(SPLITS)
DN_CONV_CH = 2 * DN_QK + DN_V


def rmsnorm(x, g):
    xf = x.astype(jnp.float32)
    r = lax.rsqrt(jnp.mean(xf * xf, axis=-1, keepdims=True) + EPS)
    return (xf * r) * g

def l2norm(x):
    xf = x.astype(jnp.float32)
    return xf * lax.rsqrt(jnp.sum(xf * xf, axis=-1, keepdims=True) + EPS)

def rotary(x):
    T, d = x.shape[1], x.shape[-1]
    inv = ROPE_BASE ** (-jnp.arange(0, d, 2, dtype=jnp.float32) / d)
    ang = jnp.arange(T, dtype=jnp.float32)[:, None] * inv[None, :]
    cos = jnp.cos(ang)[None, :, None, :]
    sin = jnp.sin(ang)[None, :, None, :]
    x1, x2 = x[..., : d // 2], x[..., d // 2:]
    return jnp.concatenate([x1 * cos - x2 * sin, x1 * sin + x2 * cos], axis=-1)

def causal_dwconv(x, w):
    K, T = w.shape[0], x.shape[1]
    xp = jnp.pad(x, ((0, 0), (K - 1, 0), (0, 0)))
    y = xp[:, K - 1:K - 1 + T] * w[K - 1]
    for k in range(K - 1):
        y = y + xp[:, k:k + T] * w[k]
    return y

def retention_chunkwise(q, k, v):
    B, T, H, dk = q.shape
    dv = v.shape[-1]
    N = T // CHUNK
    f32 = jnp.float32
    gamma = 1.0 - 2.0 ** (-5.0 - jnp.arange(H, dtype=f32))
    log_g = jnp.log(gamma)
    idx = jnp.arange(CHUNK, dtype=f32)
    qc = q.astype(f32).reshape(B, N, CHUNK, H, dk)
    kc = k.astype(f32).reshape(B, N, CHUNK, H, dk)
    vc = v.astype(f32).reshape(B, N, CHUNK, H, dv)
    diff = idx[:, None] - idx[None, :]
    causal = diff >= 0
    dmat = jnp.where(causal[None], jnp.exp(log_g[:, None, None] * jnp.where(causal, diff, 0.0)[None]), 0.0)
    scores = jnp.einsum('bnihd,bnjhd->bnhij', qc, kc) * dmat
    inner = jnp.einsum('bnhij,bnjhv->bnihv', scores, vc)
    zeta = jnp.exp(log_g[:, None] * (CHUNK - 1.0 - idx)[None, :])
    kv = jnp.einsum('bnjhd,hj,bnjhv->bnhdv', kc, zeta, vc)
    chunk_decay = jnp.exp(log_g * CHUNK)[:, None, None]

    def step(S, kv_n):
        return S * chunk_decay + kv_n, S

    _, s_prev = lax.scan(step, jnp.zeros((B, H, dk, dv), f32), jnp.moveaxis(kv, 1, 0))
    xi = jnp.exp(log_g[:, None] * (idx + 1.0)[None, :])
    cross = jnp.einsum('bnihd,nbhdv,hi->bnihv', qc, s_prev, xi)
    return (inner + cross).reshape(B, T, H, dv)

def gated_delta_chunkwise(q, k, v, g, beta):
    B, T, H, dk = q.shape
    dv = v.shape[-1]
    N = T // CHUNK
    f32 = jnp.float32

    def to_chunks(t):
        return jnp.moveaxis(t.astype(f32).reshape((B, N, CHUNK, H) + t.shape[3:]), 3, 1)

    qc = to_chunks(q) * (dk ** -0.5)
    kc = to_chunks(k)
    vc = to_chunks(v)
    gc = to_chunks(g)
    bc = to_chunks(beta)
    G = jnp.cumsum(gc, axis=-1)
    idx = jnp.arange(CHUNK)
    causal = idx[:, None] >= idx[None, :]
    strict = idx[:, None] > idx[None, :]
    diff = G[..., :, None] - G[..., None, :]
    L = jnp.where(causal, jnp.exp(jnp.where(causal, diff, 0.0)), 0.0)
    k_beta = kc * bc[..., None]
    A = jnp.where(strict, jnp.einsum('bhnid,bhnjd->bhnij', k_beta, kc) * L, 0.0)
    eye = jnp.eye(CHUNK, dtype=f32)
    rhs = jnp.concatenate([vc * bc[..., None], k_beta * jnp.exp(G)[..., None]], axis=-1)
    sol = lax.linalg.triangular_solve(eye + A, rhs, left_side=True, lower=True, unit_diagonal=True)
    u, w = sol[..., :dv], sol[..., dv:]
    attn = jnp.where(causal, jnp.einsum('bhnid,bhnjd->bhnij', qc, kc) * L, 0.0)
    q_dec = qc * jnp.exp(G)[..., None]
    k_dec = kc * jnp.exp(G[..., -1:] - G)[..., None]
    chunk_dec = jnp.exp(G[..., -1])

    def step(S, inp):
        u_n, w_n, q_n, k_n, a_n, d_n = inp
        v_new = u_n - jnp.einsum('bhcd,bhdv->bhcv', w_n, S)
        o = jnp.einsum('bhcd,bhdv->bhcv', q_n, S) + jnp.einsum('bhij,bhjv->bhiv', a_n, v_new)
        S = S * d_n[..., None, None] + jnp.einsum('bhcd,bhcv->bhdv', k_n, v_new)
        return S, o

    xs = tuple(jnp.moveaxis(t, 2, 0) for t in (u, w, q_dec, k_dec, attn, chunk_dec))
    _, o = lax.scan(step, jnp.zeros((B, H, dk, dv), f32), xs)
    return o.transpose(1, 0, 3, 2, 4).reshape(B, T, H, dv)

def second_inputs(seed: int = 0) -> dict:
    key = jax.random.key(seed)
    ks = jax.random.split(key, 20)
    f32 = jnp.float32
    nrm = lambda k, shape, s: jax.random.normal(k, shape, f32) * s
    dt = jnp.exp(jax.random.uniform(ks[6], (DEPTH, DN_HEADS), f32, np.log(1e-3), np.log(1e-1)))
    return {
        "x": jax.random.normal(ks[0], (BATCH, SEQ, D_MODEL), f32),
        "g_mix": 1.0 + nrm(ks[1], (DEPTH, D_MODEL), 0.05),
        "w_in": nrm(ks[2], (DEPTH, D_MODEL, D_IN), D_MODEL ** -0.5),
        "ret_norm_g": 1.0 + nrm(ks[3], (DEPTH, RET_V), 0.05),
        "dn_conv_w": nrm(ks[4], (DEPTH, SHORT_CONV, DN_CONV_CH), SHORT_CONV ** -0.5),
        "dn_a_log": jnp.log(jax.random.uniform(ks[5], (DEPTH, DN_HEADS), f32, 1.0, 16.0)),
        "dn_dt_bias": dt + jnp.log(-jnp.expm1(-dt)),
        "dn_norm_g": 1.0 + nrm(ks[7], (DEPTH, DN_DV), 0.05),
        "w_ret_br": nrm(ks[8], (DEPTH, RET_V, D_MODEL), RET_V ** -0.5),
        "w_dn_br": nrm(ks[9], (DEPTH, DN_V, D_MODEL), DN_V ** -0.5),
        "w_o": nrm(ks[10], (DEPTH, D_MODEL, D_MODEL), D_MODEL ** -0.5),
        "g_ffn": 1.0 + nrm(ks[11], (DEPTH, D_MODEL), 0.05),
        "w_up": nrm(ks[12], (DEPTH, D_MODEL, 2 * D_FF), D_MODEL ** -0.5),
        "ffn_conv_w": nrm(ks[13], (DEPTH, FFN_CONV, 2 * D_FF), FFN_CONV ** -0.5),
        "ffn_conv_b": nrm(ks[14], (DEPTH, 2 * D_FF), 0.01),
        "w_down": nrm(ks[15], (DEPTH, D_FF, D_MODEL), D_FF ** -0.5),
        "g_final": 1.0 + nrm(ks[16], (D_MODEL,), 0.05),
    }

def second_block(x, g_mix, w_in, ret_norm_g, dn_conv_w, dn_a_log, dn_dt_bias, dn_norm_g,
              w_ret_br, w_dn_br, w_o, g_ffn, w_up, ffn_conv_w, ffn_conv_b, w_down, g_final):
    B, T, _ = x.shape
    h = x.astype(jnp.float32)
    split_at = np.cumsum(SPLITS)[:-1].tolist()
    for l in range(DEPTH):
        u = rmsnorm(h, g_mix[l])
        proj = u @ w_in[l]
        (rq, rk, rv, rgate, dq, dk_, dv_, dz, db, da, gate_r, gate_d) = jnp.split(proj, split_at, axis=-1)

        rq = rotary(rq.reshape(B, T, RET_HEADS, RET_DK))
        rk = rotary(rk.reshape(B, T, RET_HEADS, RET_DK)) * (RET_DK ** -0.5)
        ro = retention_chunkwise(rq, rk, rv.reshape(B, T, RET_HEADS, RET_DV))
        mu = jnp.mean(ro, axis=-1, keepdims=True)
        var = jnp.mean(jnp.square(ro - mu), axis=-1, keepdims=True)
        ro = ((ro - mu) * lax.rsqrt(var + GN_EPS)).reshape(B, T, RET_V) * ret_norm_g[l]
        y_ret = (jax.nn.silu(rgate) * ro) @ w_ret_br[l]

        qkv = jax.nn.silu(causal_dwconv(jnp.concatenate([dq, dk_, dv_], axis=-1), dn_conv_w[l]))
        cq, ck, cv = jnp.split(qkv, [DN_QK, 2 * DN_QK], axis=-1)
        cq = l2norm(cq.reshape(B, T, DN_HEADS, DN_DK))
        ck = l2norm(ck.reshape(B, T, DN_HEADS, DN_DK))
        cv = cv.reshape(B, T, DN_HEADS, DN_DV)
        g = -jnp.exp(dn_a_log[l]) * jax.nn.softplus(da.astype(jnp.float32) + dn_dt_bias[l])
        beta = jax.nn.sigmoid(db.astype(jnp.float32))
        do = gated_delta_chunkwise(cq, ck, cv, g, beta)
        do = do * lax.rsqrt(jnp.mean(do * do, axis=-1, keepdims=True) + EPS) * dn_norm_g[l]
        do = do.reshape(B, T, DN_V) * jax.nn.silu(dz)
        y_dn = do @ w_dn_br[l]

        merged = jax.nn.sigmoid(gate_r) * y_ret + jax.nn.sigmoid(gate_d) * y_dn
        h = h + merged @ w_o[l]

        u2 = rmsnorm(h, g_ffn[l])
        up = causal_dwconv(u2 @ w_up[l], ffn_conv_w[l]) + ffn_conv_b[l]
        a, b = jnp.split(up, 2, axis=-1)
        h = h + (jax.nn.silu(a) * b) @ w_down[l]
    return rmsnorm(h, g_final).astype(x.dtype)


def setup_inputs(seed=0):
    out = dict(first_inputs(seed))
    for name, value in second_inputs(seed + 1).items():
        if name != "x":
            out[name + "_2"] = value
    return out


def reference(
    x, positions, g_ffn1, w1_gate, w1_up, w1_down, g_mix, w_in, g_cq, w_uq_a, w_q_idx, g_q_a,
    g_k_a, w_uv_a, w_o_a, w_o_b, w_out, g_ffn2, w2_gate, w2_up, w2_down, g_mix_2, w_in_2,
    ret_norm_g_2, dn_conv_w_2, dn_a_log_2, dn_dt_bias_2, dn_norm_g_2, w_ret_br_2, w_dn_br_2,
    w_o_2, g_ffn_2, w_up_2, ffn_conv_w_2, ffn_conv_b_2, w_down_2, g_final_2,
):
    x = first_block(
        x, positions, g_ffn1, w1_gate, w1_up, w1_down, g_mix, w_in, g_cq, w_uq_a, w_q_idx,
        g_q_a, g_k_a, w_uv_a, w_o_a, w_o_b, w_out, g_ffn2, w2_gate, w2_up, w2_down,
    )
    return second_block(
        x, g_mix_2, w_in_2, ret_norm_g_2, dn_conv_w_2, dn_a_log_2, dn_dt_bias_2, dn_norm_g_2,
        w_ret_br_2, w_dn_br_2, w_o_2, g_ffn_2, w_up_2, ffn_conv_w_2, ffn_conv_b_2, w_down_2,
        g_final_2,
    )


_drawn_inputs = setup_inputs


def setup_inputs(seed=0):
    import zlib

    import numpy as np

    out = dict(_drawn_inputs(seed))
    spreads = {}
    factors = {'g_ffn1': 3.939,
     'g_mix': 3.41,
     'g_cq': 6.108,
     'g_q_a': 8.0,
     'g_k_a': 8.0,
     'g_ffn2': 5.961,
     'ret_norm_g_2': 31.368,
     'dn_norm_g_2': 34.552,
     'ffn_conv_b_2': 64.0,
     'g_mix_2': 4.381,
     'g_ffn_2': 8.0}
    for name, (base, spread) in spreads.items():
        noise = np.random.default_rng([zlib.crc32(name.encode()), seed]).standard_normal(out[name].shape)
        drawn = base * np.exp(spread * noise) if base else spread * noise
        out[name] = __import__('jax').numpy.asarray(drawn.astype(out[name].dtype))
    for name, factor in factors.items():
        out[name] = (out[name] * factor).astype(out[name].dtype)
    return out
```

```python
import math

import numpy as np

import concourse.bass as bass
from concourse import mybir

F32 = mybir.dt.float32
F32R = mybir.dt.float32r
I32 = mybir.dt.int32
ALU = mybir.AluOpType
ACT = mybir.ActivationFunctionType
AX = mybir.AxisListType

P = 128
T = 512
NT = T // P
D = 1024
KD = D // P
FF = 2816
KF = FF // P
HALF = 256
STEPS = FF // HALF
EPS = 1e-6
GN_EPS = 1e-5
NEG = -1e30
TAKEN = -3e38
TOPK = min(256, T // 4)
TWO_PI = 2 * math.pi

NAMES = ['x', 'positions', 'g_ffn1', 'w1_gate', 'w1_up', 'w1_down', 'g_mix', 'w_in', 'g_cq', 'w_uq_a', 'w_q_idx',
         'g_q_a', 'g_k_a', 'w_uv_a', 'w_o_a', 'w_o_b', 'w_out', 'g_ffn2', 'w2_gate', 'w2_up', 'w2_down',
         'g_mix_2', 'w_in_2', 'ret_norm_g_2', 'dn_conv_w_2', 'dn_a_log_2', 'dn_dt_bias_2', 'dn_norm_g_2',
         'w_ret_br_2', 'w_dn_br_2', 'w_o_2', 'g_ffn_2', 'w_up_2', 'ffn_conv_w_2', 'ffn_conv_b_2', 'w_down_2',
         'g_final_2']


def two_blocks_kernel(nc, A, out):
    sb_next = [16512]

    def at(name, shape, dt=F32, offset=None):
        size = 4 * int(np.prod(shape[1:]))
        if offset is None:
            offset = sb_next[0]
            sb_next[0] += (size + 31) // 32 * 32
        assert offset + size <= 229368, (name, offset + size)
        return nc.alloc_sbuf_tensor_at(name, shape, dt, offset=offset)

    def sem(name):
        return nc.alloc_semaphore(name)

    raw = at("raw", [P, 2, 2048])
    wh = at("wh", [P, 2, 2048], F32R)
    wl = at("wl", [P, 2, 2048], F32R)
    xT = at("xT", [P, KD, T])
    h_hi = at("h_hi", [P, KD, T], F32R)
    h_lo = at("h_lo", [P, KD, T], F32R)
    work = at("work", [P, 4096])
    vecs = at("vecs", [P, 4, P])
    ident = at("ident", [P, P])
    ones = at("ones", [P, P])
    cos = at("cos", [P, 2 * NT, 32])
    sin = at("sin", [P, 2 * NT, 32])
    wi_raw = at("wi_raw", [P, KD, 8])
    wi_h = at("wi_h", [P, KD, 8], F32R)
    wi_l = at("wi_l", [P, KD, 8], F32R)
    eps_c = at("eps_c", [P, 1])
    one_c = at("one_c", [P, 1])
    widx = at("widx", [P, NT, 8])
    stat = at("stat", [P, 64])
    rstat = at("rstat", [P, 64])
    SCOPE = sb_next[0]

    PS = nc.alloc_psum_tensor("PS", [P, 8, 512], F32)

    G_FFN1, G_MIX, G_FFN2, G_MIX2, G_FFNB, G_FINAL, G_RET, G_DN, G_CQ = 0, 8, 16, 24, 32, 40, 48, 56, 57
    N_ROWS0 = 59

    def gain(base, k):
        return vecs[:, 0, base + k:base + k + 1]

    counts = [("up0", 22), ("dn0", 22), ("mid1", 10), ("merge1", 12), ("wout", 8), ("up1", 22), ("dn1", 22),
              ("ret", 12), ("merge2a", 8), ("dn", 16), ("merge2b", 8), ("wo", 8), ("up2", 22), ("dn2", 22)]
    U = {}
    n = 0
    for name, c in counts:
        U[name] = n
        n += c

    w_in = [sem("w_in0"), sem("w_in1")]
    w_hi = sem("w_hi")
    w_lo = sem("w_lo")
    w_used = sem("w_used")
    dve_step, act_step, pool_step = sem("dve_step"), sem("act_step"), sem("pool_step")
    count = {"d": 0, "a": 0, "p": 0}

    def dve_link(ins):
        count["d"] += 1
        ins.then_inc(dve_step, 1)
        nc.vector.wait_ge(dve_step, count["d"])

    def act_link(ins):
        count["a"] += 1
        ins.then_inc(act_step, 1)
        nc.scalar.wait_ge(act_step, count["a"])

    def pool_link(ins):
        count["p"] += 1
        ins.then_inc(pool_step, 1)
        nc.gpsimd.wait_ge(pool_step, count["p"])

    def load(sp, u, slot, pieces):
        if not isinstance(u, int) or u >= 2:
            sp.wait_ge(w_lo, u - 1)
        for dst, src in pieces:
            sp.dma_start(dst, src).then_inc(w_in[slot], 16)

    def panel(sp, u, w, k0, nk, c0):
        dst = raw[:, u % 2, 0:nk * 512].rearrange("p (k c) -> p k c", k=nk)
        src = w[k0 * P:(k0 + nk) * P, c0:c0 + 512].rearrange("(k p) c -> p k c", p=P)
        h = nk // 2
        load(sp, u, u % 2, [(dst[:, 0:h], src[:, 0:h]), (dst[:, h:nk], src[:, h:nk])])

    def round_unit(act, u, slot, half_u, size=2048):
        act.wait_ge(w_in[slot], 32 * (half_u + 1))
        if not isinstance(u, int) or u >= 2:
            act.wait_ge(w_used, u - 1)
        nc.scalar.activation(wh[:, slot, 0:size], raw[:, slot, 0:size], ACT.Copy).then_inc(w_hi, 1)

    def rounds(act, u, n, size=2048):
        for j in range(u, u + n):
            round_unit(act, j, j % 2, j // 2, size)

    def lo_unit(pool, u, slot, size=2048):
        pool.wait_ge(w_hi, u + 1)
        nc.gpsimd.tensor_tensor(wl[:, slot, 0:size], raw[:, slot, 0:size], wh[:, slot, 0:size].bitcast(F32),
                                ALU.subtract).then_inc(w_lo, 1)

    def los(pool, u, n, size=2048):
        for j in range(u, u + n):
            lo_unit(pool, j, j % 2, size)

    def mm3(dst, sh, sl, mh, ml, start, stop):
        nc.tensor.matmul(dst, sh, mh, start=start, stop=False)
        nc.tensor.matmul(dst, sh, ml, start=False, stop=False)
        return nc.tensor.matmul(dst, sl, mh, start=False, stop=stop)

    def unit_T(pe, u, slot, bank, k0, nk, mh, ml, first, last, ready=None):
        pe.wait_ge(w_lo, u + 1)
        W, L = (x[:, slot, 0:nk * 512].rearrange("p (k c) -> p k c", k=nk) for x in (wh, wl))
        for k in range(nk):
            if ready:
                pe.wait_ge(ready[0], ready[1] + k0 + k + 1)
            for m in range(4):
                ins = mm3(PS[:, bank + m, :], W[:, k, m * P:(m + 1) * P], L[:, k, m * P:(m + 1) * P],
                          mh[:, k0 + k, :], ml[:, k0 + k, :], first and k == 0, last and k == nk - 1)
        ins.then_inc(w_used, 1)
        return ins

    def unit_N(pe, u, bank, k0, nk, sh, sl, first, last, ready=None):
        pe.wait_ge(w_lo, u + 1)
        W, L = (x[:, u % 2, 0:nk * 512].rearrange("p (k c) -> p k c", k=nk) for x in (wh, wl))
        for k in range(nk):
            if ready:
                pe.wait_ge(ready[0], ready[1] + k0 + k + 1)
            for t in range(NT):
                a, b = sh[:, k0 + k, t * P:(t + 1) * P], sl[:, k0 + k, t * P:(t + 1) * P]
                dst = PS[:, bank + t, :]
                nc.tensor.matmul(dst, a, W[:, k, :], start=first and k == 0, stop=False)
                nc.tensor.matmul(dst, a, L[:, k, :], start=False, stop=False)
                ins = nc.tensor.matmul(dst, b, W[:, k, :], start=False, stop=last and k == nk - 1)
        ins.then_inc(w_used, 1)
        return ins

    crow = at("crow", [P, 4, P], offset=SCOPE)
    xnat = at("xnat", [P, NT, D], offset=SCOPE + 2048)
    posi = at("posi", [P, 2 * NT], I32, offset=SCOPE + 2048 + 16384)
    posf = at("posf", [P, 2 * NT], offset=SCOPE + 2048 + 16384 + 32)
    invf = at("invf", [P, 32], offset=SCOPE + 2048 + 16384 + 64)
    ang = at("ang", [P, 2 * NT, 32], offset=SCOPE + 2048 + 16384 + 192)
    turn = at("turn", [P, 2 * NT, 32], offset=SCOPE + 2048 + 16384 + 192 + 1024)
    over = at("over", [P, 2 * NT, 32], offset=SCOPE + 2048 + 16384 + 192 + 2048)
    consts_in, x_in, consts_set, crow_T, vecs_set, x_T, tables_set, angles_set = (
        sem(s) for s in ("consts_in", "x_in", "consts_set", "crow_T", "vecs_set", "x_T", "tables_set", "angles_set"))
    x_ready = sem("x_ready")
    wi_hi, wi_lo = sem("wi_hi"), sem("wi_lo")
    N_CONST_DMAS = 15

    def start_act_queue(act):
        rows = [(0, G_FFN1, 'g_ffn1', KD), (0, G_MIX, 'g_mix', KD), (0, G_FFN2, 'g_ffn2', KD),
                (0, G_MIX2, 'g_mix_2', KD), (0, G_FFNB, 'g_ffn_2', KD), (0, G_RET, 'ret_norm_g_2', KD),
                (0, G_DN, 'dn_norm_g_2', 1), (0, G_CQ, 'g_cq', 2)]
        for tile, row, name, n in rows:
            act.dma_start(crow[row:row + n, tile, :], A[name][0].rearrange("(k p) -> k p", p=P)).then_inc(consts_in, 16)
        act.dma_start(crow[G_FINAL:G_FINAL + KD, 0, :], A['g_final_2'].rearrange("(k p) -> k p", p=P)).then_inc(consts_in, 16)
        act.dma_start(crow[0:96, 1, :], A['dn_conv_w_2'][0].rearrange("w (k p) -> (w k) p", p=P)).then_inc(consts_in, 16)
        act.dma_start(crow[0:88, 2, :], A['ffn_conv_w_2'][0, 0:2].rearrange("w (k p) -> (w k) p", p=P)).then_inc(consts_in, 16)
        act.dma_start(crow[0:44, 3, :], A['ffn_conv_w_2'][0, 2:3].rearrange("w (k p) -> (w k) p", p=P)).then_inc(consts_in, 16)
        act.dma_start(crow[44:88, 3, :], A['ffn_conv_b_2'][0].rearrange("(k p) -> k p", p=P)).then_inc(consts_in, 16)
        act.dma_start(wi_raw[:, :, :], A['w_in'][0, :, 512:520].rearrange("(k p) c -> p k c", p=P)).then_inc(consts_in, 16)
        with nc.allow_non_contiguous_dma("512 positions, token on partition"):
            act.dma_start(posi[:, 0:NT], A['positions'][0].rearrange("(t p) -> p t", p=P)).then_inc(consts_in, 16)

    def start_sp(sp):
        xs = A['x'][0].rearrange("(t p) d -> p t d", p=P)
        for t in range(NT):
            sp.dma_start(xnat[:, t, :], xs[:, t, :]).then_inc(x_in, 16)

    def start_pool(pool):
        pool.memset(ident[:, :], 0.0)
        pool.memset(ones[:, :], 1.0)
        for j in range(32):
            f = float(np.float32(np.float32(10000.0) ** (-np.float32(2 * j) / np.float32(64))))
            pool.memset(invf[:, j:j + 1], f)
        pool.memset(eps_c[:, :], EPS)
        pool.memset(one_c[:, :], 1.0)
        pool_link(pool.iota(posi[:, NT:2 * NT], pattern=[[P, NT]], base=0, channel_multiplier=1))
        pool.affine_select(out=ident[:, :], in_=ident[:, :], compare_op=ALU.not_equal, fill=1.0, base=0,
                           pattern=[[-1, P]], channel_multiplier=1).then_inc(consts_set, 1)
        pool.wait_ge(wi_hi, 1)
        pool.tensor_tensor(wi_l[:, :, :], wi_raw[:, :, :], wi_h[:, :, :].bitcast(F32), ALU.subtract).then_inc(wi_lo, 1)

    def start_pe(pe):
        pe.wait_ge(consts_set, 1)
        pe.wait_ge(consts_in, 16 * N_CONST_DMAS)
        for tile, n in enumerate((N_ROWS0, 96, 88, 88)):
            ins = pe.transpose(PS[:, 7, tile * P:tile * P + n], crow[0:n, tile, :], ident[0:n, 0:n])
        ins.then_inc(crow_T, 1)
        pe.wait_ge(x_in, 16 * NT)
        pe.wait_ge(vecs_set, 1)
        for k in range(KD):
            for t in range(NT):
                ins = pe.transpose(PS[:, k, t * P:(t + 1) * P], xnat[:, t, k * P:(k + 1) * P], ident[:, :])
            ins.then_inc(x_T, 1)

    def start_dve(dve):
        dve.wait_ge(crow_T, 1)
        for tile, n in enumerate((N_ROWS0, 96, 88, 88)):
            ins = dve.tensor_copy(vecs[:, tile, 0:n], PS[:, 7, tile * P:tile * P + n])
        ins.then_inc(vecs_set, 1)
        for k in range(KD):
            dve.wait_ge(x_T, k + 1)
            dve.tensor_copy(xT[:, k, :], PS[:, k, :]).then_inc(x_ready, 1)
        dve.wait_ge(consts_set, 1)
        dve_link(dve.tensor_copy(posf[:, :], posi[:, :]))
        dve_link(dve.tensor_tensor(ang[:, :, :], posf[:, :].unsqueeze(2).to_broadcast([P, 2 * NT, 32]),
                                   invf[:, :].unsqueeze(1).to_broadcast([P, 2 * NT, 32]), ALU.mult))
        magic = 1.5 * 2 ** 23
        dve_link(dve.tensor_scalar(turn[:, :, :], ang[:, :, :], 1 / TWO_PI, magic, ALU.mult, ALU.add))
        dve_link(dve.tensor_scalar(turn[:, :, :], turn[:, :, :], magic, None, ALU.subtract))
        c1 = 6.28125
        c2 = float(np.round((TWO_PI - c1) * 2 ** 20) / 2 ** 20)
        c3 = TWO_PI - c1 - c2
        for c in (c1, c2, c3):
            dve_link(dve.scalar_tensor_tensor(ang[:, :, :], turn[:, :, :], -c, ang[:, :, :], ALU.mult, ALU.add))
        lim = float(np.nextafter(np.float32(math.pi), np.float32(0)))
        dve_link(dve.tensor_scalar(turn[:, :, :], ang[:, :, :], math.pi / 2, None, ALU.add))
        dve_link(dve.tensor_scalar(over[:, :, :], turn[:, :, :], math.pi, -TWO_PI, ALU.is_gt, ALU.mult))
        dve_link(dve.tensor_tensor(turn[:, :, :], turn[:, :, :], over[:, :, :], ALU.add))
        dve_link(dve.tensor_scalar(turn[:, :, :], turn[:, :, :], lim, -lim, ALU.min, ALU.max))
        dve.tensor_scalar(ang[:, :, :], ang[:, :, :], lim, -lim, ALU.min, ALU.max).then_inc(angles_set, 1)

    def start_act(act):
        act.wait_ge(consts_in, 16 * N_CONST_DMAS)
        act.activation(wi_h[:, :, :], wi_raw[:, :, :], ACT.Copy).then_inc(wi_hi, 1)
        act.wait_ge(angles_set, 1)
        act.activation(sin[:, :, :], ang[:, :, :], ACT.Sin)
        act.activation(cos[:, :, :], turn[:, :, :], ACT.Sin).then_inc(tables_set, 1)

    sq = work[:, 0:1024].rearrange("p (a b) -> p a b", a=2)
    hf = work[:, 1024:2048].rearrange("p (a b) -> p a b", a=2)
    rstd = work[:, 2048:2560]
    sq_ready, sq_used, sd_ready, hf_ready, hi_ready, h_ready = (
        sem(s) for s in ("sq_ready", "sq_used", "sd_ready", "hf_ready", "hi_ready", "h_ready"))

    def norm_act(act, n, u=None, size=2048):
        for k in range(KD):
            act.wait_ge(x_ready, KD * n + k + 1)
            if k >= 2:
                act.wait_ge(sq_used, KD * n + k - 1)
            act.activation(sq[:, k % 2, :], xT[:, k, :], ACT.Square).then_inc(sq_ready, 1)
        if u is not None:
            rounds(act, u, 2, size)
        act.wait_ge(sq_used, KD * (n + 1))
        act.activation(rstd, PS[:, 0, :], ACT.Sqrt, bias=eps_c[:, :], scale=1.0 / D).then_inc(sd_ready, 1)
        if u is not None:
            for k in range(KD):
                act.wait_ge(hf_ready, KD * n + k + 1)
                act.activation(h_hi[:, k, :], hf[:, k % 2, :], ACT.Copy).then_inc(hi_ready, 1)

    def norm_pe(pe, n):
        for k in range(KD):
            pe.wait_ge(sq_ready, KD * n + k + 1)
            ins = nc.tensor.matmul(PS[:, 0, :], ones[:, :], sq[:, k % 2, :], start=k == 0, stop=k == KD - 1)
            ins.then_inc(sq_used, 1)

    def norm_dve(dve, n, g):
        dve.wait_ge(sd_ready, n + 1)
        dve_link(dve.reciprocal(rstd, rstd))
        for k in range(KD):
            if k >= 2:
                dve.wait_ge(h_ready, KD * n + k - 1)
            dve.scalar_tensor_tensor(hf[:, k % 2, :], xT[:, k, :], gain(g, k), rstd, ALU.mult, ALU.mult).then_inc(hf_ready, 1)

    def norm_pool(pool, n, u, size=2048):
        los(pool, u, 2, size)
        for k in range(KD):
            pool.wait_ge(hi_ready, KD * n + k + 1)
            pool.tensor_tensor(h_lo[:, k, :], hf[:, k % 2, :], h_hi[:, k, :].bitcast(F32), ALU.subtract).then_inc(h_ready, 1)

    act_hi = at("act_hi", [P, KF, T], F32R, offset=SCOPE)
    act_lo = at("act_lo", [P, KF, T], F32R, offset=SCOPE + KF * T * 4)
    sg = work[:, 0:2048].rearrange("p (a b) -> p a b", a=2)
    prod = work[:, 2048:4096].rearrange("p (a b) -> p a b", a=2)
    taps_in = work[:, 0:2048].rearrange("p (a b) -> p a b", a=4)
    taps_out = work[:, 2048:4096].rearrange("p (a b) -> p a b", a=4)
    up_mm, up_ev, sg_ready, conv_done, prod_ready, a_hi, a_ready, dn_done = (
        sem(s) for s in ("up_mm", "up_ev", "sg_ready", "conv_done", "prod_ready", "a_hi", "a_ready", "dn_done"))

    def up_sp(sp, f, wg, wu):
        u0 = U[f"up{f}"]

        def step(i):
            for s in range(2):
                dst = raw[:, s, :].rearrange("p (k c) -> p k c", k=4)
                pieces = []
                for j, (w, c0) in enumerate((wg, wu)):
                    src = w[s * 512:(s + 1) * 512, bass.ds(i * HALF + c0, HALF)].rearrange("(k p) c -> p k c", p=P)
                    pieces.append((dst[:, :, j * HALF:(j + 1) * HALF], src))
                load(sp, u0 + 2 * i + s, s, pieces)

        step(0)
        with sp.Fori(1, STEPS) as i:
            step(i)

    def up_pool(pool, f):
        u0 = U[f"up{f}"]
        with pool.Fori(1, STEPS) as i:
            for s in range(2):
                lo_unit(pool, u0 + 2 * i + s, s)

    def up_pe(pe, f):
        u0, b0 = U[f"up{f}"], STEPS * f

        def step(i, bank):
            fresh = None
            if isinstance(i, int) and i == 0:
                fresh = (h_ready, KD * (0, 2, 4)[f])
            elif not isinstance(i, int) or i > 1 or f:
                pe.wait_ge(up_ev, b0 + i - 1)
            unit_T(pe, u0 + 2 * i, 0, bank, 0, 4, h_hi, h_lo, True, False, fresh)
            unit_T(pe, u0 + 2 * i + 1, 1, bank, 4, 4, h_hi, h_lo, False, True, fresh)

        step(0, 0)
        step(1, 4)
        step(2, 0)
        with pe.Fori(1, STEPS // 2) as pair:
            step(2 * pair + 1, 4)
            step(2 * pair + 2, 0)

    def up_act(act, f):
        u0, b0 = U[f"up{f}"], STEPS * f

        def evac(j, bank, par):
            act.wait_ge(w_used, u0 + 2 * j + 2)
            if f < 2:
                act.activation(sg[:, par, :].rearrange("p (a b) -> p a b", a=2), PS[:, bank:bank + 2, :],
                               ACT.Silu).then_inc(sg_ready, 1)
                act.wait_ge(up_ev, b0 + j + 1)
                src = prod[:, par, :].rearrange("p (a b) -> p a b", a=2)
            else:
                act.activation(taps_in[:, :, :], PS[:, bank:bank + 4, :], ACT.Copy).then_inc(up_ev, 1)
                act.wait_ge(conv_done, j + 1)
                act.activation(taps_out[:, 0:2, :], taps_out[:, 0:2, :], ACT.Silu).then_inc(sg_ready, 1)
                act.wait_ge(prod_ready, j + 1)
                src = taps_out[:, 0:2, :]
            act.activation(act_hi[:, bass.ds(2 * j, 2), :], src, ACT.Copy).then_inc(a_hi, 1)

        def rnd(i):
            for s in range(2):
                round_unit(act, u0 + 2 * i + s, s, u0 // 2 + i)

        with act.Fori(0, STEPS // 2) as pair:
            i = 2 * pair + 1
            rnd(i)
            evac(i - 1, 0, 0)
            rnd(i + 1)
            evac(i, 4, 1)
        return lambda: evac(STEPS - 1, 0, 0)

    def up_dve(dve, f):
        b0 = STEPS * f

        def step(j, bank, par):
            if f < 2:
                dve.wait_ge(sg_ready, b0 + j + 1)
                src = prod[:, par, :].rearrange("p (a b) -> p a b", a=2)
                dve.tensor_tensor(src, sg[:, par, :].rearrange("p (a b) -> p a b", a=2), PS[:, bank + 2:bank + 4, :],
                                  ALU.mult).then_inc(up_ev, 1)
            else:
                dve.wait_ge(up_ev, b0 + j + 1)
                dve.wait_ge(a_ready, b0 + j)
                taps(dve, j)
                dve.wait_ge(sg_ready, b0 + j + 1)
                src = taps_out[:, 0:2, :]
                dve.tensor_tensor(src, src, taps_out[:, 2:4, :], ALU.mult).then_inc(prod_ready, 1)
            dve.wait_ge(a_hi, b0 + j + 1)
            dve.tensor_tensor(act_lo[:, bass.ds(2 * j, 2), :], src, act_hi[:, bass.ds(2 * j, 2), :].bitcast(F32),
                              ALU.subtract).then_inc(a_ready, 1)

        step(0, 0, 0)
        with dve.Fori(0, STEPS // 2) as pair:
            i = 2 * pair + 1
            step(i, 4, 1)
            step(i + 1, 0, 0)

    tap_a, tap_b = sem("tap_a"), sem("tap_b")

    def taps(dve, j):
        tiles = [(m, 2 * j + m if m < 2 else KF + 2 * j + m - 2) for m in range(4)]

        def col(tile, row):
            return vecs[:, tile, bass.ds(row, 1)]

        for m, c in tiles:
            ins = dve.tensor_scalar(taps_out[:, m, :], taps_in[:, m, :], col(3, c), col(3, c + 44), ALU.mult, ALU.add)
        ins.then_inc(tap_a, 1)
        dve.wait_ge(tap_a, j + 1)
        for m, c in tiles:
            ins = dve.scalar_tensor_tensor(taps_out[:, m, 1:T], taps_in[:, m, 0:T - 1], col(2, c + 44),
                                           taps_out[:, m, 1:T], ALU.mult, ALU.add)
        ins.then_inc(tap_b, 1)
        dve.wait_ge(tap_b, j + 1)
        for m, c in tiles:
            ins = dve.scalar_tensor_tensor(taps_out[:, m, 2:T], taps_in[:, m, 0:T - 2], col(2, c),
                                           taps_out[:, m, 2:T], ALU.mult, ALU.add)
        ins.then_inc(conv_done, 1)

    def half_ready(pe, signal):
        def wait(i):
            if isinstance(i, int) and i == 0:
                pe.wait_ge(signal, 2)
            else:
                pe.wait_ge(signal, 4 if isinstance(i, int) else 2 * i)
        return wait

    def down_sp(sp, stage, w, steps):
        u0 = U[stage]
        with sp.Fori(0, steps) as i:
            for s in range(2):
                pieces = [(raw[:, s, c:c + 512], w[bass.ds((2 * i + s) * P, P), c:c + 512]) for c in (0, 512)]
                load(sp, u0 + 2 * i + s, s, pieces)

    def down_act(act, stage, steps, before=None):
        u0 = U[stage]

        def rnd(i):
            for s in range(2):
                round_unit(act, u0 + 2 * i + s, s, u0 // 2 + i, 1024)

        if before:
            rnd(0)
            before()
            with act.Fori(1, steps) as i:
                rnd(i)
        else:
            with act.Fori(0, steps) as i:
                rnd(i)

    def down_pool(pool, stage, steps):
        with pool.Fori(0, steps) as i:
            for s in range(2):
                lo_unit(pool, U[stage] + 2 * i + s, s, 1024)

    def down_pe(pe, stage, order, steps, mh, ml, ready=None):
        u0 = U[stage]

        def step(i, first=False, last=False):
            if callable(ready):
                ready(i)
            elif ready:
                pe.wait_ge(ready[0], ready[1] + i + 1)
            for s in range(2):
                pe.wait_ge(w_lo, u0 + 2 * i + s + 1)
                for m in range(KD):
                    ins = mm3(PS[:, m, :], wh[:, s, m * P:(m + 1) * P], wl[:, s, m * P:(m + 1) * P],
                              mh[:, bass.ds(2 * i + s, 1), :].rearrange("p a b -> p (a b)"),
                              ml[:, bass.ds(2 * i + s, 1), :].rearrange("p a b -> p (a b)"),
                              first and s == 0, last and s == 1)
                    if last and s == 1 and m < KD - 1:
                        ins.then_inc(dn_done, 1)
                ins.then_inc(w_used, 1)

        step(0, first=True)
        with pe.Fori(1, steps - 1) as i:
            step(i)
        step(steps - 1, last=True)

    def down_dve(dve, stage, order, steps, scale):
        for m in range(KD):
            if m < KD - 1:
                dve.wait_ge(dn_done, (KD - 1) * order + m + 1)
            else:
                dve.wait_ge(w_used, U[stage] + 2 * steps)
            dve.scalar_tensor_tensor(xT[:, m, :], PS[:, m, :], scale, xT[:, m, :], ALU.mult, ALU.add).then_inc(x_ready, 1)

    Y_B, Y_A, R1, R3 = SCOPE, SCOPE + 16384, SCOPE + 32768, SCOPE + 32768 + 24576
    QPAIRS = 4
    PER = 64

    def stack(offset, *specs):
        got = []
        for name, shape, dt in specs:
            got.append(at(name, shape, dt, offset=offset))
            offset += 4 * int(np.prod(shape[1:]))
        return got

    yb_hi, yb_lo = stack(Y_B, ("yb_hi", [P, 4, T], F32R), ("yb_lo", [P, 4, T], F32R))
    ya_hi, ya_lo = stack(Y_A, ("ya_hi", [P, 4, T], F32R), ("ya_lo", [P, 4, T], F32R))
    cq_hi, cq_lo, qn = stack(Y_A, ("cq_hi", [P, 2, T], F32R), ("cq_lo", [P, 2, T], F32R), ("qn", [P, NT, 512], F32))
    qbT, kbT, vb = stack(R1, ("qbT", [P, 4, T], F32), ("kbT", [P, 4, T], F32), ("vb", [P, NT, 512], F32))
    lg, pr, pT, olT = stack(R1, ("lg", [P, 2, T], F32), ("pr", [P, 2, T], F32), ("pT", [P, NT, 512], F32),
                            ("olT", [P, 512], F32))
    soff = [None, 0, 2 * P, 5 * P, 9 * P]
    score, lgi = stack(Y_A, ("score", [P, soff[4]], F32), ("lgi", [P, 2, T], F32))
    pn, qaT, qiT, kaT, kiT, wuv, gq, gk, lower, negtri, negone = stack(
        R3, ("pn", [P, NT, 512], F32), ("qaT", [P, 4, T], F32), ("qiT", [P, 4, T], F32), ("kaT", [P, T], F32),
        ("kiT", [P, T], F32), ("wuv", [P, 8, 64], F32), ("gq", [P, 64], F32), ("gk", [P, 64], F32),
        ("lower", [P, P], F32), ("negtri", [P, P], F32), ("negone", [P, P], F32))
    drop = at("drop", [P, soff[4]], offset=R3 + 16384)
    mg_hi, mg_lo, gt, gt2 = stack(R1, ("mg_hi", [P, KD, T], F32R), ("mg_lo", [P, KD, T], F32R),
                                  ("gt", [P, 2048], F32), ("gt2", [P, 2048], F32))
    mtmp = work[:, 0:2048]
    r1, r2 = work[:, 0:1024], work[:, 1024:2048]
    rot = work[:, 2048:4096]
    off = [0, 512, 1024, 896]
    wid = [512, 384, 256, 128]
    SPAN = 1280
    stick = work[:, 0:3 * SPAN].rearrange("p (a b) -> p a b", a=3)

    (m1_consts, m1_dma, pn_mm, pn_ev, wi_mm, wi_ev, qb_ev, kb_ev, vb_ev, cqn_set, cq_T, cq_hi_s, cq_s, kd_set, kd_T,
     kT_ev, qa_sq, qa_set, qa_T, qa_ev, qi_set, qi_T, qi_ev, m1_sd) = (
        sem("m1_" + s) for s in ("consts dma pn_mm pn_ev wi_mm wi_ev qb_ev kb_ev vb_ev cqn_set cq_T cq_hi cq_set kd_set kd_T "
                                 "kT_ev qa_sq qa_set qa_T qa_ev qi_set qi_T qi_ev sd").split())
    b_z, b_abs, b_ln, b_sp, b_spm, b_acc, b_exp, b_am, b_pv, b_hi, b_lo = (
        sem("b_" + s) for s in "z abs ln sp spm acc exp am pv hi lo".split())
    a_dot, a_relu, a_causal, a_lg, a_lgm, a_exp, a_pr, a_pT, a_pTev, a_ol, a_olev, a_o, a_yhi, a_ylo = (
        sem("a_" + s) for s in "dot relu causal lg lgm exp pr pT pTev ol olev o yhi ylo".split())
    a_rused = sem("a_rused")
    g_sig, g_mul, g_hi, mg_ready = (sem("g_" + s) for s in "sig mul hi ready".split())
    u1 = U["mid1"]

    def bcast_h(table, heads):
        return table.unsqueeze(2).to_broadcast([P, NT, heads, 32])

    def rotate(link, src, dst, tab, heads, last=None):
        c, s = bcast_h(cos[:, tab:tab + NT, :], heads), bcast_h(sin[:, tab:tab + NT, :], heads)
        n = NT * heads * 32
        a = r1[:, 0:n].rearrange("p (t h d) -> p t h d", t=NT, h=heads)
        b = r2[:, 0:n].rearrange("p (t h d) -> p t h d", t=NT, h=heads)
        x1, x2 = src[:, :, :, 0:32], src[:, :, :, 32:64]
        v = nc.vector
        v.tensor_tensor(a, x1, c, ALU.mult)
        link(v.tensor_tensor(b, x2, s, ALU.mult))
        link(v.tensor_tensor(dst[:, :, :, 0:32], a, b, ALU.subtract))
        v.tensor_tensor(a, x1, s, ALU.mult)
        link(v.tensor_tensor(b, x2, c, ALU.mult))
        return v.tensor_tensor(dst[:, :, :, 32:64], a, b, ALU.add)

    def mid1_sp(sp):
        w = A['w_in'][0]
        for j, c0 in enumerate((0, 520, 1032, 1544)):
            panel(sp, u1 + 2 * j, w, 0, 4, c0)
            panel(sp, u1 + 2 * j + 1, w, 4, 4, c0)
        panel(sp, u1 + 8, A['w_uq_a'][0], 0, 2, 0)
        panel(sp, u1 + 9, A['w_q_idx'][0], 0, 2, 0)

    def mid1_pool(pool):
        pool.wait_ge(x_ready, KD * 2)
        pool.memset(negone[:, :], -1.0)
        pool_link(pool.memset(lower[:, :], 0.0))
        pool.affine_select(out=negtri[:, :], in_=negone[:, :], compare_op=ALU.is_ge, fill=0.0, base=0,
                           pattern=[[-1, P]], channel_multiplier=1)
        pool.affine_select(out=lower[:, :], in_=lower[:, :], compare_op=ALU.is_ge, fill=NEG, base=0,
                           pattern=[[-1, P]], channel_multiplier=1).then_inc(m1_consts, 1)
        los(pool, u1 + 2, 6)
        los(pool, u1 + 8, 2, 1024)
        los(pool, U["merge1"], 2)
        for i in range(1, NT):
            pool.wait_ge(a_rused, 8 * i)
            d = score[:, soff[i] + i * P:soff[i + 1]]
            pool.affine_select(out=d, in_=d, compare_op=ALU.is_ge, fill=NEG, base=0,
                               pattern=[[-1, P]], channel_multiplier=1).then_inc(a_causal, 1)
        for h in range(8 + 1):
            if h < 8:
                pool.wait_ge(b_sp, h + 1)
                earlier_keys(pool, h).then_inc(b_spm, 1)
            if h:
                pool.wait_ge(b_exp, h)
                earlier_keys(pool, h - 1).then_inc(b_am, 1)

    def earlier_keys(pool, h):
        for j in range(NT):
            d = stick[:, h % 3, off[j]:off[j] + P]
            ins = pool.affine_select(out=d, in_=d, compare_op=ALU.is_gt, fill=0.0, base=0,
                                     pattern=[[1, P]], channel_multiplier=-1)
        return ins

    def mid1_pe(pe):
        unit_N(pe, u1, 0, 0, 4, h_hi, h_lo, True, False, (h_ready, KD))
        unit_N(pe, u1 + 1, 0, 4, 4, h_hi, h_lo, False, True, (h_ready, KD))
        pe.wait_ge(wi_lo, 1)
        for t in range(NT):
            for k in range(KD):
                a, b = h_hi[:, k, t * P:(t + 1) * P], h_lo[:, k, t * P:(t + 1) * P]
                nc.tensor.matmul(PS[:, 4 + t, 0:8], a, wi_h[:, k, :], start=k == 0, stop=False)
                nc.tensor.matmul(PS[:, 4 + t, 0:8], a, wi_l[:, k, :], start=False, stop=False)
                ins = nc.tensor.matmul(PS[:, 4 + t, 0:8], b, wi_h[:, k, :], start=False, stop=k == KD - 1)
        ins.then_inc(wi_mm, 1)
        pe.wait_ge(pn_ev, 1)
        unit_T(pe, u1 + 2, 0, 0, 0, 4, h_hi, h_lo, True, False)
        unit_T(pe, u1 + 3, 1, 0, 4, 4, h_hi, h_lo, False, True)
        pe.wait_ge(wi_ev, 1)
        unit_T(pe, u1 + 4, 0, 4, 0, 4, h_hi, h_lo, True, False)
        unit_T(pe, u1 + 5, 1, 4, 4, 4, h_hi, h_lo, False, True)
        pe.wait_ge(qb_ev, 1)
        unit_N(pe, u1 + 6, 0, 0, 4, h_hi, h_lo, True, False)
        unit_N(pe, u1 + 7, 0, 4, 4, h_hi, h_lo, False, True)
        pe.wait_ge(kb_ev, 1)
        pe.wait_ge(cqn_set, 1)
        for k in range(2):
            for t in range(NT):
                ins = pe.transpose(PS[:, 4 + k, t * P:(t + 1) * P], pn[:, t, k * P:(k + 1) * P], ident[:, :])
        ins.then_inc(cq_T, 1)
        pe.wait_ge(kd_set, 1)
        for k in range(2):
            for t in range(NT):
                ins = pe.transpose(PS[:, 6 + k, t * P:(t + 1) * P], kd[:, t, k * P:(k + 1) * P], ident[:, :])
        ins.then_inc(kd_T, 1)
        pe.wait_ge(vb_ev, 1)
        pe.wait_ge(cq_s, 1)
        unit_N(pe, u1 + 8, 0, 0, 2, cq_hi, cq_lo, True, True)
        pe.wait_ge(kT_ev, 1)
        unit_N(pe, u1 + 9, 4, 0, 2, cq_hi, cq_lo, True, True)
        for have, done, free in ((qa_set, qa_T, None), (qi_set, qi_T, qa_ev)):
            pe.wait_ge(have, 1)
            if free:
                pe.wait_ge(free, 1)
            for k in range(4):
                for t in range(NT):
                    ins = pe.transpose(PS[:, k, t * P:(t + 1) * P], rot[:, t * 512 + k * P:t * 512 + (k + 1) * P], ident[:, :])
            ins.then_inc(done, 1)
        pe.wait_ge(qi_ev, 1)

    def index_pe(pe):
        n = 0
        for i in range(1, NT):
            for h in range(8):
                r = PER * (h % 2)
                if n >= 4:
                    pe.wait_ge(a_relu, n - 3)
                nc.tensor.matmul(PS[:, n % 4, 0:(i + 1) * P], qiT[r:r + PER, h // 2, i * P:(i + 1) * P],
                                 kiT[r:r + PER, 0:(i + 1) * P], start=True, stop=True).then_inc(a_dot, 1)
                n += 1
        pe.wait_ge(a_relu, n)

    def index_act(act):
        n = 0
        for i in range(1, NT):
            for h in range(8):
                act.wait_ge(a_dot, n + 1)
                if n >= 2:
                    act.wait_ge(a_rused, n - 1)
                act.activation(lgi[:, n % 2, 0:(i + 1) * P], PS[:, n % 4, 0:(i + 1) * P], ACT.Relu).then_inc(a_relu, 1)
                n += 1

    def index_dve(dve):
        n = 0
        for i in range(1, NT):
            s = score[:, soff[i]:soff[i + 1]]
            for h in range(8):
                dve.wait_ge(a_relu, n + 1)
                w = widx[:, i, h:h + 1]
                if h == 0:
                    ins = dve.tensor_scalar(s, lgi[:, n % 2, 0:(i + 1) * P], w, None, ALU.mult)
                else:
                    dve.wait_ge(a_rused, n)
                    ins = dve.scalar_tensor_tensor(s, lgi[:, n % 2, 0:(i + 1) * P], w, s, ALU.mult, ALU.add)
                ins.then_inc(a_rused, 1)
                n += 1

    def topk_round(dve, n):
        i = 1 + n // (TOPK // 8)
        s = score[:, soff[i]:soff[i + 1]]
        if n % (TOPK // 8) == 0:
            dve.wait_ge(a_causal, i)
        dve_link(dve.max(rstat[:, 40:48], s))
        dve_link(dve.match_replace(s, rstat[:, 40:48], s, TAKEN))
        if (n + 1) % (TOPK // 8) == 0:
            dve_link(dve.tensor_scalar(drop[:, soff[i]:soff[i + 1]], s, -1e38, NEG, ALU.is_ge, ALU.mult))

    def scores_of(h):
        b = 3 * (h % 2)
        return PS[:, b:b + 3, :].rearrange("p a c -> p (a c)")[:, 0:SPAN]

    def stick_pe(pe):
        for h in range(-1, 8):
            if h + 1 < 8:
                g, z = h + 1, scores_of(h + 1)
                r = PER * (g % 2)
                if g >= 2:
                    pe.wait_ge(b_exp, g - 1)
                for j in range(NT):
                    ins = nc.tensor.matmul(z[:, off[j]:off[j] + wid[j]], kbT[r:r + PER, g // 2, j * P:(j + 1) * P],
                                           qbT[r:r + PER, g // 2, j * P:T], start=j < NT - 1, stop=False,
                                           skip_group_check=True)
                ins.then_inc(b_z, 1)
            if h >= 0:
                z = scores_of(h)
                pe.wait_ge(b_spm, h + 1)
                for j in range(NT):
                    for i in range(j, NT):
                        c = off[j] + (i - j) * P
                        ins = nc.tensor.matmul(z[:, c:c + wid[i]], negtri[:, :] if i == j else negone[:, :],
                                               stick[:, h % 3, off[i]:off[i] + wid[i]], start=False, stop=i == NT - 1,
                                               skip_group_check=True)
                ins.then_inc(b_acc, 1)
            if h >= 1:
                stick_out(pe, h - 1)
        stick_out(pe, 7)

    def stick_out(pe, h):
        r = PER * (h % 2)
        pe.wait_ge(b_am, h + 1)
        if h >= 2:
            pe.wait_ge(b_lo, h - 1)
        for j in range(NT):
            ins = nc.tensor.matmul(PS[r:r + PER, 6 + h % 2, j * P:T], vb[:, j, h * PER:(h + 1) * PER],
                                   stick[:, h % 3, off[j]:off[j] + wid[j]], start=j == 0, stop=j == NT - 1,
                                   skip_group_check=True)
        ins.then_inc(b_pv, 1)

    def stick_act(act):
        rounds(act, U["merge1"], 2)
        for h in range(-1, 8):
            if h + 1 < 8:
                g = h + 1
                e = stick[:, g % 3, :]
                act.wait_ge(b_z, g + 1)
                if g >= 3:
                    act.wait_ge(b_pv, g - 2)
                act_link(act.activation(e, scores_of(g), ACT.Abs))
                act_link(act.activation(e, e, ACT.Exp, scale=-1.0))
                act.activation(e, e, ACT.Ln, bias=one_c[:, :]).then_inc(b_ln, 1)
            if h >= 0:
                act.wait_ge(b_acc, h + 1)
                act.activation(stick[:, h % 3, :], scores_of(h), ACT.Exp).then_inc(b_exp, 1)
            if h >= 1:
                stick_hi(act, h - 1)
        stick_hi(act, 7)

    def stick_hi(act, h):
        r = PER * (h % 2)
        act.wait_ge(b_pv, h + 1)
        act.activation(yb_hi[r:r + PER, h // 2, :], PS[r:r + PER, 6 + h % 2, :], ACT.Copy).then_inc(b_hi, 1)

    def stick_dve(dve):
        share = 3 * (TOPK // 8) // 16
        for h in range(8 + 1):
            if h < 8:
                e = stick[:, h % 3, :]
                dve.wait_ge(b_ln, h + 1)
                dve.scalar_tensor_tensor(e, scores_of(h), 0.0, e, ALU.max, ALU.add).then_inc(b_sp, 1)
                for n in range(share):
                    topk_round(dve, 2 * h * share + n)
            if h:
                r = PER * ((h - 1) % 2)
                dve.wait_ge(b_hi, h)
                dve.tensor_tensor(yb_lo[r:r + PER, (h - 1) // 2, :], PS[r:r + PER, 6 + (h - 1) % 2, :],
                                  yb_hi[r:r + PER, (h - 1) // 2, :].bitcast(F32), ALU.subtract).then_inc(b_lo, 1)
            if h < 8:
                for n in range(share):
                    topk_round(dve, (2 * h + 1) * share + n)

    def sparse_pe(pe):
        pe.wait_ge(b_lo, 8)
        for i in range(NT):
            S = (i + 1) * P
            for h in range(8):
                r, g = PER * (h % 2), 8 * i + h
                if g >= 2:
                    pe.wait_ge(a_lg, g - 1)
                nc.tensor.matmul(PS[:, h % 2, 0:S], qaT[r:r + PER, h // 2, i * P:(i + 1) * P],
                                 kaT[r:r + PER, 0:S], start=True, stop=True).then_inc(a_lgm, 1)
                if h >= 1:
                    probs_pe(pe, i, h - 1)
            probs_pe(pe, i, 7)

    def probs_pe(pe, i, h):
        g = 8 * i + h
        quad = g // 4
        pe.wait_ge(a_pr, g + 1)
        if h % 4 == 0 and quad >= 1:
            pe.wait_ge(a_pTev, quad)
        for j in range(i + 1):
            ins = pe.transpose(PS[:, 2 + j, (h % 4) * P:(h % 4 + 1) * P], pr[:, h % 2, j * P:(j + 1) * P], ident[:, :])
        ins.then_inc(a_pT, 1)
        if h % 4 == 3:
            pe.wait_ge(a_pTev, quad + 1)
            if quad >= 1:
                pe.wait_ge(a_olev, quad)
            for j in range(i + 1):
                ins = nc.tensor.matmul(PS[:, 6, :], pn[:, j, 320:448], pT[:, j, :], start=j == 0, stop=j == i)
            ins.then_inc(a_ol, 1)
            pe.wait_ge(a_olev, quad + 1)
            if quad >= 1:
                pe.wait_ge(a_ylo, quad)
            for hh in range(4):
                r = PER * (hh % 2)
                ins = nc.tensor.matmul(PS[r:r + PER, 7, (hh // 2) * P:(hh // 2 + 1) * P], wuv[:, h - 3 + hh, :],
                                       olT[:, hh * P:(hh + 1) * P], start=True, stop=True)
            ins.then_inc(a_o, 1)

    def sparse_act(act):
        for i in range(NT):
            S = (i + 1) * P
            for h in range(8):
                g = 8 * i + h
                act.wait_ge(a_lg, g + 1)
                if g >= 2:
                    act.wait_ge(a_pT, g - 1)
                act.activation(pr[:, h % 2, 0:S], lg[:, h % 2, 0:S], ACT.Exp, bias=rstat[:, 32 + h % 2:33 + h % 2],
                               accum_out=rstat[:, 34 + h % 2:35 + h % 2]).then_inc(a_exp, 1)
                if h >= 1:
                    probs_act(act, i, h - 1)
            probs_act(act, i, 7)

    def probs_act(act, i, h):
        quad = (8 * i + h) // 4
        if h % 4 == 3:
            act.wait_ge(a_pT, 8 * i + h + 1)
            if quad >= 1:
                act.wait_ge(a_ol, quad)
            act.activation(pT[:, 0:i + 1, :], PS[:, 2:3 + i, :], ACT.Copy).then_inc(a_pTev, 1)
            act.wait_ge(a_o, quad + 1)
            pair = 2 * (h // 4)
            act.activation(ya_hi[:, pair:pair + 2, i * P:(i + 1) * P], PS[:, 7, 0:256].rearrange("p (a b) -> p a b", a=2),
                           ACT.Copy).then_inc(a_yhi, 1)

    def sparse_dve(dve):
        for i in range(NT):
            S = (i + 1) * P
            chosen = drop[:, soff[i]:soff[i + 1]] if i else lower[:, :]
            for h in range(8):
                g = 8 * i + h
                dve.wait_ge(a_lgm, g + 1)
                if g >= 2:
                    dve.wait_ge(a_exp, g - 1)
                dve_link(dve.tensor_tensor_reduce(out=lg[:, h % 2, 0:S], in0=PS[:, h % 2, 0:S], in1=chosen, scale=1.0,
                                                  scalar=TAKEN, op0=ALU.add, op1=ALU.max, accum_out=rstat[:, 36 + h % 2:37 + h % 2]))
                dve.tensor_scalar(rstat[:, 32 + h % 2:33 + h % 2], rstat[:, 36 + h % 2:37 + h % 2], -1.0, None,
                                  ALU.mult).then_inc(a_lg, 1)
                if h >= 1:
                    probs_dve(dve, i, h - 1)
            probs_dve(dve, i, 7)

    def probs_dve(dve, i, h):
        g = 8 * i + h
        S = (i + 1) * P
        dve.wait_ge(a_exp, g + 1)
        if g:
            dve.wait_ge(a_pr, g)
        dve_link(dve.reciprocal(rstat[:, 38:39], rstat[:, 34 + h % 2:35 + h % 2]))
        dve.tensor_scalar(pr[:, h % 2, 0:S], pr[:, h % 2, 0:S], rstat[:, 38:39], None, ALU.mult).then_inc(a_pr, 1)
        if h % 4 == 3:
            quad = g // 4
            dve.wait_ge(a_ol, quad + 1)
            dve.tensor_copy(olT[:, :], PS[:, 6, :]).then_inc(a_olev, 1)
            dve.wait_ge(a_yhi, quad + 1)
            pair = 2 * (h // 4)
            dst = ya_lo[:, pair:pair + 2, i * P:(i + 1) * P]
            dve.tensor_tensor(dst, PS[:, 7, 0:256].rearrange("p (a b) -> p a b", a=2),
                              ya_hi[:, pair:pair + 2, i * P:(i + 1) * P].bitcast(F32), ALU.subtract).then_inc(a_ylo, 1)

    kd = work[:, 2048:3072].rearrange("p (t c) -> p t c", t=NT)

    def mid1_act(act):
        act.wait_ge(x_ready, KD * 2)
        act.dma_start(wuv[:, :, :], A['w_uv_a'][0].rearrange("h c d -> c h d")).then_inc(m1_dma, 16)
        act.dma_start(gq[:, :], A['g_q_a'][0].partition_broadcast(P)).then_inc(m1_dma, 16)
        act.dma_start(gk[:, :], A['g_k_a'][0].partition_broadcast(P)).then_inc(m1_dma, 16)
        rounds(act, u1 + 2, 2)
        act.wait_ge(w_used, u1 + 2)
        act.activation(pn[:, :, :], PS[:, 0:4, :], ACT.Copy).then_inc(pn_ev, 1)
        rounds(act, u1 + 4, 2)
        act.wait_ge(w_used, u1 + 4)
        act.activation(qbT[:, :, :], PS[:, 0:4, :], ACT.Copy, scale=PER ** -0.5).then_inc(qb_ev, 1)
        act.wait_ge(m1_sd, 1)
        act.activation(stat[:, 0:8], stat[:, 0:8], ACT.Sqrt).then_inc(m1_sd, 1)
        rounds(act, u1 + 6, 2)
        rounds(act, u1 + 8, 2, 1024)
        act.wait_ge(w_used, u1 + 8)
        act.activation(vb[:, :, :], PS[:, 0:4, :], ACT.Copy).then_inc(vb_ev, 1)
        act.wait_ge(cq_T, 1)
        for k in range(2):
            ins = act.activation(cq_hi[:, k, :], PS[:, 4 + k, :], ACT.Copy, scale=gain(G_CQ, k))
        ins.then_inc(cq_hi_s, 1)
        act.wait_ge(kd_T, 1)
        act.activation(kaT[:, :], PS[:, 6, :], ACT.Copy)
        act.activation(kiT[:, :], PS[:, 7, :], ACT.Copy).then_inc(kT_ev, 1)
        act.wait_ge(w_used, u1 + 9)
        act.activation(work[:, 0:2048].rearrange("p (t c) -> p t c", t=NT), PS[:, 0:4, :], ACT.Square).then_inc(qa_sq, 1)
        act.wait_ge(m1_sd, 3)
        act.activation(stat[:, 8:40], stat[:, 8:40], ACT.Sqrt).then_inc(m1_sd, 1)
        act.wait_ge(qa_T, 1)
        act.activation(qaT[:, :, :], PS[:, 0:4, :], ACT.Copy, scale=PER ** -0.5).then_inc(qa_ev, 1)
        act.wait_ge(qi_T, 1)
        act.activation(qiT[:, :, :], PS[:, 0:4, :], ACT.Copy).then_inc(qi_ev, 1)

    def mid1_dve(dve):
        dve.wait_ge(wi_mm, 1)
        dve.tensor_scalar(widx[:, :, :], PS[:, 4:8, 0:8], 8 ** -0.5 * 64 ** -0.5, None, ALU.mult).then_inc(wi_ev, 1)
        dve.wait_ge(pn_ev, 1)
        sqs = work[:, 0:1280].rearrange("p (t c) -> p t c", t=NT)
        dve_link(dve.tensor_tensor(sqs, pn[:, :, 0:320], pn[:, :, 0:320], ALU.mult))
        dve.tensor_reduce(stat[:, 0:4], sqs[:, :, 0:256], AX.X, ALU.add)
        dve_link(dve.tensor_reduce(stat[:, 4:8], sqs[:, :, 256:320], AX.X, ALU.add))
        dve.tensor_scalar(stat[:, 0:4], stat[:, 0:4], 1 / 256, EPS, ALU.mult, ALU.add)
        dve.tensor_scalar(stat[:, 4:8], stat[:, 4:8], 1 / 64, EPS, ALU.mult, ALU.add).then_inc(m1_sd, 1)
        dve.wait_ge(m1_sd, 2)
        dve_link(dve.reciprocal(stat[:, 0:8], stat[:, 0:8]))
        dve.tensor_tensor(pn[:, :, 0:256], pn[:, :, 0:256], stat[:, 0:4].unsqueeze(2).to_broadcast([P, NT, 256]),
                          ALU.mult).then_inc(cqn_set, 1)
        dve_link(dve.tensor_tensor(pn[:, :, 256:320], pn[:, :, 256:320],
                                   stat[:, 4:8].unsqueeze(2).to_broadcast([P, NT, 64]), ALU.mult))
        dve.wait_ge(m1_dma, 48)
        dve_link(dve.tensor_tensor(pn[:, :, 256:320], pn[:, :, 256:320], gk[:, :].unsqueeze(1).to_broadcast([P, NT, 64]), ALU.mult))
        for j, c0 in enumerate((256, 448)):
            src = pn[:, :, c0:c0 + 64].unsqueeze(2)
            dst = kd[:, :, j * P:j * P + 64].unsqueeze(2)
            dve_link(rotate(dve_link, src, dst, 0, 1))
            ins = dve.tensor_copy(kd[:, :, j * P + 64:(j + 1) * P], kd[:, :, j * P:j * P + 64])
        ins.then_inc(kd_set, 1)
        dve.wait_ge(w_used, u1 + 6)
        dve.tensor_copy(kbT[:, :, :], PS[:, 4:8, :]).then_inc(kb_ev, 1)
        dve.wait_ge(cq_hi_s, 1)
        for k in range(2):
            ins = dve.scalar_tensor_tensor(cq_lo[:, k, :], PS[:, 4 + k, :], gain(G_CQ, k), cq_hi[:, k, :].bitcast(F32),
                                           ALU.mult, ALU.subtract)
        ins.then_inc(cq_s, 1)
        dve.wait_ge(qa_sq, 1)
        dve_link(dve.tensor_reduce(stat[:, 8:40], work[:, 0:2048].rearrange("p (a b) -> p a b", b=64), AX.X, ALU.add))
        dve.tensor_scalar(stat[:, 8:40], stat[:, 8:40], 1 / 64, EPS, ALU.mult, ALU.add).then_inc(m1_sd, 1)
        dve.wait_ge(m1_sd, 4)
        dve_link(dve.reciprocal(stat[:, 8:40], stat[:, 8:40]))
        q4 = qn[:, :, :].rearrange("p t (h d) -> p t h d", d=64)
        rs = stat[:, 8:40].rearrange("p (t h) -> p t h", t=NT).unsqueeze(3).to_broadcast([P, NT, 8, 64])
        dve_link(dve.tensor_tensor(q4, PS[:, 0:4, :].rearrange("p t (h d) -> p t h d", d=64), rs, ALU.mult))
        qf = qn[:, :, :].rearrange("p t (h d) -> p (t h) d", d=64)
        dve_link(dve.tensor_tensor(qf, qf, gq[:, :].unsqueeze(1).to_broadcast([P, 32, 64]), ALU.mult))
        dve.wait_ge(kd_T, 1)
        rv = rot.rearrange("p (t h d) -> p t h d", t=NT, d=64)
        rotate(dve_link, q4, rv, 0, 8).then_inc(qa_set, 1)
        dve.wait_ge(w_used, u1 + 10)
        dve.wait_ge(qa_T, 1)
        rotate(dve_link, PS[:, 4:8, :].rearrange("p t (h d) -> p t h d", d=64), rv, 0, 8).then_inc(qi_set, 1)

    um = U["merge1"]

    def merge1_sp(sp):
        w = A['w_in'][0]
        for n in range(2):
            u = um + 6 * n
            for c0, wo, d in ((2056, A['w_o_a'][0], 0), (3080, A['w_o_b'][0], 3)):
                panel(sp, u + d, w, 0, 4, c0 + 512 * n)
                panel(sp, u + d + 1, w, 4, 4, c0 + 512 * n)
                panel(sp, u + d + 2, wo, 0, 4, 512 * n)

    def merge1_pe(pe):
        for n in range(2):
            u = um + 6 * n
            for b, (yh, yl) in enumerate(((ya_hi, ya_lo), (yb_hi, yb_lo))):
                g = 2 * n + b
                v = u + 3 * b
                if g:
                    pe.wait_ge(g_sig, g)
                unit_T(pe, v, v % 2, 0, 0, 4, h_hi, h_lo, True, False)
                unit_T(pe, v + 1, (v + 1) % 2, 0, 4, 4, h_hi, h_lo, False, True)
                if g:
                    pe.wait_ge(g_mul, g)
                else:
                    pe.wait_ge(a_ylo, 8)
                unit_T(pe, v + 2, (v + 2) % 2, 4, 0, 4, yh, yl, True, True)

    def merge1_act(act):
        for n in range(2):
            for b in range(2):
                g = 2 * n + b
                v = um + 6 * n + 3 * b
                rounds(act, v, 3) if g else rounds(act, v + 2, 1)
                act.wait_ge(w_used, v + 2)
                if g >= 2:
                    act.wait_ge(g_mul, g - 1)
                act.activation((gt, gt2)[b][:, :].rearrange("p (a c) -> p a c", a=4), PS[:, 0:4, :], ACT.Sigmoid).then_inc(g_sig, 1)
            act.wait_ge(g_mul, 2 * n + 2)
            act.wait_ge(mg_ready, 2 * n + 1)
            act.activation(mg_hi[:, 4 * n:4 * n + 4, :], mtmp.rearrange("p (a c) -> p a c", a=4), ACT.Copy).then_inc(g_hi, 1)

    def merge1_dve(dve):
        for n in range(2):
            for b in range(2):
                g = 2 * n + b
                v = um + 6 * n + 3 * b
                dve.wait_ge(g_sig, g + 1)
                dve.wait_ge(w_used, v + 3)
                if g == 2:
                    dve.wait_ge(mg_ready, 2)
                dst = (mtmp, gt2[:, :])[b].rearrange("p (a c) -> p a c", a=4)
                dve.tensor_tensor(dst, (gt, gt2)[b][:, :].rearrange("p (a c) -> p a c", a=4), PS[:, 4:8, :],
                                  ALU.mult).then_inc(g_mul, 1)
            dve.wait_ge(g_mul, 2 * n + 2)
            dve.tensor_tensor(mtmp, mtmp, gt2[:, :], ALU.add).then_inc(mg_ready, 1)
            dve.wait_ge(g_hi, n + 1)
            dve.tensor_tensor(mg_lo[:, 4 * n:4 * n + 4, :], mtmp.rearrange("p (a c) -> p a c", a=4),
                              mg_hi[:, 4 * n:4 * n + 4, :].bitcast(F32), ALU.subtract).then_inc(mg_ready, 1)

    def place(offset, name, shape, dt=F32):
        return at(name, shape, dt, offset=SCOPE + offset)

    KB = 1024
    rqT, rkT = place(0, "rqT", [P, 4, T]), place(8 * KB, "rkT", [P, 4, T])
    rv, rgT = place(16 * KB, "rv", [P, NT, D]), place(32 * KB, "rgT", [P, KD, T])
    yr_hi, yr_lo = place(48 * KB, "yr_hi", [P, KD, T], F32R), place(64 * KB, "yr_lo", [P, KD, T], F32R)
    wb_raw = place(64 * KB, "wb_raw", [P, KD, 16])
    wb_h, wb_l = place(64 * KB + 512, "wb_h", [P, KD, 16], F32R), place(65 * KB, "wb_l", [P, KD, 16], F32R)
    diff = place(80 * KB, "diff", [P, T])
    diffi = place(78 * KB, "diffi", [P, T], I32)
    level = {2 ** n: place(80 * KB + 512 * n, f"level{2 ** n}", [P, P]) for n in range(7)}
    level1T = place(80 * KB + 3584, "level1T", [P, P])
    upto = place(84 * KB, "upto", [P, P])
    before = place(84 * KB + 512, "before", [P, P])
    seen = place(85 * KB, "seen", [P, P])
    small = place(85 * KB + 512, "small", [P, 256 + 24])
    beta, gl, Gn, bG, kdf, dlast = (small[:, 32 * j:32 * j + 32].rearrange("p (c h) -> p c h", c=NT) for j in range(6))
    alog, dtb = small[:, 224:232], small[:, 232:240]
    ba = place(85 * KB + 512 + 280 * 4, "ba", [P, NT, 16])
    dec = work[:, 0:1024].rearrange("p (a b) -> p a b", a=2)
    sT = work[:, 1024:3584].rearrange("p (a b) -> p a b", a=2)
    ro = work[:, 3584:4096].rearrange("p (c v) -> p c v", c=NT)
    u2 = U["ret"]
    (r2_consts, r2_dma, rq_set, rq_T, rq_ev, rk_set, rk_T, rk_ev, rv_ev, wb_hi_s, wb_lo_s, ba_mm, ba_ev, rg_ev, r_sc, r_dec,
     r_sT, r_out, r_var, r_sd, r_on, r_T, r_y, r_hi, r_lo, p_sig, p_sp, p_exp, p_ln, p_g, p_G, p_Gn, p_eG, p_done, diff_set,
     lv_set) = (
        sem("r_" + s) for s in ("consts dma rq_set rq_T rq_ev rk_set rk_T rk_ev rv_ev wbh wbl ba_mm ba_ev rg_ev sc dec sT out var "
                                "sd on T y hi lo sig sp exp ln g G Gn eG done diff level").split())
    loggam = [float(np.log(np.float32(1) - np.float32(2.0) ** np.float32(-5 - h))) for h in range(8)]

    def ret_sp(sp):
        w = A['w_in_2'][0]
        for j, c0 in enumerate((0, 512, 1024, 1536, 2048, 2560)):
            panel(sp, u2 + 2 * j, w, 0, 4, c0)
            panel(sp, u2 + 2 * j + 1, w, 4, 4, c0)

    def block_mask(pool, m, b):
        q = P // (2 * b)
        v = m[:, :].rearrange("p (q r) -> p q r", q=q)[:, :, 0:b]
        pool_link(pool.memset(m[:, :], 0.0))
        pool_link(pool.memset(v, 1.0))
        pool_link(pool.affine_select(out=v, in_=v, compare_op=ALU.is_ge, fill=0.0, base=-b,
                                     pattern=[[-2 * b, q], [0, b]], channel_multiplier=1))
        return pool.affine_select(out=v, in_=v, compare_op=ALU.is_ge, fill=0.0, base=2 * b - 1,
                                  pattern=[[2 * b, q], [0, b]], channel_multiplier=-1)

    def ret_pool(pool):
        pool.wait_ge(x_ready, KD * 4)
        for m, op, pat, cm in ((upto, ALU.is_ge, 1, -1), (before, ALU.is_gt, -1, 1), (seen, ALU.is_ge, -1, 1)):
            pool_link(pool.memset(m[:, :], 1.0))
            pool_link(pool.affine_select(out=m[:, :], in_=m[:, :], compare_op=op, fill=0.0, base=0,
                                         pattern=[[pat, P]], channel_multiplier=cm))
        pool_link(pool.iota(diffi[:, :], pattern=[[1, T]], base=0, channel_multiplier=-1))
        pool_link(pool.tensor_copy(diff[:, :], diffi[:, :]))
        pool.affine_select(out=diff[:, 0:P], in_=diff[:, 0:P], compare_op=ALU.is_ge, fill=1e7, base=0,
                           pattern=[[1, P]], channel_multiplier=-1).then_inc(diff_set, 1)
        los(pool, u2 + 2, 2)
        pool.wait_ge(wb_hi_s, 1)
        pool.tensor_tensor(wb_l[:, :, :], wb_raw[:, :, :], wb_h[:, :, :].bitcast(F32), ALU.subtract).then_inc(wb_lo_s, 1)
        los(pool, u2 + 4, 8)
        los(pool, U["merge2a"], 2)
        pool.wait_ge(r_dec, 8)
        for b in (2, 4, 8, 16, 32, 64):
            pool_link(block_mask(pool, level[b], b))
        for m, base in ((level[1], -1), (level1T, 0)):
            pool_link(pool.memset(m[:, :], 0.0))
            v = m[:, :].rearrange("p (q r) -> p q r", r=2)[:, :, (0 if base else 1):(1 if base else 2)]
            ins = pool.affine_select(out=v, in_=v, compare_op=ALU.not_equal, fill=1.0, base=base,
                                     pattern=[[-2, P // 2], [0, 1]], channel_multiplier=1)
            pool_link(ins)
        pool.memset(small[:, 240:241], 0.0).then_inc(lv_set, 1)
        los(pool, U["merge2a"] + 2, 6)

    def ret_pe(pe):
        unit_N(pe, u2, 0, 0, 4, h_hi, h_lo, True, False, (h_ready, KD * 3))
        unit_N(pe, u2 + 1, 0, 4, 4, h_hi, h_lo, False, True, (h_ready, KD * 3))
        unit_N(pe, u2 + 2, 4, 0, 4, h_hi, h_lo, True, False)
        unit_N(pe, u2 + 3, 4, 4, 4, h_hi, h_lo, False, True)

        def turn_over(have, bank, done):
            pe.wait_ge(have, 1)
            for k in range(4):
                for t in range(NT):
                    ins = pe.transpose(PS[:, bank + k, t * P:(t + 1) * P], rot[:, t * 512 + k * P:t * 512 + (k + 1) * P], ident[:, :])
            ins.then_inc(done, 1)

        turn_over(rq_set, 0, rq_T)
        pe.wait_ge(rq_ev, 1)
        unit_N(pe, u2 + 4, 0, 0, 4, h_hi, h_lo, True, False)
        unit_N(pe, u2 + 5, 0, 4, 4, h_hi, h_lo, False, True)
        turn_over(rk_set, 4, rk_T)
        pe.wait_ge(rk_ev, 1)
        unit_N(pe, u2 + 6, 4, 0, 4, h_hi, h_lo, True, False)
        unit_N(pe, u2 + 7, 4, 4, 4, h_hi, h_lo, False, True)
        pe.wait_ge(wb_lo_s, 1)
        pe.wait_ge(rv_ev, 1)
        for t in range(NT):
            for k in range(KD):
                a, b = h_hi[:, k, t * P:(t + 1) * P], h_lo[:, k, t * P:(t + 1) * P]
                nc.tensor.matmul(PS[:, t, 0:16], a, wb_h[:, k, :], start=k == 0, stop=False)
                nc.tensor.matmul(PS[:, t, 0:16], a, wb_l[:, k, :], start=False, stop=False)
                ins = nc.tensor.matmul(PS[:, t, 0:16], b, wb_h[:, k, :], start=False, stop=k == KD - 1)
        ins.then_inc(ba_mm, 1)
        pe.wait_ge(ba_ev, 1)
        unit_T(pe, u2 + 8, 0, 0, 0, 4, h_hi, h_lo, True, False)
        unit_T(pe, u2 + 9, 1, 0, 4, 4, h_hi, h_lo, False, True)
        pe.wait_ge(rv_ev, 2)
        unit_T(pe, u2 + 10, 0, 4, 0, 4, h_hi, h_lo, True, False)
        unit_T(pe, u2 + 11, 1, 4, 4, 4, h_hi, h_lo, False, True)
        pe.wait_ge(rg_ev, 2)
        pe.wait_ge(p_g, 1)
        nc.tensor.matmul(PS[:, 7, 0:32], upto[:, :], small[:, 32:64], start=True, stop=True)
        nc.tensor.matmul(PS[:, 7, 32:64], ones[:, :], small[:, 32:64], start=True, stop=True).then_inc(p_G, 1)
        pe.wait_ge(p_Gn, 1)
        ret_scores(pe, 0)
        for h in range(8):
            if h:
                ret_turn(pe, h - 1)
            pe.wait_ge(r_sT, h + 1)
            for i in range(NT):
                for j in range(i + 1):
                    c = off[j] + (i - j) * P
                    ins = nc.tensor.matmul(PS[:, 6, i * P:(i + 1) * P], sT[:, h % 2, c:c + P],
                                           rv[:, j, h * P:(h + 1) * P], start=j == 0, stop=j == i)
            ins.then_inc(r_out, 1)
            if h < 7:
                ret_scores(pe, h + 1)
        ret_turn(pe, 7)

    def ret_scores(pe, h):
        r, z = PER * (h % 2), scores_of(h)
        for j in range(NT):
            ins = nc.tensor.matmul(z[:, off[j]:off[j] + wid[j]], rkT[r:r + PER, h // 2, j * P:(j + 1) * P],
                                   rqT[r:r + PER, h // 2, j * P:T], start=True, stop=True)
        ins.then_inc(r_sc, 1)

    def ret_turn(pe, h):
        pe.wait_ge(r_on, h + 1)
        if h >= 1:
            pe.wait_ge(r_y, h)
        for i in range(NT):
            ins = pe.transpose(PS[:, 7, i * P:(i + 1) * P], ro[:, i, :], ident[:, :])
        ins.then_inc(r_T, 1)

    def ret_act(act):
        act.wait_ge(x_ready, KD * 4)
        act.dma_start(wb_raw[:, :, :], A['w_in_2'][0, :, 7168:7184].rearrange("(k p) c -> p k c", p=P)).then_inc(r2_dma, 16)
        act.dma_start(alog, A['dn_a_log_2'][0].partition_broadcast(P)).then_inc(r2_dma, 16)
        act.dma_start(dtb, A['dn_dt_bias_2'][0].partition_broadcast(P)).then_inc(r2_dma, 16)
        rounds(act, u2 + 2, 2)
        act.wait_ge(r2_dma, 48)
        act.activation(wb_h[:, :, :], wb_raw[:, :, :], ACT.Copy).then_inc(wb_hi_s, 1)
        rounds(act, u2 + 4, 2)
        act.wait_ge(rq_T, 1)
        act.activation(rqT[:, :, :], PS[:, 0:4, :], ACT.Copy).then_inc(rq_ev, 1)
        rounds(act, u2 + 6, 2)
        act.wait_ge(rk_T, 1)
        act.activation(rkT[:, :, :], PS[:, 4:8, :], ACT.Copy, scale=PER ** -0.5).then_inc(rk_ev, 1)
        rounds(act, u2 + 8, 1)
        act.wait_ge(w_used, u2 + 6)
        act.activation(rv[:, :, 0:512], PS[:, 0:4, :], ACT.Copy).then_inc(rv_ev, 1)
        rounds(act, u2 + 9, 1)
        act.wait_ge(w_used, u2 + 8)
        act.activation(rv[:, :, 512:1024], PS[:, 4:8, :], ACT.Copy).then_inc(rv_ev, 1)
        rounds(act, u2 + 10, 2)
        act.wait_ge(ba_ev, 1)
        act.activation(beta, ba[:, :, 0:8], ACT.Sigmoid).then_inc(p_sig, 1)
        act.wait_ge(p_sp, 1)
        act_link(act.activation(kdf, Gn, ACT.Abs))
        act_link(act.activation(kdf, kdf, ACT.Exp, scale=-1.0))
        act.activation(kdf, kdf, ACT.Ln, bias=one_c[:, :])
        act.activation(alog, alog, ACT.Exp).then_inc(p_ln, 1)
        act.wait_ge(w_used, u2 + 10)
        act.activation(rgT[:, 0:4, :], PS[:, 0:4, :], ACT.Silu).then_inc(rg_ev, 1)
        act.wait_ge(w_used, u2 + 12)
        act.activation(rgT[:, 4:8, :], PS[:, 4:8, :], ACT.Silu).then_inc(rg_ev, 1)
        act.wait_ge(p_Gn, 1)
        act.activation(bG, Gn, ACT.Exp)
        act.activation(dlast, dlast, ACT.Exp)
        act.activation(kdf, kdf, ACT.Exp).then_inc(p_eG, 1)
        rounds(act, U["merge2a"], 2)
        act.wait_ge(diff_set, 1)
        act.activation(dec[:, 0, :], diff[:, :], ACT.Exp, scale=loggam[0]).then_inc(r_dec, 1)
        for h in range(8):
            if h:
                ret_hi(act, h - 1)
            act.wait_ge(r_var, h + 1)
            act.activation(stat[:, 32:36], stat[:, 32:36], ACT.Sqrt).then_inc(r_sd, 1)
            if h < 7:
                act.activation(dec[:, (h + 1) % 2, :], diff[:, :], ACT.Exp, scale=loggam[h + 1]).then_inc(r_dec, 1)
        ret_hi(act, 7)

    def ret_hi(act, h):
        act.wait_ge(r_y, h + 1)
        act.activation(yr_hi[:, h, :], ro[:, :, :].rearrange("p c v -> p (c v)"), ACT.Copy).then_inc(r_hi, 1)

    def ret_dve(dve):
        rv4 = rot.rearrange("p (t h d) -> p t h d", t=NT, d=64)
        dve.wait_ge(w_used, u2 + 2)
        rotate(dve_link, PS[:, 0:4, :].rearrange("p t (h d) -> p t h d", d=64), rv4, NT, 8).then_inc(rq_set, 1)
        dve.wait_ge(w_used, u2 + 4)
        dve.wait_ge(rq_T, 1)
        rotate(dve_link, PS[:, 4:8, :].rearrange("p t (h d) -> p t h d", d=64), rv4, NT, 8).then_inc(rk_set, 1)
        dve.wait_ge(ba_mm, 1)
        dve.tensor_copy(ba[:, :, :], PS[:, 0:4, 0:16]).then_inc(ba_ev, 1)
        dve.wait_ge(r2_dma, 48)
        dve.wait_ge(ba_ev, 1)
        dve.tensor_tensor(Gn, ba[:, :, 8:16], dtb.unsqueeze(1).to_broadcast([P, NT, 8]), ALU.add).then_inc(p_sp, 1)
        dve.wait_ge(p_ln, 1)
        dve_link(dve.scalar_tensor_tensor(gl, Gn, 0.0, kdf, ALU.max, ALU.add))
        dve.scalar_tensor_tensor(gl, gl, -1.0, alog.unsqueeze(1).to_broadcast([P, NT, 8]), ALU.mult, ALU.mult).then_inc(p_g, 1)
        dve.wait_ge(p_G, 1)
        dve_link(dve.tensor_copy(small[:, 64:96], PS[:, 7, 0:32]))
        dve.tensor_copy(small[:, 160:192], PS[:, 7, 32:64])
        dve_link(dve.tensor_tensor(small[:, 128:160], PS[:, 7, 32:64], small[:, 64:96], ALU.subtract))
        dve.tensor_scalar(small[:, 128:160], small[:, 128:160], 0.0, None, ALU.min).then_inc(p_Gn, 1)
        dve.wait_ge(p_eG, 1)
        dve.wait_ge(p_sig, 1)
        dve.tensor_tensor(bG, bG, beta, ALU.mult).then_inc(p_done, 1)
        st6 = rstat[:, 0:24].rearrange("p (c s) -> p c s", c=NT)
        mv = rstat[:, 24:32].rearrange("p (c s) -> p c s", c=NT)
        for h in range(8):
            dve.wait_ge(r_sc, h + 1)
            dve.wait_ge(r_dec, h + 1)
            if h >= 2:
                dve.wait_ge(r_out, h - 1)
            z = scores_of(h)
            for j in range(NT):
                c = slice(off[j], off[j] + wid[j])
                ins = dve.tensor_tensor(sT[:, h % 2, c], z[:, c], dec[:, h % 2, 0:wid[j]], ALU.mult)
            ins.then_inc(r_sT, 1)
            if h:
                ret_gate(dve, h - 1)
            dve.wait_ge(r_out, h + 1)
            for c in range(NT):
                ins = dve.bn_stats(st6[:, c, :], PS[:, 6, c * P:(c + 1) * P])
            dve_link(ins)
            for c in range(NT):
                ins = dve.bn_aggr(mv[:, c, :], st6[:, c, :])
            dve_link(ins)
            dve.tensor_scalar(stat[:, 32:36], mv[:, :, 1:2].rearrange("p c s -> p (c s)"), GN_EPS, None, ALU.add).then_inc(r_var, 1)
            dve.wait_ge(r_sd, h + 1)
            dve_link(dve.reciprocal(stat[:, 32:36], stat[:, 32:36]))
            if h:
                dve.wait_ge(r_lo, h)
            for c in range(NT):
                ins = dve.tensor_scalar(ro[:, c, :], PS[:, 6, c * P:(c + 1) * P], mv[:, c, 0:1], stat[:, 32 + c:33 + c],
                                        ALU.subtract, ALU.mult)
            ins.then_inc(r_on, 1)
        ret_gate(dve, 7)

    def ret_gate(dve, h):
        dve.wait_ge(r_T, h + 1)
        rf = ro[:, :, :].rearrange("p c v -> p (c v)")
        dve.scalar_tensor_tensor(rf, PS[:, 7, :], gain(G_RET, h), rgT[:, h, :], ALU.mult, ALU.mult).then_inc(r_y, 1)
        dve.wait_ge(r_hi, h + 1)
        dve.tensor_tensor(yr_lo[:, h, :], rf, yr_hi[:, h, :].bitcast(F32), ALU.subtract).then_inc(r_lo, 1)

    M1 = place(0, "M1", [P, KD, T])
    do_hi, do_lo = place(16 * KB, "do_hi", [P, KD, T], F32R), place(32 * KB, "do_lo", [P, KD, T], F32R)
    mh2, ml2 = place(48 * KB, "mh2", [P, KD, T], F32R), place(64 * KB, "ml2", [P, KD, T], F32R)
    br_sig, br_mul, br_hi, br_ready = (sem("br_" + s) for s in "sig mul hi ready".split())
    gbuf = work[:, 0:2048]
    gbuf4 = gbuf.rearrange("p (a c) -> p a c", a=4)

    def branch_sp(sp, stage, gate0, w):
        u = U[stage]
        for n in range(2):
            panel(sp, u + 4 * n, A['w_in_2'][0], 0, 4, gate0 + 512 * n)
            panel(sp, u + 4 * n + 1, A['w_in_2'][0], 4, 4, gate0 + 512 * n)
            panel(sp, u + 4 * n + 2, w, 0, 4, 512 * n)
            panel(sp, u + 4 * n + 3, w, 4, 4, 512 * n)

    def branch_pe(pe, stage, b, yh, yl, ready):
        u = U[stage]
        for n in range(2):
            g = 2 * b + n
            if g % 2:
                pe.wait_ge(br_sig, g)
            if g != 2:
                unit_T(pe, u + 4 * n, 0, 0, 0, 4, h_hi, h_lo, True, False)
                unit_T(pe, u + 4 * n + 1, 1, 0, 4, 4, h_hi, h_lo, False, True)
            if g:
                pe.wait_ge(br_mul, g)
            pe.wait_ge(*ready)
            unit_T(pe, u + 4 * n + 2, 0, 4, 0, 4, yh, yl, True, False)
            unit_T(pe, u + 4 * n + 3, 1, 4, 4, 4, yh, yl, False, True)

    def branch_act(act, stage, b):
        u = U[stage]
        for n in range(2):
            g = 2 * b + n
            if g == 0:
                rounds(act, u + 2, 2)
            act.wait_ge(w_used, u + 4 * n + 2)
            if g == 1:
                act.wait_ge(br_mul, 1)
            if g == 3:
                act.wait_ge(br_ready, 2)
            act.activation(gbuf4, PS[:, 0:4, :], ACT.Sigmoid).then_inc(br_sig, 1)
            if n == 0:
                rounds(act, u + 4, 4)
            if b:
                act.wait_ge(br_ready, 2 * n + 1)
                act.activation(mh2[:, 4 * n:4 * n + 4, :], gbuf4, ACT.Copy).then_inc(br_hi, 1)

    def branch_dve(dve, stage, b):
        u = U[stage]
        for n in range(2):
            g = 2 * b + n
            dve.wait_ge(br_sig, g + 1)
            dve.wait_ge(w_used, u + 4 * n + 4)
            if b == 0:
                dve.tensor_tensor(M1[:, 4 * n:4 * n + 4, :], gbuf4, PS[:, 4:8, :], ALU.mult).then_inc(br_mul, 1)
            else:
                dve.tensor_tensor(gbuf4, gbuf4, PS[:, 4:8, :], ALU.mult).then_inc(br_mul, 1)
                dve.wait_ge(br_mul, g + 1)
                dve.tensor_tensor(gbuf4, gbuf4, M1[:, 4 * n:4 * n + 4, :], ALU.add).then_inc(br_ready, 1)
                dve.wait_ge(br_hi, n + 1)
                dve.tensor_tensor(ml2[:, 4 * n:4 * n + 4, :], gbuf4, mh2[:, 4 * n:4 * n + 4, :].bitcast(F32),
                                  ALU.subtract).then_inc(br_ready, 1)

    dz = place(32 * KB, "dz", [P, KD, T])
    cv = place(48 * KB, "cv", [P, 6, T])
    wkb, wkd, wvb, wAT, waT = (place((60 + 4 * j) * KB, "w_" + n, [P, 2, T]) for j, n in enumerate(("kb", "kd", "vb", "AT", "aT")))
    wE, wX, wT, wU = (work[:, 1024 * j:1024 * (j + 1)].rearrange("p (e t) -> p e t", e=2) for j in range(4))
    cin = work[:, 0:3072].rearrange("p (a b) -> p a b", a=6)
    ssq = rstat[:, 0:16]
    Sst = place(87 * KB, "Sst", [P, 2, P])
    ud = U["dn"]
    POINTS = {
        "pe": "qkT qT2 Grow kk ATt vT u o oT".split(),
        "act": "cinA silA sq2 sd cinB cvq eR silB eE AT uev osq osd ohi".split(),
        "dve": "cvA ss qn cvB kd eD qd A attn T0 vb oss on oy olo".split(),
    }
    passed = {e: sem("dn_" + e) for e in POINTS}
    d_X, d_Xm, d_TU, d_Um, d_wS, d_vn, d_kv, d_S = (sem("dn_" + x) for x in "X Xm TU Um wS vn kv S".split())

    def await_point(eng, who, pp, name):
        eng.wait_ge(passed[who], len(POINTS[who]) * pp + POINTS[who].index(name) + 1)

    def at_point(ins, who):
        ins.then_inc(passed[who], 1)

    def per_head(arr, pp):
        return arr[:, :, 2 * pp:2 * pp + 2].rearrange("p c h -> p h c").unsqueeze(3).to_broadcast([P, 2, NT, P])

    def chunks(x):
        return x.rearrange("p e (c j) -> p e c j", c=NT)

    def everywhere(m):
        return m[:, :].unsqueeze(1).to_broadcast([P, 2 * NT, P])

    def tiles(x):
        return x.rearrange("p e (c j) -> p (e c) j", c=NT)

    def tile_of(x, e, c):
        return x[:, e, c * P:(c + 1) * P]

    LEVELS = (2, 4, 8, 16, 32, 64)

    def delta_sp(sp):
        w = A['w_in_2'][0]
        for pp in range(4):
            for j, cols in enumerate(((3072, 4096), (5120, 6144))):
                for s in range(2):
                    dst = raw[:, s, :].rearrange("p (k c) -> p k c", k=4)
                    pieces = []
                    for a, c0 in enumerate(cols):
                        c = c0 + HALF * pp
                        src = w[s * 512:(s + 1) * 512, c:c + HALF].rearrange("(k p) c -> p k c", p=P)
                        pieces.append((dst[:, :, a * HALF:(a + 1) * HALF], src))
                    load(sp, ud + 4 * pp + 2 * j + s, s, pieces)

    def halves(x, b):
        v = x.rearrange("p (g r) -> p g r", r=2 * b)
        return v[:, :, 0:b], v[:, :, b:2 * b]

    def delta_pe(pe):
        mm = nc.tensor.matmul
        for pp in range(4):
            u = ud + 4 * pp
            if pp:
                await_point(pe, "dve", pp - 1, "oy")
            else:
                pe.wait_ge(br_sig, 2)
                pe.wait_ge(br_mul, 2)
                unit_T(pe, u, 0, 0, 0, 4, h_hi, h_lo, True, False)
                unit_T(pe, u + 1, 1, 0, 4, 4, h_hi, h_lo, False, True)
            unit_T(pe, u + 2, 0, 4, 0, 4, h_hi, h_lo, True, False)
            await_point(pe, "act", pp, "silA")
            for a in range(4):
                for c in range(NT):
                    ins = pe.transpose(tile_of(PS, a, c), tile_of(cv, a, c), ident[:, :])
            at_point(ins, "pe")
            unit_T(pe, u + 3, 1, 4, 4, 4, h_hi, h_lo, False, True)
            await_point(pe, "dve", pp, "qn")
            for a, src in ((0, wE), (2, wkd)):
                for e in range(2):
                    for c in range(NT):
                        ins = pe.transpose(tile_of(PS, a + e, c), tile_of(src, e, c), ident[:, :])
            at_point(ins, "pe")
            await_point(pe, "act", pp, "cinB")
            for e in range(2):
                for c in range(NT):
                    g = small[:, 32 + 8 * c + 2 * pp + e:33 + 8 * c + 2 * pp + e]
                    ins = mm(tile_of(PS, 4 + e, c), g.to_broadcast([P, P]), upto[:, :], start=True, stop=True)
            at_point(ins, "pe")
            await_point(pe, "act", pp, "cvq")
            for e in range(2):
                for c in range(NT):
                    k = tile_of(cv, 2 + e, c)
                    mm(tile_of(PS, 6 + e, c), k, k, start=True, stop=True)
                    ins = mm(tile_of(PS, e, c), tile_of(cv, e, c), k, start=True, stop=True)
            at_point(ins, "pe")
            for who, bank, src in (("A", 2, wU), ("attn", 4, wX)):
                await_point(pe, "dve", pp, who)
                for e in range(2):
                    for c in range(NT):
                        ins = pe.transpose(tile_of(PS, bank + e, c), tile_of(src, e, c), ident[:, :])
            at_point(ins, "pe")
            await_point(pe, "act", pp, "silB")
            for e in range(2):
                for c in range(NT):
                    ins = pe.transpose(tile_of(PS, 6 + e, c), tile_of(cv, 4 + e, c), ident[:, :])
            at_point(ins, "pe")
            await_point(pe, "dve", pp, "T0")
            for l, b in enumerate(LEVELS):
                n = 2 * (len(LEVELS) * pp + l)
                for e in range(2):
                    if l:
                        pe.wait_ge(d_Um, n - 2 + e + 1)
                    for c in range(NT):
                        ins = mm(tile_of(PS, 4 + e, c), tile_of(wAT, e, c), tile_of(wT, e, c), start=True, stop=True)
                    ins.then_inc(d_X, 1)
                next_panel(pe, u + 4, l)
                for e in range(2):
                    pe.wait_ge(d_Xm, n + e + 1)
                    for c in range(NT):
                        lo, hi = c * 64, (c + 1) * 64
                        if b < 64:
                            mm(PS[:, 6 + e, lo:hi], tile_of(wU, e, c), halves(tile_of(wX, e, c), b)[0], start=True, stop=True)
                        ins = mm(PS[:, 6 + e, 256 + lo:256 + hi], tile_of(wX, e, c), halves(tile_of(wU, e, c), b)[1],
                                 start=True, stop=True)
                    ins.then_inc(d_TU, 1)
            next_panel(pe, u + 4, 6)
            pe.wait_ge(d_Um, 2 * len(LEVELS) * (pp + 1))
            for e in range(2):
                for c in range(NT):
                    mm(tile_of(PS, 4 + e, c), tile_of(wU, e, c), tile_of(wvb, e, c), start=True, stop=True)
                    ins = mm(tile_of(PS, 6 + e, c), tile_of(wkb, e, c), tile_of(wU, e, c), start=True, stop=True)
            at_point(ins, "pe")
            next_panel(pe, u + 4, 7)
            await_point(pe, "act", pp, "uev")
            for c in range(NT):
                if c:
                    for e in range(2):
                        pe.wait_ge(d_S, 2 * (3 * pp + c - 1) + e + 1)
                        mm(PS[:, 6 + e, 0:P], tile_of(wAT, e, c), Sst[:, e, :], start=True, stop=True).then_inc(d_wS, 1)
                for e in range(2):
                    if c:
                        mm(tile_of(PS, 4 + e, c), tile_of(cv, e, c), Sst[:, e, :], start=True, stop=False)
                        pe.wait_ge(d_vn, 2 * (3 * pp + c - 1) + e + 1)
                    if c < NT - 1:
                        mm(PS[:, 6 + e, P:2 * P], tile_of(wkd, e, c), tile_of(wX, e, c), start=True, stop=True).then_inc(d_kv, 1)
                    ins = mm(tile_of(PS, 4 + e, c), tile_of(waT, e, c), tile_of(wX, e, c), start=c == 0, stop=True)
            at_point(ins, "pe")
            await_point(pe, "dve", pp, "on")
            for e in range(2):
                for c in range(NT):
                    ins = pe.transpose(tile_of(PS, 6 + e, c), tile_of(wT, e, c), ident[:, :])
            at_point(ins, "pe")

    def next_panel(pe, u, k):
        s = k // 4
        if k % 4 == 0:
            pe.wait_ge(w_lo, u + s + 1)
        for m in range(4):
            c0 = (k % 4) * 512 + m * P
            ins = mm3(PS[:, m, :], wh[:, s, c0:c0 + P], wl[:, s, c0:c0 + P], h_hi[:, k, :], h_lo[:, k, :], k == 0, k == KD - 1)
        if k % 4 == 3:
            ins.then_inc(w_used, 1)

    def delta_pool(pool):
        los(pool, ud, 16)
        los(pool, U["merge2b"], 2)

    def delta_act(act):
        for pp in range(4):
            u = ud + 4 * pp
            if pp == 0:
                rounds(act, u + 2, 2)
            act.wait_ge(w_used, u + 2)
            if pp:
                await_point(act, "dve", pp - 1, "oy")
            at_point(act.activation(cin[:, 0:4, :], PS[:, 0:4, :], ACT.Copy), "act")
            await_point(act, "dve", pp, "cvA")
            at_point(act.activation(cv[:, 0:4, :], cv[:, 0:4, :], ACT.Silu), "act")
            await_point(act, "pe", pp, "qkT")
            act.activation(wE, PS[:, 0:2, :], ACT.Square)
            at_point(act.activation(wX, PS[:, 2:4, :], ACT.Square), "act")
            await_point(act, "dve", pp, "ss")
            at_point(act.activation(ssq, ssq, ACT.Sqrt), "act")
            act.wait_ge(w_used, u + 4)
            act.activation(dz[:, 2 * pp:2 * pp + 2, :], PS[:, 6:8, :], ACT.Silu)
            at_point(act.activation(cin[:, 4:6, :], PS[:, 4:6, :], ACT.Copy), "act")
            await_point(act, "pe", pp, "qT2")
            at_point(act.activation(cv[:, 0:4, :], PS[:, 0:4, :], ACT.Copy), "act")
            await_point(act, "pe", pp, "Grow")
            at_point(act.activation(wX, PS[:, 4:6, :], ACT.Exp), "act")
            await_point(act, "dve", pp, "cvB")
            at_point(act.activation(cv[:, 4:6, :], cv[:, 4:6, :], ACT.Silu), "act")
            rounds(act, u + 4, 2)
            await_point(act, "dve", pp, "eD")
            at_point(act.activation(wE, wE, ACT.Exp, scale=-1.0), "act")
            await_point(act, "pe", pp, "ATt")
            act.activation(wAT[:, :, :], PS[:, 2:4, :], ACT.Copy)
            at_point(act.activation(waT[:, :, :], PS[:, 4:6, :], ACT.Copy), "act")
            rounds(act, u + 6, 1)
            await_point(act, "pe", pp, "u")
            act.activation(wX, PS[:, 4:6, :], ACT.Copy)
            at_point(act.activation(wAT[:, :, :], PS[:, 6:8, :], ACT.Copy), "act")
            rounds(act, u + 7, 1)
            await_point(act, "pe", pp, "o")
            at_point(act.activation(wE, PS[:, 4:6, :], ACT.Square), "act")
            await_point(act, "dve", pp, "oss")
            at_point(act.activation(ssq[:, 0:8], ssq[:, 0:8], ACT.Sqrt), "act")
            await_point(act, "dve", pp, "oy")
            at_point(act.activation(do_hi[:, 2 * pp:2 * pp + 2, :], wU, ACT.Copy), "act")

    def conv(dve, pp, lo, hi, have):
        await_point(dve, "act", pp, have)
        for back in range(4):
            for a in range(lo, hi):
                c = 8 * (a // 2) + 2 * pp + a % 2
                tap = vecs[:, 1, 24 * (3 - back) + c:24 * (3 - back) + c + 1]
                if back == 0:
                    ins = dve.tensor_scalar(cv[:, a, :], cin[:, a, :], tap, None, ALU.mult)
                else:
                    ins = dve.scalar_tensor_tensor(cv[:, a, back:T], cin[:, a, 0:T - back], tap, cv[:, a, back:T],
                                                   ALU.mult, ALU.add)
            if back < 3:
                dve_link(ins)
        at_point(ins, "dve")

    def delta_dve(dve):
        tt = nc.vector.tensor_tensor
        for pp in range(4):
            conv(dve, pp, 0, 4, "cinA")
            await_point(dve, "act", pp, "sq2")
            dve.tensor_reduce(ssq[:, 0:8], chunks(wE), AX.X, ALU.add)
            dve_link(dve.tensor_reduce(ssq[:, 8:16], chunks(wX), AX.X, ALU.add))
            at_point(dve.tensor_scalar(ssq, ssq, EPS, None, ALU.add), "dve")
            await_point(dve, "act", pp, "sd")
            dve_link(dve.reciprocal(ssq, ssq))
            dve_link(dve.tensor_scalar(ssq[:, 0:8], ssq[:, 0:8], 128 ** -0.5, None, ALU.mult))
            scale = ssq.rearrange("p (a e c) -> p a e c", a=2, e=2)
            tt(chunks(wkd[:, :, :]), chunks(PS[:, 2:4, :]), scale[:, 1].unsqueeze(3).to_broadcast([P, 2, NT, P]), ALU.mult)
            ins = tt(chunks(wE), chunks(PS[:, 0:2, :]), scale[:, 0].unsqueeze(3).to_broadcast([P, 2, NT, P]), ALU.mult)
            at_point(ins, "dve")
            conv(dve, pp, 4, 6, "cinB")
            await_point(dve, "pe", pp, "qT2")
            await_point(dve, "dve", pp, "qn")
            dve_link(tt(chunks(wkb[:, :, :]), chunks(wkd[:, :, :]), per_head(bG, pp), ALU.mult))
            at_point(tt(chunks(wkd[:, :, :]), chunks(wkd[:, :, :]), per_head(kdf, pp), ALU.mult), "dve")
            await_point(dve, "act", pp, "eR")
            dve_link(tt(chunks(wE), chunks(PS[:, 4:6, :]), per_head(Gn, pp), ALU.subtract))
            at_point(dve.tensor_scalar(wE, wE, 0.0, None, ALU.max), "dve")
            await_point(dve, "pe", pp, "kk")
            at_point(tt(cv[:, 0:2, :], cv[:, 0:2, :], wX, ALU.mult), "dve")
            await_point(dve, "act", pp, "eE")
            dve_link(tt(tiles(wT), tiles(wE), everywhere(before), ALU.mult))
            dve_link(tt(wT, PS[:, 6:8, :], wT, ALU.mult))
            at_point(tt(chunks(wU), chunks(wT), per_head(beta, pp), ALU.mult), "dve")
            dve_link(tt(tiles(wE), tiles(wE), everywhere(seen), ALU.mult))
            at_point(tt(wX, PS[:, 0:2, :], wE, ALU.mult), "dve")
            dve_link(tt(tiles(wT), tiles(wU), everywhere(level[1]), ALU.mult))
            dve_link(dve.scalar_tensor_tensor(tiles(wT), tiles(wT), -1.0, everywhere(ident), ALU.mult, ALU.add))
            await_point(dve, "act", pp, "AT")
            dve_link(tt(tiles(wU), tiles(wAT[:, :, :]), everywhere(level1T), ALU.mult))
            at_point(dve.scalar_tensor_tensor(tiles(wU), tiles(wU), -1.0, everywhere(ident), ALU.mult, ALU.add), "dve")
            await_point(dve, "pe", pp, "vT")
            at_point(tt(chunks(wvb[:, :, :]), chunks(PS[:, 6:8, :]), per_head(beta, pp), ALU.mult), "dve")
            for l, b in enumerate(LEVELS):
                n = 2 * (len(LEVELS) * pp + l)
                for e in range(2):
                    dve.wait_ge(d_X, n + e + 1)
                    mask = level[b][:, :].unsqueeze(1).to_broadcast([P, NT, P])
                    tt(wX[:, e, :].rearrange("p (c j) -> p c j", c=NT), PS[:, 4 + e, :].rearrange("p (c j) -> p c j", c=NT), mask,
                       ALU.mult).then_inc(d_Xm, 1)
                for e in range(2):
                    dve.wait_ge(d_TU, n + e + 1)
                    first, second = halves(wT[:, e, :], b)[0], halves(wU[:, e, :], b)[1]
                    if b < 64:
                        tt(first, first, PS[:, 6 + e, 0:256].rearrange("p (g r) -> p g r", r=b), ALU.subtract)
                    tt(second, second, PS[:, 6 + e, 256:512].rearrange("p (g r) -> p g r", r=b), ALU.subtract).then_inc(d_Um, 1)
            for c in range(NT):
                if c:
                    for e in range(2):
                        dve.wait_ge(d_wS, 2 * (3 * pp + c - 1) + e + 1)
                        tt(tile_of(wX, e, c), tile_of(wX, e, c), PS[:, 6 + e, 0:P], ALU.subtract).then_inc(d_vn, 1)
                if c < NT - 1:
                    for e in range(2):
                        dve.wait_ge(d_kv, 2 * (3 * pp + c) + e + 1)
                        if c == 0:
                            ins = dve.tensor_copy(Sst[:, e, :], PS[:, 6 + e, P:2 * P])
                        else:
                            h = 2 * pp + e
                            ins = dve.scalar_tensor_tensor(Sst[:, e, :], Sst[:, e, :], dlast[:, c, h:h + 1], PS[:, 6 + e, P:2 * P],
                                                           ALU.mult, ALU.add)
                        ins.then_inc(d_S, 1)
            await_point(dve, "act", pp, "osq")
            dve_link(dve.tensor_reduce(ssq[:, 0:8], chunks(wE), AX.X, ALU.add))
            at_point(dve.tensor_scalar(ssq[:, 0:8], ssq[:, 0:8], 1 / P, EPS, ALU.mult, ALU.add), "dve")
            await_point(dve, "act", pp, "osd")
            dve_link(dve.reciprocal(ssq[:, 0:8], ssq[:, 0:8]))
            rs = ssq[:, 0:8].rearrange("p (e c) -> p e c", e=2).unsqueeze(3).to_broadcast([P, 2, NT, P])
            at_point(tt(chunks(wT), chunks(PS[:, 4:6, :]), rs, ALU.mult), "dve")
            await_point(dve, "pe", pp, "oT")
            at_point(dve.scalar_tensor_tensor(wU, PS[:, 6:8, :], gain(G_DN, 0), dz[:, 2 * pp:2 * pp + 2, :], ALU.mult, ALU.mult),
                     "dve")
            await_point(dve, "act", pp, "ohi")
            at_point(tt(do_lo[:, 2 * pp:2 * pp + 2, :], wU, do_hi[:, 2 * pp:2 * pp + 2, :].bitcast(F32), ALU.subtract), "dve")

    outn = at("outn", [P, NT, D], offset=SCOPE)
    f_T, f_ev, f_out = (sem("f_" + s) for s in "T ev out".split())

    def final_pe(pe):
        for k in range(KD):
            pe.wait_ge(hf_ready, KD * 5 + k + 1)
            if k == 0:
                pe.wait_ge(sd_ready, 6)
            for t in range(NT):
                ins = pe.transpose(PS[:, k, t * P:(t + 1) * P], hf[:, k % 2, t * P:(t + 1) * P], ident[:, :])
            ins.then_inc(f_T, 1)

    def final_dve(dve):
        dve.wait_ge(sd_ready, 6)
        dve_link(dve.reciprocal(rstd, rstd))
        for k in range(KD):
            if k >= 2:
                dve.wait_ge(f_T, k - 1)
            dve.scalar_tensor_tensor(hf[:, k % 2, :], xT[:, k, :], gain(G_FINAL, k), rstd, ALU.mult, ALU.mult).then_inc(hf_ready, 1)

    def final_act(act):
        for k in range(KD):
            act.wait_ge(f_T, k + 1)
            act.activation(outn[:, :, k * P:(k + 1) * P], PS[:, k, :].rearrange("p (t c) -> p t c", t=NT), ACT.Copy).then_inc(f_ev, 1)

    def final_sp(sp):
        o = out[0].rearrange("(t p) d -> p t d", p=P)
        for j in range(2):
            sp.wait_ge(f_ev, 4 * (j + 1))
            sp.dma_start(o[:, :, j * 512:(j + 1) * 512], outn[:, :, j * 512:(j + 1) * 512]).then_inc(f_out, 16)
        sp.wait_ge(f_out, 32)

    with nc.Block() as block:
        @block.sync
        def _(sp):
            start_sp(sp)
            up_sp(sp, 0, (A['w1_gate'][0], 0), (A['w1_up'][0], 0))
            down_sp(sp, "dn0", A['w1_down'][0], STEPS)
            mid1_sp(sp)
            merge1_sp(sp)
            down_sp(sp, "wout", A['w_out'][0], KD // 2)
            up_sp(sp, 1, (A['w2_gate'][0], 0), (A['w2_up'][0], 0))
            down_sp(sp, "dn1", A['w2_down'][0], STEPS)
            ret_sp(sp)
            branch_sp(sp, "merge2a", 7184, A['w_ret_br_2'][0])
            delta_sp(sp)
            branch_sp(sp, "merge2b", 8208, A['w_dn_br_2'][0])
            down_sp(sp, "wo", A['w_o_2'][0], KD // 2)
            up_sp(sp, 2, (A['w_up_2'][0], 0), (A['w_up_2'][0], FF))
            down_sp(sp, "dn2", A['w_down_2'][0], STEPS)
            final_sp(sp)

        @block.gpsimd
        def _(pool):
            start_pool(pool)
            norm_pool(pool, 0, U["up0"])
            up_pool(pool, 0)
            down_pool(pool, "dn0", STEPS)
            norm_pool(pool, 1, U["mid1"])
            mid1_pool(pool)
            los(pool, U["merge1"] + 2, 10)
            down_pool(pool, "wout", KD // 2)
            norm_pool(pool, 2, U["up1"])
            up_pool(pool, 1)
            down_pool(pool, "dn1", STEPS)
            norm_pool(pool, 3, U["ret"])
            ret_pool(pool)
            delta_pool(pool)
            los(pool, U["merge2b"] + 2, 6)
            down_pool(pool, "wo", KD // 2)
            norm_pool(pool, 4, U["up2"])
            up_pool(pool, 2)
            down_pool(pool, "dn2", STEPS)

        @block.scalar
        def _(act):
            start_act_queue(act)
            start_act(act)
            norm_act(act, 0, U["up0"])
            down_act(act, "dn0", STEPS, up_act(act, 0))
            norm_act(act, 1, U["mid1"])
            mid1_act(act)
            index_act(act)
            stick_act(act)
            sparse_act(act)
            merge1_act(act)
            down_act(act, "wout", KD // 2)
            norm_act(act, 2, U["up1"])
            down_act(act, "dn1", STEPS, up_act(act, 1))
            norm_act(act, 3, U["ret"])
            ret_act(act)
            branch_act(act, "merge2a", 0)
            rounds(act, U["dn"], 2)
            delta_act(act)
            branch_act(act, "merge2b", 1)
            down_act(act, "wo", KD // 2)
            norm_act(act, 4, U["up2"])
            down_act(act, "dn2", STEPS, up_act(act, 2))
            norm_act(act, 5)
            final_act(act)

        @block.vector
        def _(dve):
            start_dve(dve)
            norm_dve(dve, 0, G_FFN1)
            up_dve(dve, 0)
            down_dve(dve, "dn0", 0, STEPS, 0.5)
            norm_dve(dve, 1, G_MIX)
            mid1_dve(dve)
            index_dve(dve)
            stick_dve(dve)
            sparse_dve(dve)
            merge1_dve(dve)
            down_dve(dve, "wout", 1, KD // 2, 1.0)
            norm_dve(dve, 2, G_FFN2)
            up_dve(dve, 1)
            down_dve(dve, "dn1", 2, STEPS, 0.5)
            norm_dve(dve, 3, G_MIX2)
            ret_dve(dve)
            branch_dve(dve, "merge2a", 0)
            dve.wait_ge(lv_set, 1)
            delta_dve(dve)
            branch_dve(dve, "merge2b", 1)
            down_dve(dve, "wo", 3, KD // 2, 1.0)
            norm_dve(dve, 4, G_FFNB)
            up_dve(dve, 2)
            down_dve(dve, "dn2", 4, STEPS, 1.0)
            final_dve(dve)

        @block.tensor
        def _(pe):
            start_pe(pe)
            norm_pe(pe, 0)
            up_pe(pe, 0)
            pe.wait_ge(up_ev, STEPS)
            down_pe(pe, "dn0", 0, STEPS, act_hi, act_lo, (a_ready, 0))
            norm_pe(pe, 1)
            mid1_pe(pe)
            index_pe(pe)
            stick_pe(pe)
            sparse_pe(pe)
            merge1_pe(pe)
            pe.wait_ge(g_mul, 4)
            down_pe(pe, "wout", 1, KD // 2, mg_hi, mg_lo, half_ready(pe, mg_ready))
            norm_pe(pe, 2)
            up_pe(pe, 1)
            pe.wait_ge(up_ev, 2 * STEPS)
            down_pe(pe, "dn1", 2, STEPS, act_hi, act_lo, (a_ready, STEPS))
            norm_pe(pe, 3)
            ret_pe(pe)
            branch_pe(pe, "merge2a", 0, yr_hi, yr_lo, (r_lo, 8))
            delta_pe(pe)
            await_point(pe, "dve", 3, "oy")
            branch_pe(pe, "merge2b", 1, do_hi, do_lo, (passed["dve"], 4 * len(POINTS["dve"])))
            pe.wait_ge(br_mul, 4)
            down_pe(pe, "wo", 3, KD // 2, mh2, ml2, half_ready(pe, br_ready))
            norm_pe(pe, 4)
            up_pe(pe, 2)
            pe.wait_ge(up_ev, 3 * STEPS)
            down_pe(pe, "dn2", 4, STEPS, act_hi, act_lo, (a_ready, 2 * STEPS))
            norm_pe(pe, 5)
            final_pe(pe)


def kernel(**inputs):
    import numpy as _np
    import concourse.bacc as _bacc
    from concourse import mybir as _mybir
    from concourse.bass_utils import run_bass_kernel_spmd as _run

    nc = _bacc.Bacc("TRN2", target_bir_lowering=False, num_devices=1)
    arrays, args = {}, {}
    for name in NAMES:
        a = _np.ascontiguousarray(inputs[name])
        arrays[f"in_{name}_dram"] = a
        args[name] = nc.dram_tensor(f"in_{name}_dram", a.shape, _mybir.dt.from_np(a.dtype), kind="ExternalInput").ap()
    out = nc.dram_tensor("out_0_dram", (1, T, D), F32, kind="ExternalOutput").ap()
    two_blocks_kernel(nc, args, out)
    r = _run(nc, [arrays], core_ids=[0])
    return r.results[0]["out_0_dram"]
```

```python
import math

import numpy as np

import concourse.bass as bass
from concourse import mybir

F32 = mybir.dt.float32
F32R = mybir.dt.float32r
I32 = mybir.dt.int32
ALU = mybir.AluOpType
ACT = mybir.ActivationFunctionType
AX = mybir.AxisListType

P = 128
T = 512
NT = T // P
D = 1024
KD = D // P
FF = 2816
KF = FF // P
HALF = 256
STEPS = FF // HALF
EPS = 1e-6
GN_EPS = 1e-5
NEG = -1e30
TAKEN = -3e38
TOPK = min(256, T // 4)
TWO_PI = 2 * math.pi

NAMES = ['x', 'positions', 'g_ffn1', 'w1_gate', 'w1_up', 'w1_down', 'g_mix', 'w_in', 'g_cq', 'w_uq_a', 'w_q_idx',
         'g_q_a', 'g_k_a', 'w_uv_a', 'w_o_a', 'w_o_b', 'w_out', 'g_ffn2', 'w2_gate', 'w2_up', 'w2_down',
         'g_mix_2', 'w_in_2', 'ret_norm_g_2', 'dn_conv_w_2', 'dn_a_log_2', 'dn_dt_bias_2', 'dn_norm_g_2',
         'w_ret_br_2', 'w_dn_br_2', 'w_o_2', 'g_ffn_2', 'w_up_2', 'ffn_conv_w_2', 'ffn_conv_b_2', 'w_down_2',
         'g_final_2']


def two_blocks_kernel(nc, A, out):
    sb_next = [16512]

    def at(name, shape, dt=F32, offset=None):
        size = 4 * int(np.prod(shape[1:]))
        if offset is None:
            offset = sb_next[0]
            sb_next[0] += (size + 31) // 32 * 32
        assert offset + size <= 229368, (name, offset + size)
        return nc.alloc_sbuf_tensor_at(name, shape, dt, offset=offset)

    def sem(name):
        return nc.alloc_semaphore(name)

    raw = at("raw", [P, 2, 2048])
    wh = at("wh", [P, 2, 2048], F32R)
    wl = at("wl", [P, 2, 2048], F32R)
    xT = at("xT", [P, KD, T])
    h_hi = at("h_hi", [P, KD, T], F32R)
    h_lo = at("h_lo", [P, KD, T], F32R)
    work = at("work", [P, 4096])
    vecs = at("vecs", [P, 4, P])
    ident = at("ident", [P, P])
    ones = at("ones", [P, P])
    cos = at("cos", [P, 2 * NT, 32])
    sin = at("sin", [P, 2 * NT, 32])
    wi_raw = at("wi_raw", [P, KD, 8])
    wi_h = at("wi_h", [P, KD, 8], F32R)
    wi_l = at("wi_l", [P, KD, 8], F32R)
    eps_c = at("eps_c", [P, 1])
    one_c = at("one_c", [P, 1])
    widx = at("widx", [P, NT, 8])
    stat = at("stat", [P, 64])
    rstat = at("rstat", [P, 64])
    SCOPE = sb_next[0]

    PS = nc.alloc_psum_tensor("PS", [P, 8, 512], F32)

    G_FFN1, G_MIX, G_FFN2, G_MIX2, G_FFNB, G_FINAL, G_RET, G_DN, G_CQ = 0, 8, 16, 24, 32, 40, 48, 56, 57
    N_ROWS0 = 59

    def gain(base, k):
        return vecs[:, 0, base + k:base + k + 1]

    counts = [("up0", 22), ("dn0", 22), ("mid1", 10), ("merge1", 12), ("wout", 8), ("up1", 22), ("dn1", 22),
              ("ret", 12), ("merge2a", 8), ("dn", 16), ("merge2b", 8), ("wo", 8), ("up2", 22), ("dn2", 22)]
    U = {}
    n = 0
    for name, c in counts:
        U[name] = n
        n += c

    w_in = [sem("w_in0"), sem("w_in1")]
    w_hi = sem("w_hi")
    w_lo = sem("w_lo")
    w_used = sem("w_used")
    dve_step, act_step, pool_step = sem("dve_step"), sem("act_step"), sem("pool_step")
    count = {"d": 0, "a": 0, "p": 0}

    def dve_link(ins):
        count["d"] += 1
        ins.then_inc(dve_step, 1)
        nc.vector.wait_ge(dve_step, count["d"])

    def act_link(ins):
        count["a"] += 1
        ins.then_inc(act_step, 1)
        nc.scalar.wait_ge(act_step, count["a"])

    def pool_link(ins):
        count["p"] += 1
        ins.then_inc(pool_step, 1)
        nc.gpsimd.wait_ge(pool_step, count["p"])

    def load(sp, u, slot, pieces):
        if not isinstance(u, int) or u >= 2:
            sp.wait_ge(w_lo, u - 1)
        for dst, src in pieces:
            sp.dma_start(dst, src).then_inc(w_in[slot], 16)

    def panel(sp, u, w, k0, nk, c0):
        dst = raw[:, u % 2, 0:nk * 512].rearrange("p (k c) -> p k c", k=nk)
        src = w[k0 * P:(k0 + nk) * P, c0:c0 + 512].rearrange("(k p) c -> p k c", p=P)
        h = nk // 2
        load(sp, u, u % 2, [(dst[:, 0:h], src[:, 0:h]), (dst[:, h:nk], src[:, h:nk])])

    def round_unit(act, u, slot, half_u, size=2048):
        act.wait_ge(w_in[slot], 32 * (half_u + 1))
        if not isinstance(u, int) or u >= 2:
            act.wait_ge(w_used, u - 1)
        nc.scalar.activation(wh[:, slot, 0:size], raw[:, slot, 0:size], ACT.Copy).then_inc(w_hi, 1)

    def rounds(act, u, n, size=2048):
        for j in range(u, u + n):
            round_unit(act, j, j % 2, j // 2, size)

    def lo_unit(pool, u, slot, size=2048):
        pool.wait_ge(w_hi, u + 1)
        nc.gpsimd.tensor_tensor(wl[:, slot, 0:size], raw[:, slot, 0:size], wh[:, slot, 0:size].bitcast(F32),
                                ALU.subtract).then_inc(w_lo, 1)

    def los(pool, u, n, size=2048):
        for j in range(u, u + n):
            lo_unit(pool, j, j % 2, size)

    def mm3(dst, sh, sl, mh, ml, start, stop):
        nc.tensor.matmul(dst, sh, mh, start=start, stop=False)
        nc.tensor.matmul(dst, sh, ml, start=False, stop=False)
        return nc.tensor.matmul(dst, sl, mh, start=False, stop=stop)

    def unit_T(pe, u, slot, bank, k0, nk, mh, ml, first, last, ready=None):
        pe.wait_ge(w_lo, u + 1)
        W, L = (x[:, slot, 0:nk * 512].rearrange("p (k c) -> p k c", k=nk) for x in (wh, wl))
        for k in range(nk):
            if ready:
                pe.wait_ge(ready[0], ready[1] + k0 + k + 1)
            for m in range(4):
                ins = mm3(PS[:, bank + m, :], W[:, k, m * P:(m + 1) * P], L[:, k, m * P:(m + 1) * P],
                          mh[:, k0 + k, :], ml[:, k0 + k, :], first and k == 0, last and k == nk - 1)
        ins.then_inc(w_used, 1)
        return ins

    def unit_N(pe, u, bank, k0, nk, sh, sl, first, last, ready=None):
        pe.wait_ge(w_lo, u + 1)
        W, L = (x[:, u % 2, 0:nk * 512].rearrange("p (k c) -> p k c", k=nk) for x in (wh, wl))
        for k in range(nk):
            if ready:
                pe.wait_ge(ready[0], ready[1] + k0 + k + 1)
            for t in range(NT):
                a, b = sh[:, k0 + k, t * P:(t + 1) * P], sl[:, k0 + k, t * P:(t + 1) * P]
                dst = PS[:, bank + t, :]
                nc.tensor.matmul(dst, a, W[:, k, :], start=first and k == 0, stop=False)
                nc.tensor.matmul(dst, a, L[:, k, :], start=False, stop=False)
                ins = nc.tensor.matmul(dst, b, W[:, k, :], start=False, stop=last and k == nk - 1)
        ins.then_inc(w_used, 1)
        return ins

    crow = at("crow", [P, 4, P], offset=SCOPE)
    xnat = at("xnat", [P, NT, D], offset=SCOPE + 2048)
    posi = at("posi", [P, 2 * NT], I32, offset=SCOPE + 2048 + 16384)
    posf = at("posf", [P, 2 * NT], offset=SCOPE + 2048 + 16384 + 32)
    invf = at("invf", [P, 32], offset=SCOPE + 2048 + 16384 + 64)
    ang = at("ang", [P, 2 * NT, 32], offset=SCOPE + 2048 + 16384 + 192)
    turn = at("turn", [P, 2 * NT, 32], offset=SCOPE + 2048 + 16384 + 192 + 1024)
    over = at("over", [P, 2 * NT, 32], offset=SCOPE + 2048 + 16384 + 192 + 2048)
    consts_in, x_in, consts_set, crow_T, vecs_set, x_T, tables_set, angles_set = (
        sem(s) for s in ("consts_in", "x_in", "consts_set", "crow_T", "vecs_set", "x_T", "tables_set", "angles_set"))
    x_ready = sem("x_ready")
    wi_hi, wi_lo = sem("wi_hi"), sem("wi_lo")
    N_CONST_DMAS = 15

    def start_act_queue(act):
        rows = [(0, G_FFN1, 'g_ffn1', KD), (0, G_MIX, 'g_mix', KD), (0, G_FFN2, 'g_ffn2', KD),
                (0, G_MIX2, 'g_mix_2', KD), (0, G_FFNB, 'g_ffn_2', KD), (0, G_RET, 'ret_norm_g_2', KD),
                (0, G_DN, 'dn_norm_g_2', 1), (0, G_CQ, 'g_cq', 2)]
        for tile, row, name, n in rows:
            act.dma_start(crow[row:row + n, tile, :], A[name][0].rearrange("(k p) -> k p", p=P)).then_inc(consts_in, 16)
        act.dma_start(crow[G_FINAL:G_FINAL + KD, 0, :], A['g_final_2'].rearrange("(k p) -> k p", p=P)).then_inc(consts_in, 16)
        act.dma_start(crow[0:96, 1, :], A['dn_conv_w_2'][0].rearrange("w (k p) -> (w k) p", p=P)).then_inc(consts_in, 16)
        act.dma_start(crow[0:88, 2, :], A['ffn_conv_w_2'][0, 0:2].rearrange("w (k p) -> (w k) p", p=P)).then_inc(consts_in, 16)
        act.dma_start(crow[0:44, 3, :], A['ffn_conv_w_2'][0, 2:3].rearrange("w (k p) -> (w k) p", p=P)).then_inc(consts_in, 16)
        act.dma_start(crow[44:88, 3, :], A['ffn_conv_b_2'][0].rearrange("(k p) -> k p", p=P)).then_inc(consts_in, 16)
        act.dma_start(wi_raw[:, :, :], A['w_in'][0, :, 512:520].rearrange("(k p) c -> p k c", p=P)).then_inc(consts_in, 16)
        with nc.allow_non_contiguous_dma("512 positions, token on partition"):
            act.dma_start(posi[:, 0:NT], A['positions'][0].rearrange("(t p) -> p t", p=P)).then_inc(consts_in, 16)

    def start_sp(sp):
        xs = A['x'][0].rearrange("(t p) d -> p t d", p=P)
        for t in range(NT):
            sp.dma_start(xnat[:, t, :], xs[:, t, :]).then_inc(x_in, 16)

    def start_pool(pool):
        pool.memset(ident[:, :], 0.0)
        pool.memset(ones[:, :], 1.0)
        for j in range(32):
            f = float(np.float32(np.float32(10000.0) ** (-np.float32(2 * j) / np.float32(64))))
            pool.memset(invf[:, j:j + 1], f)
        pool.memset(eps_c[:, :], EPS)
        pool.memset(one_c[:, :], 1.0)
        pool_link(pool.iota(posi[:, NT:2 * NT], pattern=[[P, NT]], base=0, channel_multiplier=1))
        pool.affine_select(out=ident[:, :], in_=ident[:, :], compare_op=ALU.not_equal, fill=1.0, base=0,
                           pattern=[[-1, P]], channel_multiplier=1).then_inc(consts_set, 1)
        pool.wait_ge(wi_hi, 1)
        pool.tensor_tensor(wi_l[:, :, :], wi_raw[:, :, :], wi_h[:, :, :].bitcast(F32), ALU.subtract).then_inc(wi_lo, 1)

    def start_pe(pe):
        pe.wait_ge(consts_set, 1)
        pe.wait_ge(consts_in, 16 * N_CONST_DMAS)
        for tile, n in enumerate((N_ROWS0, 96, 88, 88)):
            ins = pe.transpose(PS[:, 7, tile * P:tile * P + n], crow[0:n, tile, :], ident[0:n, 0:n])
        ins.then_inc(crow_T, 1)
        pe.wait_ge(x_in, 16 * NT)
        pe.wait_ge(vecs_set, 1)
        for k in range(KD):
            for t in range(NT):
                ins = pe.transpose(PS[:, k, t * P:(t + 1) * P], xnat[:, t, k * P:(k + 1) * P], ident[:, :])
            ins.then_inc(x_T, 1)

    def start_dve(dve):
        dve.wait_ge(crow_T, 1)
        for tile, n in enumerate((N_ROWS0, 96, 88, 88)):
            ins = dve.tensor_copy(vecs[:, tile, 0:n], PS[:, 7, tile * P:tile * P + n])
        ins.then_inc(vecs_set, 1)
        for k in range(KD):
            dve.wait_ge(x_T, k + 1)
            dve.tensor_copy(xT[:, k, :], PS[:, k, :]).then_inc(x_ready, 1)
        dve.wait_ge(consts_set, 1)
        dve_link(dve.tensor_copy(posf[:, :], posi[:, :]))
        dve_link(dve.tensor_tensor(ang[:, :, :], posf[:, :].unsqueeze(2).to_broadcast([P, 2 * NT, 32]),
                                   invf[:, :].unsqueeze(1).to_broadcast([P, 2 * NT, 32]), ALU.mult))
        magic = 1.5 * 2 ** 23
        dve_link(dve.tensor_scalar(turn[:, :, :], ang[:, :, :], 1 / TWO_PI, magic, ALU.mult, ALU.add))
        dve_link(dve.tensor_scalar(turn[:, :, :], turn[:, :, :], magic, None, ALU.subtract))
        c1 = 6.28125
        c2 = float(np.round((TWO_PI - c1) * 2 ** 20) / 2 ** 20)
        c3 = TWO_PI - c1 - c2
        for c in (c1, c2, c3):
            dve_link(dve.scalar_tensor_tensor(ang[:, :, :], turn[:, :, :], -c, ang[:, :, :], ALU.mult, ALU.add))
        lim = float(np.nextafter(np.float32(math.pi), np.float32(0)))
        dve_link(dve.tensor_scalar(turn[:, :, :], ang[:, :, :], math.pi / 2, None, ALU.add))
        dve_link(dve.tensor_scalar(over[:, :, :], turn[:, :, :], math.pi, -TWO_PI, ALU.is_gt, ALU.mult))
        dve_link(dve.tensor_tensor(turn[:, :, :], turn[:, :, :], over[:, :, :], ALU.add))
        dve_link(dve.tensor_scalar(turn[:, :, :], turn[:, :, :], lim, -lim, ALU.min, ALU.max))
        dve.tensor_scalar(ang[:, :, :], ang[:, :, :], lim, -lim, ALU.min, ALU.max).then_inc(angles_set, 1)

    def start_act(act):
        act.wait_ge(consts_in, 16 * N_CONST_DMAS)
        act.activation(wi_h[:, :, :], wi_raw[:, :, :], ACT.Copy).then_inc(wi_hi, 1)
        act.wait_ge(angles_set, 1)
        act.activation(sin[:, :, :], ang[:, :, :], ACT.Sin)
        act.activation(cos[:, :, :], turn[:, :, :], ACT.Sin).then_inc(tables_set, 1)

    sq = work[:, 0:1024].rearrange("p (a b) -> p a b", a=2)
    hf = work[:, 1024:2048].rearrange("p (a b) -> p a b", a=2)
    rstd = work[:, 2048:2560]
    sq_ready, sq_used, sd_ready, hf_ready, hi_ready, h_ready = (
        sem(s) for s in ("sq_ready", "sq_used", "sd_ready", "hf_ready", "hi_ready", "h_ready"))

    def norm_act(act, n, u=None):
        if u is not None:
            rounds(act, u, 1)
        act.activation(stat[:, 63:64], eps_c[:, :], ACT.Sqrt)
        for k in range(KD):
            act.wait_ge(x_ready, KD * n + k + 1)
            if k >= 2:
                act.wait_ge(sq_used, KD * n + k - 1)
            act.activation(sq[:, k % 2, :], xT[:, k, :], ACT.Square).then_inc(sq_ready, 1)
        act.wait_ge(sq_used, KD * (n + 1))
        act.activation(rstd, PS[:, 0, :], ACT.Sqrt, bias=eps_c[:, :], scale=1.0 / D).then_inc(sd_ready, 1)
        if u is not None:
            for k in range(KD):
                act.wait_ge(hf_ready, KD * n + k + 1)
                act.activation(h_hi[:, k, :], hf[:, k % 2, :], ACT.Copy).then_inc(hi_ready, 1)
                if k == 1:
                    rounds(act, u + 1, 1)

    def norm_pe(pe, n):
        for k in range(KD):
            pe.wait_ge(sq_ready, KD * n + k + 1)
            ins = nc.tensor.matmul(PS[:, 0, :], ones[:, :], sq[:, k % 2, :], start=k == 0, stop=k == KD - 1)
            ins.then_inc(sq_used, 1)

    def norm_dve(dve, n, g):
        dve.wait_ge(sd_ready, n + 1)
        dve_link(dve.reciprocal(rstd, rstd))
        for k in range(KD):
            if k >= 2:
                dve.wait_ge(h_ready, KD * n + k - 1)
            dve.scalar_tensor_tensor(hf[:, k % 2, :], xT[:, k, :], gain(g, k), rstd, ALU.mult, ALU.mult).then_inc(hf_ready, 1)

    def norm_pool(pool, n, u):
        los(pool, u, 1)
        for k in range(KD):
            pool.wait_ge(hi_ready, KD * n + k + 1)
            pool.tensor_tensor(h_lo[:, k, :], hf[:, k % 2, :], h_hi[:, k, :].bitcast(F32), ALU.subtract).then_inc(h_ready, 1)
            if k == 3:
                los(pool, u + 1, 1)

    act_hi = at("act_hi", [P, KF, T], F32R, offset=SCOPE)
    act_lo = at("act_lo", [P, KF, T], F32R, offset=SCOPE + KF * T * 4)
    sg = work[:, 0:2048].rearrange("p (a b) -> p a b", a=2)
    prod = work[:, 2048:4096].rearrange("p (a b) -> p a b", a=2)
    taps_in = work[:, 0:2048].rearrange("p (a b) -> p a b", a=4)
    taps_out = work[:, 2048:4096].rearrange("p (a b) -> p a b", a=4)
    up_mm, up_ev, sg_ready, conv_done, prod_ready, a_hi, a_ready, dn_done = (
        sem(s) for s in ("up_mm", "up_ev", "sg_ready", "conv_done", "prod_ready", "a_hi", "a_ready", "dn_done"))

    def up_sp(sp, f, wg, wu):
        u0 = U[f"up{f}"]

        def step(i):
            for s in range(2):
                dst = raw[:, s, :].rearrange("p (k c) -> p k c", k=4)
                pieces = []
                for j, (w, c0) in enumerate((wg, wu)):
                    src = w[s * 512:(s + 1) * 512, bass.ds(i * HALF + c0, HALF)].rearrange("(k p) c -> p k c", p=P)
                    pieces.append((dst[:, :, j * HALF:(j + 1) * HALF], src))
                load(sp, u0 + 2 * i + s, s, pieces)

        step(0)
        with sp.Fori(1, STEPS) as i:
            step(i)

    def up_pool(pool, f):
        u0 = U[f"up{f}"]
        with pool.Fori(1, STEPS) as i:
            for s in range(2):
                lo_unit(pool, u0 + 2 * i + s, s)

    def up_pe(pe, f):
        u0, b0 = U[f"up{f}"], STEPS * f

        def step(i, bank):
            fresh = None
            if isinstance(i, int) and i == 0:
                fresh = (h_ready, KD * (0, 2, 4)[f])
            elif not isinstance(i, int) or i > 1 or f:
                pe.wait_ge(up_ev, b0 + i - 1)
            unit_T(pe, u0 + 2 * i, 0, bank, 0, 4, h_hi, h_lo, True, False, fresh)
            unit_T(pe, u0 + 2 * i + 1, 1, bank, 4, 4, h_hi, h_lo, False, True, fresh)

        step(0, 0)
        step(1, 4)
        step(2, 0)
        with pe.Fori(1, STEPS // 2) as pair:
            step(2 * pair + 1, 4)
            step(2 * pair + 2, 0)

    def up_act(act, f):
        u0, b0 = U[f"up{f}"], STEPS * f

        def evac(j, bank):
            act.wait_ge(w_used, u0 + 2 * j + 2)
            if f < 2:
                par = bank // 4
                act.activation(sg[:, par, :].rearrange("p (a b) -> p a b", a=2), PS[:, bank:bank + 2, :],
                               ACT.Silu).then_inc(sg_ready, 1)
            else:
                act.activation(taps_in[:, :, :], PS[:, bank:bank + 4, :], ACT.Copy).then_inc(up_ev, 1)

        def high_part(j, bank):
            if f < 2:
                act.wait_ge(up_ev, b0 + j + 1)
                src = prod[:, bank // 4, :].rearrange("p (a b) -> p a b", a=2)
            else:
                act.wait_ge(conv_done, j + 1)
                act.activation(taps_out[:, 0:2, :], taps_out[:, 0:2, :], ACT.Silu).then_inc(sg_ready, 1)
                act.wait_ge(prod_ready, j + 1)
                src = taps_out[:, 0:2, :]
            act.activation(act_hi[:, bass.ds(2 * j, 2), :], src, ACT.Copy).then_inc(a_hi, 1)

        def between(j, bank):
            round_unit(act, u0 + 2 * j + 3, 1, u0 // 2 + j + 1)
            evac(j, bank)
            round_unit(act, u0 + 2 * j + 4, 0, u0 // 2 + j + 2)
            high_part(j, bank)

        round_unit(act, u0 + 2, 0, u0 // 2 + 1)
        with act.Fori(0, STEPS // 2) as pair:
            between(2 * pair, 0)
            between(2 * pair + 1, 4)

        def last():
            evac(STEPS - 1, 0)
            high_part(STEPS - 1, 0)

        return last

    def up_dve(dve, f):
        b0 = STEPS * f

        def step(j, bank, par):
            if f < 2:
                dve.wait_ge(sg_ready, b0 + j + 1)
                src = prod[:, par, :].rearrange("p (a b) -> p a b", a=2)
                dve.tensor_tensor(src, sg[:, par, :].rearrange("p (a b) -> p a b", a=2), PS[:, bank + 2:bank + 4, :],
                                  ALU.mult).then_inc(up_ev, 1)
            else:
                dve.wait_ge(up_ev, b0 + j + 1)
                dve.wait_ge(a_ready, b0 + j)
                taps(dve, j)
                dve.wait_ge(sg_ready, b0 + j + 1)
                src = taps_out[:, 0:2, :]
                dve.tensor_tensor(src, src, taps_out[:, 2:4, :], ALU.mult).then_inc(prod_ready, 1)
            dve.wait_ge(a_hi, b0 + j + 1)
            dve.tensor_tensor(act_lo[:, bass.ds(2 * j, 2), :], src, act_hi[:, bass.ds(2 * j, 2), :].bitcast(F32),
                              ALU.subtract).then_inc(a_ready, 1)

        step(0, 0, 0)
        with dve.Fori(0, STEPS // 2) as pair:
            i = 2 * pair + 1
            step(i, 4, 1)
            step(i + 1, 0, 0)

    tap_a, tap_b = sem("tap_a"), sem("tap_b")

    def taps(dve, j):
        tiles = [(m, 2 * j + m if m < 2 else KF + 2 * j + m - 2) for m in range(4)]

        def col(tile, row):
            return vecs[:, tile, bass.ds(row, 1)]

        for m, c in tiles:
            ins = dve.tensor_scalar(taps_out[:, m, :], taps_in[:, m, :], col(3, c), col(3, c + 44), ALU.mult, ALU.add)
        ins.then_inc(tap_a, 1)
        dve.wait_ge(tap_a, j + 1)
        for m, c in tiles:
            ins = dve.scalar_tensor_tensor(taps_out[:, m, 1:T], taps_in[:, m, 0:T - 1], col(2, c + 44),
                                           taps_out[:, m, 1:T], ALU.mult, ALU.add)
        ins.then_inc(tap_b, 1)
        dve.wait_ge(tap_b, j + 1)
        for m, c in tiles:
            ins = dve.scalar_tensor_tensor(taps_out[:, m, 2:T], taps_in[:, m, 0:T - 2], col(2, c),
                                           taps_out[:, m, 2:T], ALU.mult, ALU.add)
        ins.then_inc(conv_done, 1)

    def half_ready(pe, signal):
        def wait(i):
            if isinstance(i, int) and i == 0:
                pe.wait_ge(signal, 2)
            else:
                pe.wait_ge(signal, 4 if isinstance(i, int) else 2 * i)
        return wait

    def down_sp(sp, stage, w, steps):
        u0 = U[stage]
        with sp.Fori(0, steps) as i:
            for s in range(2):
                pieces = [(raw[:, s, c:c + 512], w[bass.ds((2 * i + s) * P, P), c:c + 512]) for c in (0, 512)]
                load(sp, u0 + 2 * i + s, s, pieces)

    def down_act(act, stage, steps, before=None, ahead=False):
        u0 = U[stage]

        def rnd(i):
            for s in range(2):
                round_unit(act, u0 + 2 * i + s, s, u0 // 2 + i, 1024)

        if ahead:
            with act.Fori(1, steps) as i:
                rnd(i)
        elif before:
            round_unit(act, u0 + 1, 1, u0 // 2, 1024)
            before()
            with act.Fori(1, steps) as i:
                rnd(i)
        else:
            with act.Fori(0, steps) as i:
                rnd(i)

    def down_pool(pool, stage, steps):
        with pool.Fori(0, steps) as i:
            for s in range(2):
                lo_unit(pool, U[stage] + 2 * i + s, s, 1024)

    def down_pe(pe, stage, order, steps, mh, ml, ready=None):
        u0 = U[stage]

        def step(i, first=False, last=False):
            if callable(ready):
                ready(i)
            elif ready:
                pe.wait_ge(ready[0], ready[1] + i + 1)
            for s in range(2):
                pe.wait_ge(w_lo, u0 + 2 * i + s + 1)
                for m in range(KD):
                    ins = mm3(PS[:, m, :], wh[:, s, m * P:(m + 1) * P], wl[:, s, m * P:(m + 1) * P],
                              mh[:, bass.ds(2 * i + s, 1), :].rearrange("p a b -> p (a b)"),
                              ml[:, bass.ds(2 * i + s, 1), :].rearrange("p a b -> p (a b)"),
                              first and s == 0, last and s == 1)
                    if last and s == 1 and m < KD - 1:
                        ins.then_inc(dn_done, 1)
                ins.then_inc(w_used, 1)

        step(0, first=True)
        with pe.Fori(1, steps - 1) as i:
            step(i)
        step(steps - 1, last=True)

    def down_dve(dve, stage, order, steps, scale):
        for m in range(KD):
            if m < KD - 1:
                dve.wait_ge(dn_done, (KD - 1) * order + m + 1)
            else:
                dve.wait_ge(w_used, U[stage] + 2 * steps)
            dve.scalar_tensor_tensor(xT[:, m, :], PS[:, m, :], scale, xT[:, m, :], ALU.mult, ALU.add).then_inc(x_ready, 1)

    Y_B, Y_A, R1, R3 = SCOPE, SCOPE + 16384, SCOPE + 32768, SCOPE + 32768 + 24576
    PER = 64

    def stack(offset, *specs):
        got = []
        for name, shape, dt in specs:
            got.append(at(name, shape, dt, offset=offset))
            offset += 4 * int(np.prod(shape[1:]))
        return got

    yb_hi, yb_lo = stack(Y_B, ("yb_hi", [P, 4, T], F32R), ("yb_lo", [P, 4, T], F32R))
    ya_hi, ya_lo = stack(Y_A, ("ya_hi", [P, 4, T], F32R), ("ya_lo", [P, 4, T], F32R))
    cq_hi, cq_lo, qn = stack(Y_A, ("cq_hi", [P, 2, T], F32R), ("cq_lo", [P, 2, T], F32R), ("qn", [P, NT, 512], F32))
    qbT, kbT, vb = stack(R1, ("qbT", [P, 4, T], F32), ("kbT", [P, 4, T], F32), ("vb", [P, NT, 512], F32))
    lg, pr, pT, olT = stack(R1, ("lg", [P, 2, T], F32), ("pr", [P, 3, T], F32), ("pT", [P, NT, 512], F32),
                            ("olT", [P, 512], F32))
    soff = [None, 0, 2 * P, 5 * P, 9 * P]
    score, lgi = stack(Y_A, ("score", [P, soff[4]], F32), ("lgi", [P, 2, T], F32))
    pn, qaT, qiT, kaT, kiT, wuv, gq, gk, lower, negtri, negone = stack(
        R3, ("pn", [P, NT, 512], F32), ("qaT", [P, 4, T], F32), ("qiT", [P, 4, T], F32), ("kaT", [P, T], F32),
        ("kiT", [P, T], F32), ("wuv", [P, 8, 64], F32), ("gq", [P, 64], F32), ("gk", [P, 64], F32),
        ("lower", [P, P], F32), ("negtri", [P, P], F32), ("negone", [P, P], F32))
    drop = at("drop", [P, soff[4]], offset=R3 + 16384)
    rqa = at("rqa", [P, 2048], offset=Y_A)
    mg_hi, mg_lo, gt, gt2 = stack(R1, ("mg_hi", [P, KD, T], F32R), ("mg_lo", [P, KD, T], F32R),
                                  ("gt", [P, 2048], F32), ("gt2", [P, 2048], F32))
    mtmp = work[:, 0:2048]
    r1, r2 = work[:, 0:1024], work[:, 1024:2048]
    rot = work[:, 2048:4096]
    off = [0, 512, 1024, 896]
    wid = [512, 384, 256, 128]
    SPAN = 1280
    stick = work[:, 0:3 * SPAN].rearrange("p (a b) -> p a b", a=3)

    (m1_consts, m1_dma, pn_mm, pn_ev, wi_mm, wi_ev, qb_ev, kb_ev, vb_ev, cqn_set, cq_T, cq_hi_s, cq_s, kd_set, kd_T,
     kT_ev, qa_sq, qa_set, qa_T, qa_ev, qi_set, qi_T, qi_ev, m1_sd) = (
        sem("m1_" + s) for s in ("consts dma pn_mm pn_ev wi_mm wi_ev qb_ev kb_ev vb_ev cqn_set cq_T cq_hi cq_set kd_set kd_T "
                                 "kT_ev qa_sq qa_set qa_T qa_ev qi_set qi_T qi_ev sd").split())
    b_z, b_ln, b_sp, b_spm, b_acc, b_exp, b_am, b_pv, b_hi, b_lo = (
        sem("b_" + s) for s in "z ln sp spm acc exp am pv hi lo".split())
    a_dot, a_relu, a_causal, a_lg, a_lgm, a_exp, a_pr, a_pT, a_pTev, a_ol, a_olev, a_o, a_yhi, a_ylo = (
        sem("a_" + s) for s in "dot relu causal lg lgm exp pr pT pTev ol olev o yhi ylo".split())
    a_rused, wuv_in = sem("a_rused"), sem("wuv_in")
    g_sig, g_mul, g_hi, mg_ready = (sem("g_" + s) for s in "sig mul hi ready".split())
    u1 = U["mid1"]

    def bcast_h(table, heads):
        return table.unsqueeze(2).to_broadcast([P, NT, heads, 32])

    def rotate(link, src, dst, tab, heads, last=None):
        c, s = bcast_h(cos[:, tab:tab + NT, :], heads), bcast_h(sin[:, tab:tab + NT, :], heads)
        n = NT * heads * 32
        a = r1[:, 0:n].rearrange("p (t h d) -> p t h d", t=NT, h=heads)
        b = r2[:, 0:n].rearrange("p (t h d) -> p t h d", t=NT, h=heads)
        x1, x2 = src[:, :, :, 0:32], src[:, :, :, 32:64]
        v = nc.vector
        v.tensor_tensor(a, x1, c, ALU.mult)
        link(v.tensor_tensor(b, x2, s, ALU.mult))
        link(v.tensor_tensor(dst[:, :, :, 0:32], a, b, ALU.subtract))
        v.tensor_tensor(a, x1, s, ALU.mult)
        link(v.tensor_tensor(b, x2, c, ALU.mult))
        return v.tensor_tensor(dst[:, :, :, 32:64], a, b, ALU.add)

    def mid1_sp(sp):
        w = A['w_in'][0]
        for u, c0 in ((u1, 0), (u1 + 2, 520), (u1 + 6, 1032), (u1 + 8, 1544)):
            if u == u1 + 6:
                panel(sp, u1 + 4, A['w_uq_a'][0], 0, 2, 0)
                panel(sp, u1 + 5, A['w_q_idx'][0], 0, 2, 0)
            panel(sp, u, w, 0, 4, c0)
            panel(sp, u + 1, w, 4, 4, c0)

    def mid1_pool(pool):
        pool.wait_ge(x_ready, KD * 2)
        pool.memset(negone[:, :], -1.0)
        pool_link(pool.memset(lower[:, :], 0.0))
        pool.affine_select(out=negtri[:, :], in_=negone[:, :], compare_op=ALU.is_ge, fill=0.0, base=0,
                           pattern=[[-1, P]], channel_multiplier=1)
        pool.affine_select(out=lower[:, :], in_=lower[:, :], compare_op=ALU.is_ge, fill=NEG, base=0,
                           pattern=[[-1, P]], channel_multiplier=1).then_inc(m1_consts, 1)
        los(pool, u1 + 2, 2)
        los(pool, u1 + 4, 2, 1024)
        los(pool, u1 + 6, 4)
        los(pool, U["merge1"], 2)
        for i in range(1, NT):
            pool.wait_ge(a_rused, 8 * i)
            d = score[:, soff[i] + i * P:soff[i + 1]]
            pool.affine_select(out=d, in_=d, compare_op=ALU.is_ge, fill=NEG, base=0,
                               pattern=[[-1, P]], channel_multiplier=1).then_inc(a_causal, 1)
        for h in range(8 + 1):
            if h < 8:
                pool.wait_ge(b_sp, h + 1)
                earlier_keys(pool, h).then_inc(b_spm, 1)
            if h:
                pool.wait_ge(b_exp, h)
                earlier_keys(pool, h - 1).then_inc(b_am, 1)

    def earlier_keys(pool, h):
        for j in range(NT):
            d = stick[:, h % 3, off[j]:off[j] + P]
            ins = pool.affine_select(out=d, in_=d, compare_op=ALU.is_gt, fill=0.0, base=0,
                                     pattern=[[1, P]], channel_multiplier=-1)
        return ins

    wiT = work[0:8, 3072:3584]
    wi_cp, wi_T = sem("wi_copied"), sem("wi_turned")

    def narrow_product(wide_hi, wide_lo, dst):
        for k in range(KD):
            ins = mm3(dst, wide_hi[:, k, :], wide_lo[:, k, :], h_hi[:, k, :], h_lo[:, k, :], k == 0, k == KD - 1)
        return ins

    def mid1_pe(pe):
        unit_N(pe, u1, 0, 0, 4, h_hi, h_lo, True, False, (h_ready, KD))
        unit_N(pe, u1 + 1, 0, 4, 4, h_hi, h_lo, False, True, (h_ready, KD))
        unit_T(pe, u1 + 2, 0, 4, 0, 4, h_hi, h_lo, True, False)
        unit_T(pe, u1 + 3, 1, 4, 4, 4, h_hi, h_lo, False, True)
        pe.wait_ge(pn_ev, 1)
        pe.wait_ge(wi_lo, 1)
        narrow_product(wi_h, wi_l, PS[0:8, 3, :]).then_inc(wi_mm, 1)
        pe.wait_ge(cqn_set, 1)
        for k in range(2):
            for t in range(NT):
                ins = pe.transpose(PS[:, k, t * P:(t + 1) * P], pn[:, t, k * P:(k + 1) * P], ident[:, :])
        ins.then_inc(cq_T, 1)
        pe.wait_ge(wi_cp, 1)
        for t in range(NT):
            ins = pe.transpose(PS[:, 2, 8 * t:8 * t + 8], wiT[:, t * P:(t + 1) * P], ident[0:8, 0:8])
        ins.then_inc(wi_T, 1)
        pe.wait_ge(wi_ev, 1)
        pe.wait_ge(kd_set, 1)
        for k in range(2):
            for t in range(NT):
                ins = pe.transpose(PS[:, 2 + k, t * P:(t + 1) * P], kd[:, t, k * P:(k + 1) * P], ident[:, :])
        ins.then_inc(kd_T, 1)
        pe.wait_ge(qb_ev, 1)
        pe.wait_ge(cq_s, 1)
        unit_N(pe, u1 + 4, 4, 0, 2, cq_hi, cq_lo, True, True)
        pe.wait_ge(kT_ev, 1)
        unit_N(pe, u1 + 5, 0, 0, 2, cq_hi, cq_lo, True, True)
        pe.wait_ge(qa_sq, 1)
        unit_T(pe, u1 + 6, 0, 4, 0, 4, h_hi, h_lo, True, False)
        unit_T(pe, u1 + 7, 1, 4, 4, 4, h_hi, h_lo, False, True)
        pe.wait_ge(qi_set, 1)
        unit_N(pe, u1 + 8, 0, 0, 4, h_hi, h_lo, True, False)
        unit_N(pe, u1 + 9, 0, 4, 4, h_hi, h_lo, False, True)
        for have, src, free, bank, done in ((qi_set, rot, kb_ev, 4, qi_T), (qa_set, rqa, vb_ev, 0, qa_T)):
            pe.wait_ge(have, 1)
            pe.wait_ge(free, 1)
            for k in range(4):
                for t in range(NT):
                    ins = pe.transpose(PS[:, bank + k, t * P:(t + 1) * P], src[:, t * 512 + k * P:t * 512 + (k + 1) * P],
                                       ident[:, :])
            ins.then_inc(done, 1)
        pe.wait_ge(qi_ev, 1)
        pe.wait_ge(qa_ev, 1)

    def index_pe(pe):
        n = 0
        for i in range(1, NT):
            for h in range(8):
                r = PER * (h % 2)
                if n >= 4:
                    pe.wait_ge(a_relu, n - 3)
                nc.tensor.matmul(PS[:, n % 4, 0:(i + 1) * P], qiT[r:r + PER, h // 2, i * P:(i + 1) * P],
                                 kiT[r:r + PER, 0:(i + 1) * P], start=True, stop=True).then_inc(a_dot, 1)
                n += 1
        pe.wait_ge(a_relu, n)

    def index_act(act):
        n = 0
        for i in range(1, NT):
            for h in range(8):
                act.wait_ge(a_dot, n + 1)
                if n >= 2:
                    act.wait_ge(a_rused, n - 1)
                act.activation(lgi[:, n % 2, 0:(i + 1) * P], PS[:, n % 4, 0:(i + 1) * P], ACT.Relu).then_inc(a_relu, 1)
                n += 1

    def index_dve(dve):
        n = 0
        for i in range(1, NT):
            s = score[:, soff[i]:soff[i + 1]]
            for h in range(8):
                dve.wait_ge(a_relu, n + 1)
                w = widx[:, i, h:h + 1]
                if h == 0:
                    ins = dve.tensor_scalar(s, lgi[:, n % 2, 0:(i + 1) * P], w, None, ALU.mult)
                else:
                    dve.wait_ge(a_rused, n)
                    ins = dve.scalar_tensor_tensor(s, lgi[:, n % 2, 0:(i + 1) * P], w, s, ALU.mult, ALU.add)
                ins.then_inc(a_rused, 1)
                n += 1

    def topk_round(dve, n):
        i = 1 + n // (TOPK // 8)
        s = score[:, soff[i]:soff[i + 1]]
        if n % (TOPK // 8) == 0:
            dve.wait_ge(a_causal, i)
        dve_link(dve.max(rstat[:, 40:48], s))
        dve_link(dve.match_replace(s, rstat[:, 40:48], s, TAKEN))
        if (n + 1) % (TOPK // 8) == 0:
            dve_link(dve.tensor_scalar(drop[:, soff[i]:soff[i + 1]], s, -1e38, NEG, ALU.is_ge, ALU.mult))

    def scores_of(h):
        b = 3 * (h % 2)
        return PS[:, b:b + 3, :].rearrange("p a c -> p (a c)")[:, 0:SPAN]

    def stick_pe(pe):
        for h in range(-1, 8):
            if h + 1 < 8:
                g, z = h + 1, scores_of(h + 1)
                r = PER * (g % 2)
                if g >= 2:
                    pe.wait_ge(b_exp, g - 1)
                for j in range(NT):
                    ins = nc.tensor.matmul(z[:, off[j]:off[j] + wid[j]], kbT[r:r + PER, g // 2, j * P:(j + 1) * P],
                                           qbT[r:r + PER, g // 2, j * P:T], start=j < NT - 1, stop=False,
                                           skip_group_check=True)
                ins.then_inc(b_z, 1)
            if h >= 0:
                z = scores_of(h)
                pe.wait_ge(b_spm, h + 1)
                for j in range(NT):
                    for i in range(j, NT):
                        c = off[j] + (i - j) * P
                        ins = nc.tensor.matmul(z[:, c:c + wid[i]], negtri[:, :] if i == j else negone[:, :],
                                               stick[:, h % 3, off[i]:off[i] + wid[i]], start=False, stop=i == NT - 1,
                                               skip_group_check=True)
                ins.then_inc(b_acc, 1)
            if h >= 1:
                stick_out(pe, h - 1)
        stick_out(pe, 7)

    def stick_out(pe, h):
        r = PER * (h % 2)
        pe.wait_ge(b_am, h + 1)
        if h >= 2:
            pe.wait_ge(b_lo, h - 1)
        for j in range(NT):
            ins = nc.tensor.matmul(PS[r:r + PER, 6 + h % 2, j * P:T], vb[:, j, h * PER:(h + 1) * PER],
                                   stick[:, h % 3, off[j]:off[j] + wid[j]], start=j == 0, stop=j == NT - 1,
                                   skip_group_check=True)
        ins.then_inc(b_pv, 1)

    def stick_act(act):
        rounds(act, U["merge1"], 2)
        for h in range(-1, 8):
            if h + 1 < 8:
                g = h + 1
                e = stick[:, g % 3, :]
                act.wait_ge(b_z, g + 1)
                if g >= 3:
                    act.wait_ge(b_pv, g - 2)
                act_link(act.activation(e, scores_of(g), ACT.Abs))
                act_link(act.activation(e, e, ACT.Exp, scale=-1.0))
                act.activation(e, e, ACT.Ln, bias=one_c[:, :]).then_inc(b_ln, 1)
            if h >= 0:
                act.wait_ge(b_acc, h + 1)
                act.activation(stick[:, h % 3, :], scores_of(h), ACT.Exp).then_inc(b_exp, 1)
            if h >= 1:
                stick_hi(act, h - 1)
        stick_hi(act, 7)

    def stick_hi(act, h):
        r = PER * (h % 2)
        act.wait_ge(b_pv, h + 1)
        act.activation(yb_hi[r:r + PER, h // 2, :], PS[r:r + PER, 6 + h % 2, :], ACT.Copy).then_inc(b_hi, 1)

    def stick_dve(dve):
        share = 3 * (TOPK // 8) // 16
        for h in range(8 + 1):
            if h < 8:
                e = stick[:, h % 3, :]
                dve.wait_ge(b_ln, h + 1)
                dve.scalar_tensor_tensor(e, scores_of(h), 0.0, e, ALU.max, ALU.add).then_inc(b_sp, 1)
                for n in range(share):
                    topk_round(dve, 2 * h * share + n)
            if h:
                r = PER * ((h - 1) % 2)
                dve.wait_ge(b_hi, h)
                dve.tensor_tensor(yb_lo[r:r + PER, (h - 1) // 2, :], PS[r:r + PER, 6 + (h - 1) % 2, :],
                                  yb_hi[r:r + PER, (h - 1) // 2, :].bitcast(F32), ALU.subtract).then_inc(b_lo, 1)
            if h < 8:
                for n in range(share):
                    topk_round(dve, (2 * h + 1) * share + n)

    LAG, GS = 2, 8 * NT

    def sparse_pe(pe):
        pe.wait_ge(wuv_in, 16)
        pe.wait_ge(b_lo, 8)
        for g in range(GS + LAG + 3):
            if g < GS:
                i, h = g // 8, g % 8
                r, S = PER * (h % 2), (i + 1) * P
                if g >= 2:
                    pe.wait_ge(a_lg, g - 1)
                nc.tensor.matmul(PS[:, g % 2, 0:S], qaT[r:r + PER, h // 2, i * P:(i + 1) * P],
                                 kaT[r:r + PER, 0:S], start=True, stop=True).then_inc(a_lgm, 1)
            n = g - LAG
            if n >= 4 and n % 4 == 0:
                quad = n // 4 - 1
                tiles_seen = quad // 2 + 1
                pe.wait_ge(a_pTev, quad + 1)
                if quad:
                    pe.wait_ge(a_olev, quad)
                for j in range(tiles_seen):
                    ins = nc.tensor.matmul(PS[:, 6, :], pn[:, j, 320:448], pT[:, j, :], start=j == 0, stop=j == tiles_seen - 1)
                ins.then_inc(a_ol, 1)
            if 0 <= n < GS:
                i, h = n // 8, n % 8
                pe.wait_ge(a_pr, n + 1)
                for j in range(i + 1):
                    ins = pe.transpose(PS[:, 2 + j, (h % 4) * P:(h % 4 + 1) * P], pr[:, n % 3, j * P:(j + 1) * P], ident[:, :])
                ins.then_inc(a_pT, 1)
            if n >= 5 and n % 4 == 1:
                quad = n // 4 - 1
                pe.wait_ge(a_olev, quad + 1)
                if quad:
                    pe.wait_ge(a_ylo, quad)
                for hh in range(4):
                    r = PER * (hh % 2)
                    ins = nc.tensor.matmul(PS[r:r + PER, 7, (hh // 2) * P:(hh // 2 + 1) * P], wuv[:, 4 * (quad % 2) + hh, :],
                                           olT[:, hh * P:(hh + 1) * P], start=True, stop=True)
                ins.then_inc(a_o, 1)

    def quad_of_y(y, quad):
        i, pair = quad // 2, 2 * (quad % 2)
        return y[:, pair:pair + 2, i * P:(i + 1) * P]

    def sparse_act(act):
        for g in range(GS + LAG + 3):
            if g < GS:
                S = (g // 8 + 1) * P
                act.wait_ge(a_lg, g + 1)
                if g >= 3:
                    act.wait_ge(a_pT, g - 2)
                act.activation(pr[:, g % 3, 0:S], lg[:, g % 2, 0:S], ACT.Exp, bias=rstat[:, 32 + g % 2:33 + g % 2],
                               accum_out=rstat[:, 48 + g % 3:49 + g % 3]).then_inc(a_exp, 1)
            n = g - LAG
            if 0 <= n < GS and n % 4 == 3:
                act.wait_ge(a_pT, n + 1)
                if n >= 4:
                    act.wait_ge(a_ol, n // 4)
                act.activation(pT[:, 0:n // 8 + 1, :], PS[:, 2:3 + n // 8, :], ACT.Copy).then_inc(a_pTev, 1)
            if n >= 5 and n % 4 == 1:
                quad = n // 4 - 1
                act.wait_ge(a_o, quad + 1)
                act.activation(quad_of_y(ya_hi, quad), PS[:, 7, 0:256].rearrange("p (a b) -> p a b", a=2),
                               ACT.Copy).then_inc(a_yhi, 1)

    def sparse_dve(dve):
        for g in range(GS + LAG + 3):
            n = g - LAG
            if 0 <= n < GS:
                S = (n // 8 + 1) * P
                dve.wait_ge(a_exp, n + 1)
                if n:
                    dve.wait_ge(a_pr, n)
                dve_link(dve.reciprocal(rstat[:, 38:39], rstat[:, 48 + n % 3:49 + n % 3]))
                dve.tensor_scalar(pr[:, n % 3, 0:S], pr[:, n % 3, 0:S], rstat[:, 38:39], None, ALU.mult).then_inc(a_pr, 1)
            if g < GS:
                i = g // 8
                S = (i + 1) * P
                chosen = drop[:, soff[i]:soff[i + 1]] if i else lower[:, :]
                dve.wait_ge(a_lgm, g + 1)
                if g >= 2:
                    dve.wait_ge(a_exp, g - 1)
                dve_link(dve.tensor_tensor_reduce(out=lg[:, g % 2, 0:S], in0=PS[:, g % 2, 0:S], in1=chosen, scale=1.0,
                                                  scalar=TAKEN, op0=ALU.add, op1=ALU.max, accum_out=rstat[:, 52 + g % 2:53 + g % 2]))
                dve.tensor_scalar(rstat[:, 32 + g % 2:33 + g % 2], rstat[:, 52 + g % 2:53 + g % 2], -1.0, None,
                                  ALU.mult).then_inc(a_lg, 1)
            if n >= 4 and n % 4 == 0:
                dve.wait_ge(a_ol, n // 4)
                dve.tensor_copy(olT[:, :], PS[:, 6, :]).then_inc(a_olev, 1)
            if n >= 5 and n % 4 == 1:
                quad = n // 4 - 1
                dve.wait_ge(a_yhi, quad + 1)
                dve.tensor_tensor(quad_of_y(ya_lo, quad), PS[:, 7, 0:256].rearrange("p (a b) -> p a b", a=2),
                                  quad_of_y(ya_hi, quad).bitcast(F32), ALU.subtract).then_inc(a_ylo, 1)

    kd = work[:, 2048:3072].rearrange("p (t c) -> p t c", t=NT)

    def mid1_act(act):
        act.wait_ge(x_ready, KD * 2)
        act.dma_start(gq[:, :], A['g_q_a'][0].partition_broadcast(P)).then_inc(m1_dma, 16)
        act.dma_start(gk[:, :], A['g_k_a'][0].partition_broadcast(P)).then_inc(m1_dma, 16)
        act.dma_start(wuv[:, :, :], A['w_uv_a'][0].rearrange("h c d -> c h d")).then_inc(wuv_in, 16)
        rounds(act, u1 + 2, 2)
        act.wait_ge(w_used, u1 + 2)
        act.activation(pn[:, :, :], PS[:, 0:4, :], ACT.Copy).then_inc(pn_ev, 1)
        act.wait_ge(m1_sd, 1)
        act.activation(stat[:, 0:8], stat[:, 0:8], ACT.Sqrt).then_inc(m1_sd, 1)
        rounds(act, u1 + 4, 1, 1024)
        act.wait_ge(w_used, u1 + 4)
        act.activation(qbT[:, :, :], PS[:, 4:8, :], ACT.Copy, scale=PER ** -0.5).then_inc(qb_ev, 1)
        rounds(act, u1 + 5, 1, 1024)
        act.wait_ge(wi_mm, 1)
        act.activation(wiT, PS[0:8, 3, :], ACT.Copy).then_inc(wi_cp, 1)
        act.wait_ge(cq_T, 1)
        for k in range(2):
            ins = act.activation(cq_hi[:, k, :], PS[:, k, :], ACT.Copy, scale=gain(G_CQ, k))
        ins.then_inc(cq_hi_s, 1)
        act.wait_ge(kd_T, 1)
        act.activation(kaT[:, :], PS[:, 2, :], ACT.Copy)
        act.activation(kiT[:, :], PS[:, 3, :], ACT.Copy).then_inc(kT_ev, 1)
        rounds(act, u1 + 6, 1)
        act.wait_ge(w_used, u1 + 5)
        act.activation(work[:, 0:2048].rearrange("p (t c) -> p t c", t=NT), PS[:, 4:8, :], ACT.Square)
        act.activation(qn[:, :, :], PS[:, 4:8, :], ACT.Copy).then_inc(qa_sq, 1)
        rounds(act, u1 + 7, 1)
        act.wait_ge(m1_sd, 3)
        act.activation(stat[:, 8:40], stat[:, 8:40], ACT.Sqrt).then_inc(m1_sd, 1)
        rounds(act, u1 + 8, 1)
        act.wait_ge(w_used, u1 + 8)
        act.activation(kbT[:, :, :], PS[:, 4:8, :], ACT.Copy).then_inc(kb_ev, 1)
        rounds(act, u1 + 9, 1)
        act.wait_ge(w_used, u1 + 10)
        act.activation(vb[:, :, :], PS[:, 0:4, :], ACT.Copy).then_inc(vb_ev, 1)
        act.wait_ge(qi_T, 1)
        act.activation(qiT[:, :, :], PS[:, 4:8, :], ACT.Copy).then_inc(qi_ev, 1)
        act.wait_ge(qa_T, 1)
        act.activation(qaT[:, :, :], PS[:, 0:4, :], ACT.Copy, scale=PER ** -0.5).then_inc(qa_ev, 1)

    def mid1_dve(dve):
        dve.wait_ge(pn_ev, 1)
        sqs = work[:, 0:1280].rearrange("p (t c) -> p t c", t=NT)
        dve_link(dve.tensor_tensor(sqs, pn[:, :, 0:320], pn[:, :, 0:320], ALU.mult))
        dve.tensor_reduce(stat[:, 0:4], sqs[:, :, 0:256], AX.X, ALU.add)
        dve_link(dve.tensor_reduce(stat[:, 4:8], sqs[:, :, 256:320], AX.X, ALU.add))
        dve.tensor_scalar(stat[:, 0:4], stat[:, 0:4], 1 / 256, EPS, ALU.mult, ALU.add)
        dve.tensor_scalar(stat[:, 4:8], stat[:, 4:8], 1 / 64, EPS, ALU.mult, ALU.add).then_inc(m1_sd, 1)
        dve.wait_ge(m1_sd, 2)
        dve_link(dve.reciprocal(stat[:, 0:8], stat[:, 0:8]))
        dve.tensor_tensor(pn[:, :, 0:256], pn[:, :, 0:256], stat[:, 0:4].unsqueeze(2).to_broadcast([P, NT, 256]),
                          ALU.mult).then_inc(cqn_set, 1)
        dve_link(dve.tensor_tensor(pn[:, :, 256:320], pn[:, :, 256:320],
                                   stat[:, 4:8].unsqueeze(2).to_broadcast([P, NT, 64]), ALU.mult))
        dve.wait_ge(m1_dma, 32)
        dve_link(dve.tensor_tensor(pn[:, :, 256:320], pn[:, :, 256:320], gk[:, :].unsqueeze(1).to_broadcast([P, NT, 64]), ALU.mult))
        for j, c0 in enumerate((256, 448)):
            src = pn[:, :, c0:c0 + 64].unsqueeze(2)
            dst = kd[:, :, j * P:j * P + 64].unsqueeze(2)
            dve_link(rotate(dve_link, src, dst, 0, 1))
            ins = dve.tensor_copy(kd[:, :, j * P + 64:(j + 1) * P], kd[:, :, j * P:j * P + 64])
        ins.then_inc(kd_set, 1)
        dve.wait_ge(wi_T, 1)
        dve.tensor_scalar(widx[:, :, :].rearrange("p t h -> p (t h)"), PS[:, 2, 0:32], 8 ** -0.5 * 64 ** -0.5, None, ALU.mult).then_inc(wi_ev, 1)
        dve.wait_ge(cq_hi_s, 1)
        for k in range(2):
            ins = dve.scalar_tensor_tensor(cq_lo[:, k, :], PS[:, k, :], gain(G_CQ, k), cq_hi[:, k, :].bitcast(F32),
                                           ALU.mult, ALU.subtract)
        ins.then_inc(cq_s, 1)
        dve.wait_ge(qa_sq, 1)
        dve_link(dve.tensor_reduce(stat[:, 8:40], work[:, 0:2048].rearrange("p (a b) -> p a b", b=64), AX.X, ALU.add))
        dve.tensor_scalar(stat[:, 8:40], stat[:, 8:40], 1 / 64, EPS, ALU.mult, ALU.add).then_inc(m1_sd, 1)
        dve.wait_ge(w_used, u1 + 6)
        dve.wait_ge(kd_T, 1)
        rv = rot.rearrange("p (t h d) -> p t h d", t=NT, d=64)
        rotate(dve_link, PS[:, 0:4, :].rearrange("p t (h d) -> p t h d", d=64), rv, 0, 8).then_inc(qi_set, 1)
        dve.wait_ge(qi_set, 1)
        dve.wait_ge(m1_sd, 4)
        dve_link(dve.reciprocal(stat[:, 8:40], stat[:, 8:40]))
        q4 = qn[:, :, :].rearrange("p t (h d) -> p t h d", d=64)
        rs = stat[:, 8:40].rearrange("p (t h) -> p t h", t=NT).unsqueeze(3).to_broadcast([P, NT, 8, 64])
        dve_link(dve.tensor_tensor(q4, q4, rs, ALU.mult))
        qf = qn[:, :, :].rearrange("p t (h d) -> p (t h) d", d=64)
        dve_link(dve.tensor_tensor(qf, qf, gq[:, :].unsqueeze(1).to_broadcast([P, 32, 64]), ALU.mult))
        rotate(dve_link, q4, rqa.rearrange("p (t h d) -> p t h d", t=NT, d=64), 0, 8).then_inc(qa_set, 1)

    um = U["merge1"]

    def merge1_sp(sp):
        w = A['w_in'][0]
        for n in range(2):
            u = um + 6 * n
            for c0, wo, d in ((2056, A['w_o_a'][0], 0), (3080, A['w_o_b'][0], 3)):
                panel(sp, u + d, w, 0, 4, c0 + 512 * n)
                panel(sp, u + d + 1, w, 4, 4, c0 + 512 * n)
                panel(sp, u + d + 2, wo, 0, 4, 512 * n)

    def merge1_pe(pe):
        for n in range(2):
            u = um + 6 * n
            for b, (yh, yl) in enumerate(((ya_hi, ya_lo), (yb_hi, yb_lo))):
                g = 2 * n + b
                v = u + 3 * b
                if g:
                    pe.wait_ge(g_sig, g)
                unit_T(pe, v, v % 2, 0, 0, 4, h_hi, h_lo, True, False)
                unit_T(pe, v + 1, (v + 1) % 2, 0, 4, 4, h_hi, h_lo, False, True)
                if g:
                    pe.wait_ge(g_mul, g)
                else:
                    pe.wait_ge(a_ylo, 8)
                unit_T(pe, v + 2, (v + 2) % 2, 4, 0, 4, yh, yl, True, True)

    def merge1_act(act):
        for n in range(2):
            for b in range(2):
                g = 2 * n + b
                v = um + 6 * n + 3 * b
                following = 2048 if g < 3 else 1024
                rounds(act, v + 2, 1)
                rounds(act, v + 3, 1, following)
                if g >= 2:
                    act.wait_ge(g_mul, g - 1)
                act.activation((gt, gt2)[b][:, :].rearrange("p (a c) -> p a c", a=4), PS[:, 0:4, :], ACT.Sigmoid).then_inc(g_sig, 1)
                rounds(act, v + 4, 1, following)
            act.wait_ge(g_mul, 2 * n + 2)
            act.wait_ge(mg_ready, 2 * n + 1)
            act.activation(mg_hi[:, 4 * n:4 * n + 4, :], mtmp.rearrange("p (a c) -> p a c", a=4), ACT.Copy).then_inc(g_hi, 1)

    def merge1_dve(dve):
        for n in range(2):
            for b in range(2):
                g = 2 * n + b
                v = um + 6 * n + 3 * b
                dve.wait_ge(g_sig, g + 1)
                dve.wait_ge(w_used, v + 3)
                if g == 2:
                    dve.wait_ge(mg_ready, 2)
                dst = (mtmp, gt2[:, :])[b].rearrange("p (a c) -> p a c", a=4)
                dve.tensor_tensor(dst, (gt, gt2)[b][:, :].rearrange("p (a c) -> p a c", a=4), PS[:, 4:8, :],
                                  ALU.mult).then_inc(g_mul, 1)
            dve.wait_ge(g_mul, 2 * n + 2)
            dve.tensor_tensor(mtmp, mtmp, gt2[:, :], ALU.add).then_inc(mg_ready, 1)
            dve.wait_ge(g_hi, n + 1)
            dve.tensor_tensor(mg_lo[:, 4 * n:4 * n + 4, :], mtmp.rearrange("p (a c) -> p a c", a=4),
                              mg_hi[:, 4 * n:4 * n + 4, :].bitcast(F32), ALU.subtract).then_inc(mg_ready, 1)

    def place(offset, name, shape, dt=F32):
        return at(name, shape, dt, offset=SCOPE + offset)

    KB = 1024
    rqT, rkT = place(0, "rqT", [P, 4, T]), place(8 * KB, "rkT", [P, 4, T])
    rv, rgT = place(16 * KB, "rv", [P, NT, D]), place(32 * KB, "rgT", [P, KD, T])
    yr_hi, yr_lo = place(48 * KB, "yr_hi", [P, KD, T], F32R), place(64 * KB, "yr_lo", [P, KD, T], F32R)
    wb_raw = place(64 * KB, "wb_raw", [P, KD, 16])
    wb_h, wb_l = place(64 * KB + 512, "wb_h", [P, KD, 16], F32R), place(65 * KB, "wb_l", [P, KD, 16], F32R)
    diff = place(80 * KB, "diff", [P, T])
    diffi = place(78 * KB, "diffi", [P, T], I32)
    level = {2 ** n: place(80 * KB + 512 * n, f"level{2 ** n}", [P, P]) for n in range(7)}
    level1T = place(80 * KB + 3584, "level1T", [P, P])
    upto = place(84 * KB, "upto", [P, P])
    before = place(84 * KB + 512, "before", [P, P])
    seen = place(85 * KB, "seen", [P, P])
    small = place(85 * KB + 512, "small", [P, 256 + 24])
    beta, gl, Gn, bG, kdf, dlast = (small[:, 32 * j:32 * j + 32].rearrange("p (c h) -> p c h", c=NT) for j in range(6))
    alog, dtb = small[:, 224:232], small[:, 232:240]
    ba = place(85 * KB + 512 + 280 * 4, "ba", [P, NT, 16])
    dec = work[:, 0:1024].rearrange("p (a b) -> p a b", a=2)
    sT = work[:, 1024:3584].rearrange("p (a b) -> p a b", a=2)
    ro = work[:, 3584:4096].rearrange("p (c v) -> p c v", c=NT)
    u2 = U["ret"]
    (r2_consts, r2_dma, rq_set, rq_T, rq_ev, rk_set, rk_T, rk_ev, rv_ev, wb_hi_s, wb_lo_s, ba_mm, ba_ev, rg_ev, r_sc, r_dec,
     r_sT, r_out, r_var, r_sd, r_on, r_T, r_y, r_hi, r_lo, p_sig, p_sp, p_exp, p_ln, p_g, p_G, p_Gn, p_eG, p_done, diff_set,
     lv_set) = (
        sem("r_" + s) for s in ("consts dma rq_set rq_T rq_ev rk_set rk_T rk_ev rv_ev wbh wbl ba_mm ba_ev rg_ev sc dec sT out var "
                                "sd on T y hi lo sig sp exp ln g G Gn eG done diff level").split())
    loggam = [float(np.log(np.float32(1) - np.float32(2.0) ** np.float32(-5 - h))) for h in range(8)]

    def ret_sp(sp):
        w = A['w_in_2'][0]
        for j, c0 in enumerate((0, 512, 1024, 1536, 2048, 2560)):
            panel(sp, u2 + 2 * j, w, 0, 4, c0)
            panel(sp, u2 + 2 * j + 1, w, 4, 4, c0)

    def block_mask(pool, m, b):
        q = P // (2 * b)
        v = m[:, :].rearrange("p (q r) -> p q r", q=q)[:, :, 0:b]
        pool_link(pool.memset(m[:, :], 0.0))
        pool_link(pool.memset(v, 1.0))
        pool_link(pool.affine_select(out=v, in_=v, compare_op=ALU.is_ge, fill=0.0, base=-b,
                                     pattern=[[-2 * b, q], [0, b]], channel_multiplier=1))
        return pool.affine_select(out=v, in_=v, compare_op=ALU.is_ge, fill=0.0, base=2 * b - 1,
                                  pattern=[[2 * b, q], [0, b]], channel_multiplier=-1)

    def ret_pool(pool):
        pool.wait_ge(x_ready, KD * 4)
        for m, op, pat, cm in ((upto, ALU.is_ge, 1, -1), (before, ALU.is_gt, -1, 1), (seen, ALU.is_ge, -1, 1)):
            pool_link(pool.memset(m[:, :], 1.0))
            pool_link(pool.affine_select(out=m[:, :], in_=m[:, :], compare_op=op, fill=0.0, base=0,
                                         pattern=[[pat, P]], channel_multiplier=cm))
        pool_link(pool.iota(diffi[:, :], pattern=[[1, T]], base=0, channel_multiplier=-1))
        pool_link(pool.tensor_copy(diff[:, :], diffi[:, :]))
        pool.affine_select(out=diff[:, 0:P], in_=diff[:, 0:P], compare_op=ALU.is_ge, fill=1e7, base=0,
                           pattern=[[1, P]], channel_multiplier=-1).then_inc(diff_set, 1)
        los(pool, u2 + 2, 2)
        pool.wait_ge(wb_hi_s, 1)
        pool.tensor_tensor(wb_l[:, :, :], wb_raw[:, :, :], wb_h[:, :, :].bitcast(F32), ALU.subtract).then_inc(wb_lo_s, 1)
        los(pool, u2 + 4, 8)
        los(pool, U["merge2a"], 2)
        pool.wait_ge(r_dec, 8)
        for b in (2, 4, 8, 16, 32, 64):
            pool_link(block_mask(pool, level[b], b))
        for m, base in ((level[1], -1), (level1T, 0)):
            pool_link(pool.memset(m[:, :], 0.0))
            v = m[:, :].rearrange("p (q r) -> p q r", r=2)[:, :, (0 if base else 1):(1 if base else 2)]
            ins = pool.affine_select(out=v, in_=v, compare_op=ALU.not_equal, fill=1.0, base=base,
                                     pattern=[[-2, P // 2], [0, 1]], channel_multiplier=1)
            pool_link(ins)
        pool.memset(small[:, 240:241], 0.0).then_inc(lv_set, 1)
        los(pool, U["merge2a"] + 2, 6)

    baT = work[0:16, 2048:2560]
    ba_cp, ba_T = sem("ba_copied"), sem("ba_turned")

    def ret_pe(pe):
        unit_N(pe, u2, 0, 0, 4, h_hi, h_lo, True, False, (h_ready, KD * 3))
        unit_N(pe, u2 + 1, 0, 4, 4, h_hi, h_lo, False, True, (h_ready, KD * 3))
        unit_N(pe, u2 + 2, 4, 0, 4, h_hi, h_lo, True, False)
        unit_N(pe, u2 + 3, 4, 4, 4, h_hi, h_lo, False, True)

        def turn_over(have, bank, done):
            pe.wait_ge(have, 1)
            for k in range(4):
                for t in range(NT):
                    ins = pe.transpose(PS[:, bank + k, t * P:(t + 1) * P], rot[:, t * 512 + k * P:t * 512 + (k + 1) * P], ident[:, :])
            ins.then_inc(done, 1)

        turn_over(rq_set, 0, rq_T)
        pe.wait_ge(rq_ev, 1)
        unit_N(pe, u2 + 4, 0, 0, 4, h_hi, h_lo, True, False)
        unit_N(pe, u2 + 5, 0, 4, 4, h_hi, h_lo, False, True)
        turn_over(rk_set, 4, rk_T)
        pe.wait_ge(rk_ev, 1)
        unit_N(pe, u2 + 6, 4, 0, 4, h_hi, h_lo, True, False)
        unit_N(pe, u2 + 7, 4, 4, 4, h_hi, h_lo, False, True)
        pe.wait_ge(wb_lo_s, 1)
        pe.wait_ge(rv_ev, 1)
        narrow_product(wb_h, wb_l, PS[0:16, 0, :]).then_inc(ba_mm, 1)
        pe.wait_ge(ba_cp, 1)
        for t in range(NT):
            ins = pe.transpose(PS[:, 1, 16 * t:16 * t + 16], baT[:, t * P:(t + 1) * P], ident[0:16, 0:16])
        ins.then_inc(ba_T, 1)
        pe.wait_ge(ba_ev, 1)
        unit_T(pe, u2 + 8, 0, 0, 0, 4, h_hi, h_lo, True, False)
        unit_T(pe, u2 + 9, 1, 0, 4, 4, h_hi, h_lo, False, True)
        pe.wait_ge(rv_ev, 2)
        unit_T(pe, u2 + 10, 0, 4, 0, 4, h_hi, h_lo, True, False)
        unit_T(pe, u2 + 11, 1, 4, 4, 4, h_hi, h_lo, False, True)
        pe.wait_ge(rg_ev, 2)
        ret_scores(pe, 0)
        pe.wait_ge(p_g, 1)
        nc.tensor.matmul(PS[:, 7, 0:32], upto[:, :], small[:, 32:64], start=True, stop=True)
        nc.tensor.matmul(PS[:, 7, 32:64], ones[:, :], small[:, 32:64], start=True, stop=True).then_inc(p_G, 1)
        pe.wait_ge(p_Gn, 1)
        for h in range(8):
            if h:
                ret_turn(pe, h - 1)
            pe.wait_ge(r_sT, h + 1)
            for i in range(NT):
                for j in range(i + 1):
                    c = off[j] + (i - j) * P
                    ins = nc.tensor.matmul(PS[:, 6, i * P:(i + 1) * P], sT[:, h % 2, c:c + P],
                                           rv[:, j, h * P:(h + 1) * P], start=j == 0, stop=j == i)
            ins.then_inc(r_out, 1)
            if h < 7:
                ret_scores(pe, h + 1)
        ret_turn(pe, 7)

    def ret_scores(pe, h):
        r, z = PER * (h % 2), scores_of(h)
        for j in range(NT):
            ins = nc.tensor.matmul(z[:, off[j]:off[j] + wid[j]], rkT[r:r + PER, h // 2, j * P:(j + 1) * P],
                                   rqT[r:r + PER, h // 2, j * P:T], start=True, stop=True)
        ins.then_inc(r_sc, 1)

    def ret_turn(pe, h):
        pe.wait_ge(r_on, h + 1)
        if h >= 1:
            pe.wait_ge(r_y, h)
        for i in range(NT):
            ins = pe.transpose(PS[:, 7, i * P:(i + 1) * P], ro[:, i, :], ident[:, :])
        ins.then_inc(r_T, 1)

    def ret_act(act):
        act.wait_ge(x_ready, KD * 4)
        act.dma_start(wb_raw[:, :, :], A['w_in_2'][0, :, 7168:7184].rearrange("(k p) c -> p k c", p=P)).then_inc(r2_dma, 16)
        act.dma_start(alog, A['dn_a_log_2'][0].partition_broadcast(P)).then_inc(r2_dma, 16)
        act.dma_start(dtb, A['dn_dt_bias_2'][0].partition_broadcast(P)).then_inc(r2_dma, 16)
        rounds(act, u2 + 2, 2)
        act.wait_ge(r2_dma, 48)
        act.activation(wb_h[:, :, :], wb_raw[:, :, :], ACT.Copy).then_inc(wb_hi_s, 1)
        rounds(act, u2 + 4, 2)
        act.wait_ge(rq_T, 1)
        act.activation(rqT[:, :, :], PS[:, 0:4, :], ACT.Copy).then_inc(rq_ev, 1)
        rounds(act, u2 + 6, 2)
        act.wait_ge(rk_T, 1)
        act.activation(rkT[:, :, :], PS[:, 4:8, :], ACT.Copy, scale=PER ** -0.5).then_inc(rk_ev, 1)
        rounds(act, u2 + 8, 1)
        act.wait_ge(w_used, u2 + 6)
        act.activation(rv[:, :, 0:512], PS[:, 0:4, :], ACT.Copy).then_inc(rv_ev, 1)
        rounds(act, u2 + 9, 1)
        act.wait_ge(w_used, u2 + 8)
        act.activation(rv[:, :, 512:1024], PS[:, 4:8, :], ACT.Copy).then_inc(rv_ev, 1)
        rounds(act, u2 + 10, 2)
        act.wait_ge(ba_ev, 1)
        act.activation(beta, ba[:, :, 0:8], ACT.Sigmoid).then_inc(p_sig, 1)
        act.wait_ge(p_sp, 1)
        act_link(act.activation(kdf, Gn, ACT.Abs))
        act_link(act.activation(kdf, kdf, ACT.Exp, scale=-1.0))
        act.activation(kdf, kdf, ACT.Ln, bias=one_c[:, :])
        act.activation(alog, alog, ACT.Exp).then_inc(p_ln, 1)
        act.wait_ge(w_used, u2 + 10)
        act.activation(rgT[:, 0:4, :], PS[:, 0:4, :], ACT.Silu).then_inc(rg_ev, 1)
        act.wait_ge(w_used, u2 + 12)
        act.activation(rgT[:, 4:8, :], PS[:, 4:8, :], ACT.Silu).then_inc(rg_ev, 1)
        act.wait_ge(diff_set, 1)
        act.activation(dec[:, 0, :], diff[:, :], ACT.Exp, scale=loggam[0]).then_inc(r_dec, 1)
        act.wait_ge(p_Gn, 1)
        act.activation(bG, Gn, ACT.Exp)
        act.activation(dlast, dlast, ACT.Exp)
        act.activation(kdf, kdf, ACT.Exp).then_inc(p_eG, 1)
        rounds(act, U["merge2a"], 2)
        for h in range(8):
            if h:
                ret_hi(act, h - 1)
            act.wait_ge(r_var, h + 1)
            act.activation(stat[:, 32:36], stat[:, 32:36], ACT.Sqrt).then_inc(r_sd, 1)
            if h < 7:
                act.activation(dec[:, (h + 1) % 2, :], diff[:, :], ACT.Exp, scale=loggam[h + 1]).then_inc(r_dec, 1)
        ret_hi(act, 7)

    def ret_hi(act, h):
        act.wait_ge(r_y, h + 1)
        act.activation(yr_hi[:, h, :], ro[:, :, :].rearrange("p c v -> p (c v)"), ACT.Copy).then_inc(r_hi, 1)

    def ret_dve(dve):
        rv4 = rot.rearrange("p (t h d) -> p t h d", t=NT, d=64)
        dve.wait_ge(w_used, u2 + 2)
        rotate(dve_link, PS[:, 0:4, :].rearrange("p t (h d) -> p t h d", d=64), rv4, NT, 8).then_inc(rq_set, 1)
        dve.wait_ge(w_used, u2 + 4)
        dve.wait_ge(rq_T, 1)
        rotate(dve_link, PS[:, 4:8, :].rearrange("p t (h d) -> p t h d", d=64), rv4, NT, 8).then_inc(rk_set, 1)
        dve.wait_ge(ba_mm, 1)
        dve.wait_ge(rk_T, 1)
        dve.tensor_copy(baT, PS[0:16, 0, :]).then_inc(ba_cp, 1)
        dve.wait_ge(ba_T, 1)
        dve.tensor_copy(ba[:, :, :].rearrange("p t h -> p (t h)"), PS[:, 1, 0:64]).then_inc(ba_ev, 1)
        dve.wait_ge(r2_dma, 48)
        dve.wait_ge(ba_ev, 1)
        dve.tensor_tensor(Gn, ba[:, :, 8:16], dtb.unsqueeze(1).to_broadcast([P, NT, 8]), ALU.add).then_inc(p_sp, 1)
        dve.wait_ge(p_ln, 1)
        dve_link(dve.scalar_tensor_tensor(gl, Gn, 0.0, kdf, ALU.max, ALU.add))
        dve.scalar_tensor_tensor(gl, gl, -1.0, alog.unsqueeze(1).to_broadcast([P, NT, 8]), ALU.mult, ALU.mult).then_inc(p_g, 1)
        dve.wait_ge(p_G, 1)
        dve_link(dve.tensor_copy(small[:, 64:96], PS[:, 7, 0:32]))
        dve.tensor_copy(small[:, 160:192], PS[:, 7, 32:64])
        dve_link(dve.tensor_tensor(small[:, 128:160], PS[:, 7, 32:64], small[:, 64:96], ALU.subtract))
        dve.tensor_scalar(small[:, 128:160], small[:, 128:160], 0.0, None, ALU.min).then_inc(p_Gn, 1)
        dve.wait_ge(p_eG, 1)
        dve.wait_ge(p_sig, 1)
        dve.tensor_tensor(bG, bG, beta, ALU.mult).then_inc(p_done, 1)
        st6 = rstat[:, 0:24].rearrange("p (c s) -> p c s", c=NT)
        mv = rstat[:, 24:32].rearrange("p (c s) -> p c s", c=NT)
        for h in range(8):
            dve.wait_ge(r_sc, h + 1)
            dve.wait_ge(r_dec, h + 1)
            if h >= 2:
                dve.wait_ge(r_out, h - 1)
            z = scores_of(h)
            for j in range(NT):
                c = slice(off[j], off[j] + wid[j])
                ins = dve.tensor_tensor(sT[:, h % 2, c], z[:, c], dec[:, h % 2, 0:wid[j]], ALU.mult)
            ins.then_inc(r_sT, 1)
            if h:
                ret_gate(dve, h - 1)
            dve.wait_ge(r_out, h + 1)
            for c in range(NT):
                ins = dve.bn_stats(st6[:, c, :], PS[:, 6, c * P:(c + 1) * P])
            dve_link(ins)
            for c in range(NT):
                ins = dve.bn_aggr(mv[:, c, :], st6[:, c, :])
            dve_link(ins)
            dve.tensor_scalar(stat[:, 32:36], mv[:, :, 1:2].rearrange("p c s -> p (c s)"), GN_EPS, None, ALU.add).then_inc(r_var, 1)
            dve.wait_ge(r_sd, h + 1)
            dve_link(dve.reciprocal(stat[:, 32:36], stat[:, 32:36]))
            if h:
                dve.wait_ge(r_lo, h)
            for c in range(NT):
                ins = dve.tensor_scalar(ro[:, c, :], PS[:, 6, c * P:(c + 1) * P], mv[:, c, 0:1], stat[:, 32 + c:33 + c],
                                        ALU.subtract, ALU.mult)
            ins.then_inc(r_on, 1)
        ret_gate(dve, 7)

    def ret_gate(dve, h):
        dve.wait_ge(r_T, h + 1)
        rf = ro[:, :, :].rearrange("p c v -> p (c v)")
        dve.scalar_tensor_tensor(rf, PS[:, 7, :], gain(G_RET, h), rgT[:, h, :], ALU.mult, ALU.mult).then_inc(r_y, 1)
        dve.wait_ge(r_hi, h + 1)
        dve.tensor_tensor(yr_lo[:, h, :], rf, yr_hi[:, h, :].bitcast(F32), ALU.subtract).then_inc(r_lo, 1)

    M1 = place(0, "M1", [P, KD, T])
    do_hi, do_lo = place(16 * KB, "do_hi", [P, KD, T], F32R), place(32 * KB, "do_lo", [P, KD, T], F32R)
    mh2, ml2 = place(48 * KB, "mh2", [P, KD, T], F32R), place(64 * KB, "ml2", [P, KD, T], F32R)
    br_sig, br_mul, br_hi, br_ready = (sem("br_" + s) for s in "sig mul hi ready".split())
    gbuf = work[:, 0:2048]
    gbuf4 = gbuf.rearrange("p (a c) -> p a c", a=4)

    def branch_sp(sp, stage, gate0, w):
        u = U[stage]
        for n in range(2):
            panel(sp, u + 4 * n, A['w_in_2'][0], 0, 4, gate0 + 512 * n)
            panel(sp, u + 4 * n + 1, A['w_in_2'][0], 4, 4, gate0 + 512 * n)
            panel(sp, u + 4 * n + 2, w, 0, 4, 512 * n)
            panel(sp, u + 4 * n + 3, w, 4, 4, 512 * n)

    def branch_pe(pe, stage, b, yh, yl, ready):
        u = U[stage]
        for n in range(2):
            g = 2 * b + n
            if g % 2:
                pe.wait_ge(br_sig, g)
            if g != 2:
                unit_T(pe, u + 4 * n, 0, 0, 0, 4, h_hi, h_lo, True, False)
                unit_T(pe, u + 4 * n + 1, 1, 0, 4, 4, h_hi, h_lo, False, True)
            if g:
                pe.wait_ge(br_mul, g)
            pe.wait_ge(*ready)
            unit_T(pe, u + 4 * n + 2, 0, 4, 0, 4, yh, yl, True, False)
            unit_T(pe, u + 4 * n + 3, 1, 4, 4, 4, yh, yl, False, True)

    def branch_act(act, stage, b):
        u = U[stage]
        for n in range(2):
            g = 2 * b + n
            if g == 0:
                rounds(act, u + 2, 2)
            act.wait_ge(w_used, u + 4 * n + 2)
            if g == 1:
                act.wait_ge(br_mul, 1)
            if g == 3:
                act.wait_ge(br_ready, 2)
            act.activation(gbuf4, PS[:, 0:4, :], ACT.Sigmoid).then_inc(br_sig, 1)
            if n == 0:
                rounds(act, u + 4, 4)
            if n and b:
                rounds(act, u + 8, 2, 1024)
            if b:
                act.wait_ge(br_ready, 2 * n + 1)
                act.activation(mh2[:, 4 * n:4 * n + 4, :], gbuf4, ACT.Copy).then_inc(br_hi, 1)

    def branch_dve(dve, stage, b):
        u = U[stage]
        for n in range(2):
            g = 2 * b + n
            dve.wait_ge(br_sig, g + 1)
            dve.wait_ge(w_used, u + 4 * n + 4)
            if b == 0:
                dve.tensor_tensor(M1[:, 4 * n:4 * n + 4, :], gbuf4, PS[:, 4:8, :], ALU.mult).then_inc(br_mul, 1)
            else:
                dve.tensor_tensor(gbuf4, gbuf4, PS[:, 4:8, :], ALU.mult).then_inc(br_mul, 1)
                dve.wait_ge(br_mul, g + 1)
                dve.tensor_tensor(gbuf4, gbuf4, M1[:, 4 * n:4 * n + 4, :], ALU.add).then_inc(br_ready, 1)
                dve.wait_ge(br_hi, n + 1)
                dve.tensor_tensor(ml2[:, 4 * n:4 * n + 4, :], gbuf4, mh2[:, 4 * n:4 * n + 4, :].bitcast(F32),
                                  ALU.subtract).then_inc(br_ready, 1)

    dz = place(32 * KB, "dz", [P, KD, T])
    cv = place(48 * KB, "cv", [P, 6, T])
    wkb, wkd, wvb, wAT, waT = (place((60 + 4 * j) * KB, "w_" + n, [P, 2, T]) for j, n in enumerate(("kb", "kd", "vb", "AT", "aT")))
    wE, wX, wT, wU = (work[:, 1024 * j:1024 * (j + 1)].rearrange("p (e t) -> p e t", e=2) for j in range(4))
    cin = work[:, 0:3072].rearrange("p (a b) -> p a b", a=6)
    ssq = rstat[:, 0:16]
    Sst = place(87 * KB, "Sst", [P, 2, P])
    ud = U["dn"]
    POINTS = {
        "pe": "qkT qT2 Grow kk ATt vT u o oT".split(),
        "act": "cinA silA sq2 sd cinB cvq eR silB eE AT uev osq osd ohi".split(),
        "dve": "cvA ss qn cvB eD A attn T0 vb oss on oy olo".split(),
    }
    passed = {e: sem("dn_" + e) for e in POINTS}
    d_scaled = sem("dn_scaled")
    d_X, d_Xm, d_TU, d_Um, d_wS, d_vn, d_kv, d_S = (sem("dn_" + x) for x in "X Xm TU Um wS vn kv S".split())

    def await_point(eng, who, pp, name):
        eng.wait_ge(passed[who], len(POINTS[who]) * pp + POINTS[who].index(name) + 1)

    def at_point(ins, who):
        ins.then_inc(passed[who], 1)

    def per_head(arr, pp):
        return arr[:, :, 2 * pp:2 * pp + 2].rearrange("p c h -> p h c").unsqueeze(3).to_broadcast([P, 2, NT, P])

    def chunks(x):
        return x.rearrange("p e (c j) -> p e c j", c=NT)

    def everywhere(m):
        return m[:, :].unsqueeze(1).to_broadcast([P, 2 * NT, P])

    def tiles(x):
        return x.rearrange("p e (c j) -> p (e c) j", c=NT)

    def tile_of(x, e, c):
        return x[:, e, c * P:(c + 1) * P]

    LEVELS = (2, 4, 8, 16, 32, 64)

    def delta_sp(sp):
        w = A['w_in_2'][0]
        for pp in range(4):
            for j, cols in enumerate(((3072, 4096), (5120, 6144))):
                for s in range(2):
                    dst = raw[:, s, :].rearrange("p (k c) -> p k c", k=4)
                    pieces = []
                    for a, c0 in enumerate(cols):
                        c = c0 + HALF * pp
                        src = w[s * 512:(s + 1) * 512, c:c + HALF].rearrange("(k p) c -> p k c", p=P)
                        pieces.append((dst[:, :, a * HALF:(a + 1) * HALF], src))
                    load(sp, ud + 4 * pp + 2 * j + s, s, pieces)

    def halves(x, b):
        v = x.rearrange("p (g r) -> p g r", r=2 * b)
        return v[:, :, 0:b], v[:, :, b:2 * b]

    def delta_pe(pe):
        mm = nc.tensor.matmul
        for pp in range(4):
            u = ud + 4 * pp
            if pp:
                await_point(pe, "dve", pp - 1, "oy")
            else:
                pe.wait_ge(br_sig, 2)
                pe.wait_ge(br_mul, 2)
                unit_T(pe, u, 0, 0, 0, 4, h_hi, h_lo, True, False)
                unit_T(pe, u + 1, 1, 0, 4, 4, h_hi, h_lo, False, True)
            unit_T(pe, u + 2, 0, 4, 0, 4, h_hi, h_lo, True, False)
            await_point(pe, "act", pp, "silA")
            for a in range(4):
                for c in range(NT):
                    ins = pe.transpose(tile_of(PS, a, c), tile_of(cv, a, c), ident[:, :])
            at_point(ins, "pe")
            unit_T(pe, u + 3, 1, 4, 4, 4, h_hi, h_lo, False, True)
            await_point(pe, "dve", pp, "qn")
            for a, src in ((0, wE), (2, wkd)):
                for e in range(2):
                    for c in range(NT):
                        ins = pe.transpose(tile_of(PS, a + e, c), tile_of(src, e, c), ident[:, :])
            at_point(ins, "pe")
            await_point(pe, "act", pp, "cinB")
            for e in range(2):
                for c in range(NT):
                    g = small[:, 32 + 8 * c + 2 * pp + e:33 + 8 * c + 2 * pp + e]
                    ins = mm(tile_of(PS, 4 + e, c), g.to_broadcast([P, P]), upto[:, :], start=True, stop=True)
            at_point(ins, "pe")
            await_point(pe, "act", pp, "cvq")
            for e in range(2):
                for c in range(NT):
                    k = tile_of(cv, 2 + e, c)
                    mm(tile_of(PS, 6 + e, c), k, k, start=True, stop=True)
                    ins = mm(tile_of(PS, e, c), tile_of(cv, e, c), k, start=True, stop=True)
            at_point(ins, "pe")
            for who, bank, src in (("A", 2, wU), ("attn", 4, wX)):
                await_point(pe, "dve", pp, who)
                for e in range(2):
                    for c in range(NT):
                        ins = pe.transpose(tile_of(PS, bank + e, c), tile_of(src, e, c), ident[:, :])
            at_point(ins, "pe")
            await_point(pe, "act", pp, "silB")
            for e in range(2):
                for c in range(NT):
                    ins = pe.transpose(tile_of(PS, 6 + e, c), tile_of(cv, 4 + e, c), ident[:, :])
            at_point(ins, "pe")
            await_point(pe, "dve", pp, "T0")
            for l, b in enumerate(LEVELS):
                n = 2 * (len(LEVELS) * pp + l)
                for e in range(2):
                    if l:
                        pe.wait_ge(d_Um, n - 2 + e + 1)
                    for c in range(NT):
                        ins = mm(tile_of(PS, 4 + e, c), tile_of(wAT, e, c), tile_of(wT, e, c), start=True, stop=True)
                    ins.then_inc(d_X, 1)
                next_panel(pe, u + 4, l)
                for e in range(2):
                    pe.wait_ge(d_Xm, n + e + 1)
                    for c in range(NT):
                        lo, hi = c * 64, (c + 1) * 64
                        if b < 64:
                            mm(PS[:, 6 + e, lo:hi], tile_of(wU, e, c), halves(tile_of(wX, e, c), b)[0], start=True, stop=True)
                        ins = mm(PS[:, 6 + e, 256 + lo:256 + hi], tile_of(wX, e, c), halves(tile_of(wU, e, c), b)[1],
                                 start=True, stop=True)
                    ins.then_inc(d_TU, 1)
            next_panel(pe, u + 4, 6)
            pe.wait_ge(d_Um, 2 * len(LEVELS) * (pp + 1))
            pe.wait_ge(d_scaled, 3 * (pp + 1))
            for e in range(2):
                for c in range(NT):
                    mm(tile_of(PS, 4 + e, c), tile_of(wU, e, c), tile_of(wvb, e, c), start=True, stop=True)
                    ins = mm(tile_of(PS, 6 + e, c), tile_of(wkb, e, c), tile_of(wU, e, c), start=True, stop=True)
            at_point(ins, "pe")
            next_panel(pe, u + 4, 7)
            await_point(pe, "act", pp, "uev")
            for c in range(NT):
                if c:
                    for e in range(2):
                        pe.wait_ge(d_S, 2 * (3 * pp + c - 1) + e + 1)
                        mm(PS[:, 6 + e, 0:P], tile_of(wAT, e, c), Sst[:, e, :], start=True, stop=True).then_inc(d_wS, 1)
                for e in range(2):
                    if c:
                        mm(tile_of(PS, 4 + e, c), tile_of(cv, e, c), Sst[:, e, :], start=True, stop=False)
                        pe.wait_ge(d_vn, 2 * (3 * pp + c - 1) + e + 1)
                    if c < NT - 1:
                        mm(PS[:, 6 + e, P:2 * P], tile_of(wkd, e, c), tile_of(wX, e, c), start=True, stop=True).then_inc(d_kv, 1)
                    ins = mm(tile_of(PS, 4 + e, c), tile_of(waT, e, c), tile_of(wX, e, c), start=c == 0, stop=True)
            at_point(ins, "pe")
            await_point(pe, "dve", pp, "on")
            for e in range(2):
                for c in range(NT):
                    ins = pe.transpose(tile_of(PS, 6 + e, c), tile_of(wT, e, c), ident[:, :])
            at_point(ins, "pe")

    def next_panel(pe, u, k):
        s = k // 4
        if k % 4 == 0:
            pe.wait_ge(w_lo, u + s + 1)
        for m in range(4):
            c0 = (k % 4) * 512 + m * P
            ins = mm3(PS[:, m, :], wh[:, s, c0:c0 + P], wl[:, s, c0:c0 + P], h_hi[:, k, :], h_lo[:, k, :], k == 0, k == KD - 1)
        if k % 4 == 3:
            ins.then_inc(w_used, 1)

    def delta_pool(pool):
        los(pool, ud, 4)
        for pp in range(4):
            await_point(pool, "pe", pp, "qT2")
            pool.tensor_tensor(chunks(wkb[:, :, :]), chunks(wkd[:, :, :]), per_head(bG, pp), ALU.mult).then_inc(d_scaled, 1)
            pool.wait_ge(d_scaled, 3 * pp + 1)
            pool.tensor_tensor(chunks(wkd[:, :, :]), chunks(wkd[:, :, :]), per_head(kdf, pp), ALU.mult).then_inc(d_scaled, 1)
            await_point(pool, "act", pp, "eR")
            await_point(pool, "pe", pp, "kk")
            pool.tensor_tensor(cv[:, 0:2, :], cv[:, 0:2, :], wX, ALU.mult).then_inc(d_scaled, 1)
            los(pool, ud + 4 * pp + 4, 4)

    def delta_act(act):
        for pp in range(4):
            u = ud + 4 * pp
            if pp == 0:
                rounds(act, u + 2, 2)
            act.wait_ge(w_used, u + 2)
            if pp:
                await_point(act, "dve", pp - 1, "oy")
            at_point(act.activation(cin[:, 0:4, :], PS[:, 0:4, :], ACT.Copy), "act")
            await_point(act, "dve", pp, "cvA")
            at_point(act.activation(cv[:, 0:4, :], cv[:, 0:4, :], ACT.Silu), "act")
            await_point(act, "pe", pp, "qkT")
            act.activation(wE, PS[:, 0:2, :], ACT.Square)
            at_point(act.activation(wX, PS[:, 2:4, :], ACT.Square), "act")
            await_point(act, "dve", pp, "ss")
            at_point(act.activation(ssq, ssq, ACT.Sqrt), "act")
            act.wait_ge(w_used, u + 4)
            act.activation(dz[:, 2 * pp:2 * pp + 2, :], PS[:, 6:8, :], ACT.Silu)
            at_point(act.activation(cin[:, 4:6, :], PS[:, 4:6, :], ACT.Copy), "act")
            await_point(act, "pe", pp, "qT2")
            at_point(act.activation(cv[:, 0:4, :], PS[:, 0:4, :], ACT.Copy), "act")
            await_point(act, "pe", pp, "Grow")
            at_point(act.activation(wX, PS[:, 4:6, :], ACT.Exp), "act")
            await_point(act, "dve", pp, "cvB")
            at_point(act.activation(cv[:, 4:6, :], cv[:, 4:6, :], ACT.Silu), "act")
            rounds(act, u + 4, 2)
            await_point(act, "dve", pp, "eD")
            at_point(act.activation(wE, wE, ACT.Exp, scale=-1.0), "act")
            await_point(act, "pe", pp, "ATt")
            act.activation(wAT[:, :, :], PS[:, 2:4, :], ACT.Copy)
            at_point(act.activation(waT[:, :, :], PS[:, 4:6, :], ACT.Copy), "act")
            rounds(act, u + 6, 1)
            await_point(act, "pe", pp, "u")
            act.activation(wX, PS[:, 4:6, :], ACT.Copy)
            at_point(act.activation(wAT[:, :, :], PS[:, 6:8, :], ACT.Copy), "act")
            rounds(act, u + 7, 1)
            await_point(act, "pe", pp, "o")
            at_point(act.activation(wE, PS[:, 4:6, :], ACT.Square), "act")
            await_point(act, "dve", pp, "oss")
            at_point(act.activation(ssq[:, 0:8], ssq[:, 0:8], ACT.Sqrt), "act")
            await_point(act, "dve", pp, "oy")
            at_point(act.activation(do_hi[:, 2 * pp:2 * pp + 2, :], wU, ACT.Copy), "act")

    def conv(dve, pp, lo, hi, have):
        await_point(dve, "act", pp, have)
        for back in range(4):
            for a in range(lo, hi):
                c = 8 * (a // 2) + 2 * pp + a % 2
                tap = vecs[:, 1, 24 * (3 - back) + c:24 * (3 - back) + c + 1]
                if back == 0:
                    ins = dve.tensor_scalar(cv[:, a, :], cin[:, a, :], tap, None, ALU.mult)
                else:
                    ins = dve.scalar_tensor_tensor(cv[:, a, back:T], cin[:, a, 0:T - back], tap, cv[:, a, back:T],
                                                   ALU.mult, ALU.add)
            if back < 3:
                dve_link(ins)
        at_point(ins, "dve")

    def delta_dve(dve):
        tt = nc.vector.tensor_tensor
        for pp in range(4):
            conv(dve, pp, 0, 4, "cinA")
            await_point(dve, "act", pp, "sq2")
            dve.tensor_reduce(ssq[:, 0:8], chunks(wE), AX.X, ALU.add)
            dve_link(dve.tensor_reduce(ssq[:, 8:16], chunks(wX), AX.X, ALU.add))
            at_point(dve.tensor_scalar(ssq, ssq, EPS, None, ALU.add), "dve")
            await_point(dve, "act", pp, "sd")
            dve_link(dve.reciprocal(ssq, ssq))
            dve_link(dve.tensor_scalar(ssq[:, 0:8], ssq[:, 0:8], 128 ** -0.5, None, ALU.mult))
            scale = ssq.rearrange("p (a e c) -> p a e c", a=2, e=2)
            tt(chunks(wkd[:, :, :]), chunks(PS[:, 2:4, :]), scale[:, 1].unsqueeze(3).to_broadcast([P, 2, NT, P]), ALU.mult)
            ins = tt(chunks(wE), chunks(PS[:, 0:2, :]), scale[:, 0].unsqueeze(3).to_broadcast([P, 2, NT, P]), ALU.mult)
            at_point(ins, "dve")
            conv(dve, pp, 4, 6, "cinB")
            await_point(dve, "act", pp, "eR")
            dve_link(tt(chunks(wE), chunks(PS[:, 4:6, :]), per_head(Gn, pp), ALU.subtract))
            at_point(dve.tensor_scalar(wE, wE, 0.0, None, ALU.max), "dve")
            await_point(dve, "pe", pp, "kk")
            await_point(dve, "act", pp, "eE")
            dve_link(tt(tiles(wT), tiles(wE), everywhere(before), ALU.mult))
            dve_link(tt(wT, PS[:, 6:8, :], wT, ALU.mult))
            at_point(tt(chunks(wU), chunks(wT), per_head(beta, pp), ALU.mult), "dve")
            dve_link(tt(tiles(wE), tiles(wE), everywhere(seen), ALU.mult))
            dve.wait_ge(d_scaled, 3 * (pp + 1))
            at_point(tt(wX, PS[:, 0:2, :], wE, ALU.mult), "dve")
            dve_link(tt(tiles(wT), tiles(wU), everywhere(level[1]), ALU.mult))
            dve_link(dve.scalar_tensor_tensor(tiles(wT), tiles(wT), -1.0, everywhere(ident), ALU.mult, ALU.add))
            await_point(dve, "act", pp, "AT")
            dve_link(tt(tiles(wU), tiles(wAT[:, :, :]), everywhere(level1T), ALU.mult))
            at_point(dve.scalar_tensor_tensor(tiles(wU), tiles(wU), -1.0, everywhere(ident), ALU.mult, ALU.add), "dve")
            await_point(dve, "pe", pp, "vT")
            at_point(tt(chunks(wvb[:, :, :]), chunks(PS[:, 6:8, :]), per_head(beta, pp), ALU.mult), "dve")
            for l, b in enumerate(LEVELS):
                n = 2 * (len(LEVELS) * pp + l)
                for e in range(2):
                    dve.wait_ge(d_X, n + e + 1)
                    mask = level[b][:, :].unsqueeze(1).to_broadcast([P, NT, P])
                    tt(wX[:, e, :].rearrange("p (c j) -> p c j", c=NT), PS[:, 4 + e, :].rearrange("p (c j) -> p c j", c=NT), mask,
                       ALU.mult).then_inc(d_Xm, 1)
                for e in range(2):
                    dve.wait_ge(d_TU, n + e + 1)
                    first, second = halves(wT[:, e, :], b)[0], halves(wU[:, e, :], b)[1]
                    if b < 64:
                        tt(first, first, PS[:, 6 + e, 0:256].rearrange("p (g r) -> p g r", r=b), ALU.subtract)
                    tt(second, second, PS[:, 6 + e, 256:512].rearrange("p (g r) -> p g r", r=b), ALU.subtract).then_inc(d_Um, 1)
            for c in range(NT):
                if c:
                    for e in range(2):
                        dve.wait_ge(d_wS, 2 * (3 * pp + c - 1) + e + 1)
                        tt(tile_of(wX, e, c), tile_of(wX, e, c), PS[:, 6 + e, 0:P], ALU.subtract).then_inc(d_vn, 1)
                if c < NT - 1:
                    for e in range(2):
                        dve.wait_ge(d_kv, 2 * (3 * pp + c) + e + 1)
                        if c == 0:
                            ins = dve.tensor_copy(Sst[:, e, :], PS[:, 6 + e, P:2 * P])
                        else:
                            h = 2 * pp + e
                            ins = dve.scalar_tensor_tensor(Sst[:, e, :], Sst[:, e, :], dlast[:, c, h:h + 1], PS[:, 6 + e, P:2 * P],
                                                           ALU.mult, ALU.add)
                        ins.then_inc(d_S, 1)
            await_point(dve, "act", pp, "osq")
            dve_link(dve.tensor_reduce(ssq[:, 0:8], chunks(wE), AX.X, ALU.add))
            at_point(dve.tensor_scalar(ssq[:, 0:8], ssq[:, 0:8], 1 / P, EPS, ALU.mult, ALU.add), "dve")
            await_point(dve, "act", pp, "osd")
            dve_link(dve.reciprocal(ssq[:, 0:8], ssq[:, 0:8]))
            rs = ssq[:, 0:8].rearrange("p (e c) -> p e c", e=2).unsqueeze(3).to_broadcast([P, 2, NT, P])
            at_point(tt(chunks(wT), chunks(PS[:, 4:6, :]), rs, ALU.mult), "dve")
            await_point(dve, "pe", pp, "oT")
            at_point(dve.scalar_tensor_tensor(wU, PS[:, 6:8, :], gain(G_DN, 0), dz[:, 2 * pp:2 * pp + 2, :], ALU.mult, ALU.mult),
                     "dve")
            await_point(dve, "act", pp, "ohi")
            at_point(tt(do_lo[:, 2 * pp:2 * pp + 2, :], wU, do_hi[:, 2 * pp:2 * pp + 2, :].bitcast(F32), ALU.subtract), "dve")

    outn = at("outn", [P, NT, D], offset=SCOPE)
    f_T, f_ev, f_out = (sem("f_" + s) for s in "T ev out".split())

    def final_pe(pe):
        for k in range(KD):
            pe.wait_ge(hf_ready, KD * 5 + k + 1)
            if k == 0:
                pe.wait_ge(sd_ready, 6)
            for t in range(NT):
                ins = pe.transpose(PS[:, k, t * P:(t + 1) * P], hf[:, k % 2, t * P:(t + 1) * P], ident[:, :])
            ins.then_inc(f_T, 1)

    def final_dve(dve):
        dve.wait_ge(sd_ready, 6)
        dve_link(dve.reciprocal(rstd, rstd))
        for k in range(KD):
            if k >= 2:
                dve.wait_ge(f_T, k - 1)
            dve.scalar_tensor_tensor(hf[:, k % 2, :], xT[:, k, :], gain(G_FINAL, k), rstd, ALU.mult, ALU.mult).then_inc(hf_ready, 1)

    def final_act(act):
        for k in range(KD):
            act.wait_ge(f_T, k + 1)
            act.activation(outn[:, :, k * P:(k + 1) * P], PS[:, k, :].rearrange("p (t c) -> p t c", t=NT), ACT.Copy).then_inc(f_ev, 1)

    def final_sp(sp):
        o = out[0].rearrange("(t p) d -> p t d", p=P)
        for j in range(2):
            sp.wait_ge(f_ev, 4 * (j + 1))
            sp.dma_start(o[:, :, j * 512:(j + 1) * 512], outn[:, :, j * 512:(j + 1) * 512]).then_inc(f_out, 16)
        sp.wait_ge(f_out, 32)

    with nc.Block() as block:
        @block.sync
        def _(sp):
            start_sp(sp)
            up_sp(sp, 0, (A['w1_gate'][0], 0), (A['w1_up'][0], 0))
            down_sp(sp, "dn0", A['w1_down'][0], STEPS)
            mid1_sp(sp)
            merge1_sp(sp)
            down_sp(sp, "wout", A['w_out'][0], KD // 2)
            up_sp(sp, 1, (A['w2_gate'][0], 0), (A['w2_up'][0], 0))
            down_sp(sp, "dn1", A['w2_down'][0], STEPS)
            ret_sp(sp)
            branch_sp(sp, "merge2a", 7184, A['w_ret_br_2'][0])
            delta_sp(sp)
            branch_sp(sp, "merge2b", 8208, A['w_dn_br_2'][0])
            down_sp(sp, "wo", A['w_o_2'][0], KD // 2)
            up_sp(sp, 2, (A['w_up_2'][0], 0), (A['w_up_2'][0], FF))
            down_sp(sp, "dn2", A['w_down_2'][0], STEPS)
            final_sp(sp)

        @block.gpsimd
        def _(pool):
            start_pool(pool)
            norm_pool(pool, 0, U["up0"])
            up_pool(pool, 0)
            down_pool(pool, "dn0", STEPS)
            norm_pool(pool, 1, U["mid1"])
            mid1_pool(pool)
            los(pool, U["merge1"] + 2, 10)
            down_pool(pool, "wout", KD // 2)
            norm_pool(pool, 2, U["up1"])
            up_pool(pool, 1)
            down_pool(pool, "dn1", STEPS)
            norm_pool(pool, 3, U["ret"])
            ret_pool(pool)
            delta_pool(pool)
            los(pool, U["merge2b"] + 4, 4)
            down_pool(pool, "wo", KD // 2)
            norm_pool(pool, 4, U["up2"])
            up_pool(pool, 2)
            down_pool(pool, "dn2", STEPS)

        @block.scalar
        def _(act):
            start_act_queue(act)
            start_act(act)
            norm_act(act, 0, U["up0"])
            down_act(act, "dn0", STEPS, up_act(act, 0))
            norm_act(act, 1, U["mid1"])
            mid1_act(act)
            index_act(act)
            stick_act(act)
            sparse_act(act)
            merge1_act(act)
            down_act(act, "wout", KD // 2, ahead=True)
            norm_act(act, 2, U["up1"])
            down_act(act, "dn1", STEPS, up_act(act, 1))
            norm_act(act, 3, U["ret"])
            ret_act(act)
            branch_act(act, "merge2a", 0)
            rounds(act, U["dn"], 2)
            delta_act(act)
            branch_act(act, "merge2b", 1)
            down_act(act, "wo", KD // 2, ahead=True)
            norm_act(act, 4, U["up2"])
            down_act(act, "dn2", STEPS, up_act(act, 2))
            norm_act(act, 5)
            final_act(act)

        @block.vector
        def _(dve):
            start_dve(dve)
            norm_dve(dve, 0, G_FFN1)
            up_dve(dve, 0)
            down_dve(dve, "dn0", 0, STEPS, 0.5)
            norm_dve(dve, 1, G_MIX)
            mid1_dve(dve)
            index_dve(dve)
            stick_dve(dve)
            sparse_dve(dve)
            merge1_dve(dve)
            down_dve(dve, "wout", 1, KD // 2, 1.0)
            norm_dve(dve, 2, G_FFN2)
            up_dve(dve, 1)
            down_dve(dve, "dn1", 2, STEPS, 0.5)
            norm_dve(dve, 3, G_MIX2)
            ret_dve(dve)
            branch_dve(dve, "merge2a", 0)
            dve.wait_ge(lv_set, 1)
            delta_dve(dve)
            branch_dve(dve, "merge2b", 1)
            down_dve(dve, "wo", 3, KD // 2, 1.0)
            norm_dve(dve, 4, G_FFNB)
            up_dve(dve, 2)
            down_dve(dve, "dn2", 4, STEPS, 1.0)
            final_dve(dve)

        @block.tensor
        def _(pe):
            start_pe(pe)
            norm_pe(pe, 0)
            up_pe(pe, 0)
            pe.wait_ge(up_ev, STEPS)
            down_pe(pe, "dn0", 0, STEPS, act_hi, act_lo, (a_ready, 0))
            norm_pe(pe, 1)
            mid1_pe(pe)
            index_pe(pe)
            stick_pe(pe)
            sparse_pe(pe)
            merge1_pe(pe)
            pe.wait_ge(g_mul, 4)
            down_pe(pe, "wout", 1, KD // 2, mg_hi, mg_lo, half_ready(pe, mg_ready))
            norm_pe(pe, 2)
            up_pe(pe, 1)
            pe.wait_ge(up_ev, 2 * STEPS)
            down_pe(pe, "dn1", 2, STEPS, act_hi, act_lo, (a_ready, STEPS))
            norm_pe(pe, 3)
            ret_pe(pe)
            branch_pe(pe, "merge2a", 0, yr_hi, yr_lo, (r_lo, 8))
            delta_pe(pe)
            await_point(pe, "dve", 3, "oy")
            branch_pe(pe, "merge2b", 1, do_hi, do_lo, (passed["dve"], 4 * len(POINTS["dve"])))
            pe.wait_ge(br_mul, 4)
            down_pe(pe, "wo", 3, KD // 2, mh2, ml2, half_ready(pe, br_ready))
            norm_pe(pe, 4)
            up_pe(pe, 2)
            pe.wait_ge(up_ev, 3 * STEPS)
            down_pe(pe, "dn2", 4, STEPS, act_hi, act_lo, (a_ready, 2 * STEPS))
            norm_pe(pe, 5)
            final_pe(pe)


def kernel(**inputs):
    import numpy as _np
    import concourse.bacc as _bacc
    from concourse import mybir as _mybir
    from concourse.bass_utils import run_bass_kernel_spmd as _run

    nc = _bacc.Bacc("TRN2", target_bir_lowering=False, num_devices=1)
    arrays, args = {}, {}
    for name in NAMES:
        a = _np.ascontiguousarray(inputs[name])
        arrays[f"in_{name}_dram"] = a
        args[name] = nc.dram_tensor(f"in_{name}_dram", a.shape, _mybir.dt.from_np(a.dtype), kind="ExternalInput").ap()
    out = nc.dram_tensor("out_0_dram", (1, T, D), F32, kind="ExternalOutput").ap()
    two_blocks_kernel(nc, args, out)
    r = _run(nc, [arrays], core_ids=[0])
    return r.results[0]["out_0_dram"]
```
